# Optimizing a Trainium2 kernel written in Bass

```python
import numpy as np
import jax, jax.numpy as jnp
from jax import lax

D_MODEL = 1024
BATCH = 1
SEQ = 1024
DEPTH = 1

GRID_W = 64
WIN_R = 8
WIN_C = 16
NA_HEADS = 8
NA_HEAD_DIM = D_MODEL // 16
NA_WIDTH = NA_HEADS * NA_HEAD_DIM
GLA_HEADS = 4
GLA_DK = D_MODEL // 16
GLA_DV = D_MODEL // 8
GLA_KEY_WIDTH = GLA_HEADS * GLA_DK
GLA_VAL_WIDTH = GLA_HEADS * GLA_DV
GLA_RANK = 16
GLA_TAU = 16.0
HGRN_HEADS = 4
HGRN_DK = 128
HGRN_DV = D_MODEL // 8
HGRN_KEY_WIDTH = HGRN_HEADS * HGRN_DK
HGRN_VAL_WIDTH = HGRN_HEADS * HGRN_DV
CHUNK = 16
N_BRANCHES = 3
PROJ_SIZES = (NA_WIDTH, NA_WIDTH, NA_WIDTH,
              GLA_KEY_WIDTH, GLA_KEY_WIDTH, GLA_VAL_WIDTH, GLA_VAL_WIDTH, 2 * GLA_RANK,
              HGRN_KEY_WIDTH, 2 * HGRN_KEY_WIDTH, HGRN_VAL_WIDTH, HGRN_VAL_WIDTH,
              N_BRANCHES * D_MODEL)
PROJ_WIDTH = sum(PROJ_SIZES)
FFN_HIDDEN = ((8 * D_MODEL // 3 + 255) // 256) * 256
N_MOD = 6
RMS_EPS = 1e-6
NEG_INF = -1e30
F_FLOOR = 1e-30

kernel_name = 'hybrid_na_gla_hgrn2_encoder'

def rmsnorm(x, w):
    xf = x.astype(jnp.float32)
    y = xf * lax.rsqrt(jnp.mean(xf * xf, axis=-1, keepdims=True) + RMS_EPS)
    return (y * w.astype(jnp.float32)).astype(x.dtype)

def to_heads(a, n):
    b, t, _ = a.shape
    return a.reshape(b, t, n, -1).transpose(0, 2, 1, 3)

def from_heads(a):
    b, h, t, d = a.shape
    return a.transpose(0, 2, 1, 3).reshape(b, t, h * d)

def neighborhood_attention(q, k, v, rpb):
    bsz, t, _ = q.shape
    rows = t // GRID_W
    wr = min(WIN_R, rows)
    def grid(a):
        return a.reshape(bsz, rows, GRID_W, NA_HEADS, NA_HEAD_DIM).transpose(0, 3, 1, 2, 4)
    qg = grid(q) * (NA_HEAD_DIM ** -0.5)
    kg, vg = grid(k), grid(v)
    r = jnp.arange(rows)
    row_start = jnp.clip(r - WIN_R // 2, 0, rows - wr)
    row_idx = row_start[:, None] + jnp.arange(wr)[None, :]
    k_band = kg[:, :, row_idx]
    v_band = vg[:, :, row_idx]
    col = jnp.arange(GRID_W)
    col_start = jnp.clip(col - WIN_C // 2, 0, GRID_W - WIN_C)
    col_mask = (col[None, :] >= col_start[:, None]) & (col[None, :] < col_start[:, None] + WIN_C)
    row_off = row_idx - r[:, None] + (WIN_R - 1)
    col_off = jnp.clip(col[None, :] - col[:, None], -(WIN_C - 1), WIN_C - 1) + (WIN_C - 1)
    bias = rpb[:, row_off[:, None, :, None], col_off[None, :, None, :]]
    s = jnp.einsum('bhrqd,bhrjkd->bhrqjk', qg, k_band).astype(jnp.float32) + bias.astype(jnp.float32)
    s = jnp.where(col_mask[:, None, :], s, NEG_INF)
    p = jax.nn.softmax(s.reshape(bsz, NA_HEADS, rows, GRID_W, wr * GRID_W), axis=-1)
    p = p.reshape(s.shape).astype(v.dtype)
    o = jnp.einsum('bhrqjk,bhrjkd->bhrqd', p, v_band)
    return o.transpose(0, 2, 3, 1, 4).reshape(bsz, t, NA_WIDTH)

def chunk_gated_linear_attention(q, k, v, log_a):
    bsz, nh, t, dk = q.shape
    dv = v.shape[-1]
    n = t // CHUNK
    q, k, v, log_a = [a.astype(jnp.float32).reshape(bsz, nh, n, CHUNK, a.shape[-1]) for a in (q, k, v, log_a)]
    b = jnp.cumsum(log_a, axis=3)
    tri = jnp.tril(jnp.ones((CHUNK, CHUNK), dtype=bool))[:, :, None]
    diff = b[:, :, :, :, None, :] - b[:, :, :, None, :, :]
    decay = jnp.where(tri, jnp.exp(jnp.where(tri, diff, 0.0)), 0.0)
    scores = jnp.einsum('bhnid,bhnjd,bhnijd->bhnij', q, k, decay)
    o_intra = jnp.einsum('bhnij,bhnjv->bhniv', scores, v)
    b_last = b[:, :, :, -1:, :]
    q_dec = q * jnp.exp(b)
    k_dec = k * jnp.exp(b_last - b)
    a_chunk = jnp.exp(b_last[:, :, :, 0, :])
    def step(state, xs):
        qn, kn, vn, an = xs
        o = jnp.einsum('bhid,bhdv->bhiv', qn, state)
        state = an[..., None] * state + jnp.einsum('bhjd,bhjv->bhdv', kn, vn)
        return state, o
    xs = tuple(jnp.moveaxis(a, 2, 0) for a in (q_dec, k_dec, v, a_chunk))
    _, o_inter = lax.scan(step, jnp.zeros((bsz, nh, dk, dv), jnp.float32), xs)
    o = o_intra + jnp.moveaxis(o_inter, 0, 2)
    return o.reshape(bsz, nh, t, dv)

def bidirectional_gla(q, k_fwd, k_bwd, v, la_fwd, la_bwd):
    flip = lambda a: jnp.flip(a, axis=2)
    fwd = chunk_gated_linear_attention(q, k_fwd, v, la_fwd)
    bwd = chunk_gated_linear_attention(flip(q), flip(k_bwd), flip(v), flip(la_bwd))
    return fwd + flip(bwd)

def gla_branch(q, k, v, g, lr, lr_up, lr_bias, norm_w):
    bsz, t, _ = q.shape
    z = jnp.einsum('btsr,srk->btsk', lr.reshape(bsz, t, 2, GLA_RANK), lr_up) + lr_bias
    log_a = jax.nn.log_sigmoid(z.astype(jnp.float32)) / GLA_TAU
    la_f = to_heads(log_a[:, :, 0], GLA_HEADS)
    la_b = to_heads(log_a[:, :, 1], GLA_HEADS)
    qh = to_heads(q, GLA_HEADS) * (GLA_DK ** -0.5)
    kh = to_heads(k, GLA_HEADS)
    vh = to_heads(v, GLA_HEADS)
    o = bidirectional_gla(qh, kh, kh, vh, la_f, la_b)
    o = rmsnorm(o, norm_w) * jax.nn.silu(to_heads(g, GLA_HEADS).astype(jnp.float32))
    return from_heads(o).astype(q.dtype)

def hgrn2_branch(q, f, i, g, lb, norm_w):
    bsz, t, _ = q.shape
    z = f.reshape(bsz, t, 2, HGRN_KEY_WIDTH).astype(jnp.float32)
    lbf = lb.astype(jnp.float32)
    forget = lbf + (1.0 - lbf) * jax.nn.sigmoid(z)
    log_f = jnp.log(jnp.maximum(forget, F_FLOOR))
    k_in = (1.0 - lbf) * jax.nn.sigmoid(-z)
    qh = to_heads(jax.nn.silu(q), HGRN_HEADS)
    vh = to_heads(i, HGRN_HEADS)
    o = bidirectional_gla(qh,
                          to_heads(k_in[:, :, 0], HGRN_HEADS), to_heads(k_in[:, :, 1], HGRN_HEADS), vh,
                          to_heads(log_f[:, :, 0], HGRN_HEADS), to_heads(log_f[:, :, 1], HGRN_HEADS))
    o = rmsnorm(o, norm_w) * jax.nn.silu(to_heads(g, HGRN_HEADS).astype(jnp.float32))
    return from_heads(o).astype(q.dtype)

def setup_inputs(seed: int = 0) -> dict:
    key = jax.random.key(seed)
    ks = jax.random.split(key, 24)
    nrm = lambda k, shape, scale: jax.random.normal(k, shape, jnp.float32) * scale
    return {
        'x': nrm(ks[0], (BATCH, SEQ, D_MODEL), 1.0),
        'c': nrm(ks[1], (BATCH, D_MODEL), 1.0),
        'w_ada': nrm(ks[2], (DEPTH, D_MODEL, N_MOD * D_MODEL), D_MODEL ** -0.5),
        'b_ada': nrm(ks[3], (DEPTH, N_MOD * D_MODEL), 0.02),
        'norm1_w': 1.0 + nrm(ks[4], (DEPTH, D_MODEL), 0.02),
        'w_in': nrm(ks[5], (DEPTH, D_MODEL, PROJ_WIDTH), D_MODEL ** -0.5),
        'na_rpb': nrm(ks[6], (DEPTH, NA_HEADS, 2 * WIN_R - 1, 2 * WIN_C - 1), 0.1),
        'gla_lr_up': nrm(ks[7], (DEPTH, 2, GLA_RANK, GLA_KEY_WIDTH), GLA_RANK ** -0.5),
        'gla_lr_bias': nrm(ks[8], (DEPTH, 2, GLA_KEY_WIDTH), 0.02),
        'gla_norm_w': 1.0 + nrm(ks[9], (DEPTH, GLA_DV), 0.02),
        'hgrn_lb_logits': nrm(ks[10], (DEPTH, 2 * HGRN_KEY_WIDTH), 1.0),
        'hgrn_norm_w': 1.0 + nrm(ks[11], (DEPTH, HGRN_DV), 0.02),
        'w_proj_na': nrm(ks[12], (DEPTH, NA_WIDTH, D_MODEL), NA_WIDTH ** -0.5),
        'w_proj_gla': nrm(ks[13], (DEPTH, GLA_VAL_WIDTH, D_MODEL), GLA_VAL_WIDTH ** -0.5),
        'w_proj_hgrn': nrm(ks[14], (DEPTH, HGRN_VAL_WIDTH, D_MODEL), HGRN_VAL_WIDTH ** -0.5),
        'w_out': nrm(ks[15], (DEPTH, D_MODEL, D_MODEL), D_MODEL ** -0.5),
        'norm2_w': 1.0 + nrm(ks[16], (DEPTH, D_MODEL), 0.02),
        'w_ffn_gate': nrm(ks[17], (DEPTH, D_MODEL, FFN_HIDDEN), D_MODEL ** -0.5),
        'w_ffn_up': nrm(ks[18], (DEPTH, D_MODEL, FFN_HIDDEN), D_MODEL ** -0.5),
        'w_ffn_down': nrm(ks[19], (DEPTH, FFN_HIDDEN, D_MODEL), FFN_HIDDEN ** -0.5),
        'final_norm_w': 1.0 + nrm(ks[20], (D_MODEL,), 0.02),
    }

def reference(x, c, w_ada, b_ada, norm1_w, w_in, na_rpb, gla_lr_up, gla_lr_bias, gla_norm_w,
              hgrn_lb_logits, hgrn_norm_w, w_proj_na, w_proj_gla, w_proj_hgrn, w_out, norm2_w,
              w_ffn_gate, w_ffn_up, w_ffn_down, final_norm_w):
    split_points = [int(s) for s in np.cumsum(PROJ_SIZES)[:-1]]
    lb_p = jax.nn.softmax(hgrn_lb_logits.astype(jnp.float32), axis=0)
    lb_all = jnp.clip(jnp.cumsum(lb_p, axis=0) - lb_p[0], 0.0, 1.0)
    c_act = jax.nn.silu(c)
    for l in range(DEPTH):
        mod = c_act @ w_ada[l] + b_ada[l]
        shift1, scale1, gate1, shift2, scale2, gate2 = jnp.split(mod[:, None, :], N_MOD, axis=-1)
        h = rmsnorm(x, norm1_w[l]) * (1.0 + scale1) + shift1
        p = h @ w_in[l]
        (na_q, na_k, na_v, gla_q, gla_k, gla_v, gla_g, gla_lr,
         hg_q, hg_f, hg_i, hg_g, gates) = jnp.split(p, split_points, axis=-1)
        o_na = neighborhood_attention(na_q, na_k, na_v, na_rpb[l])
        o_gla = gla_branch(gla_q, gla_k, gla_v, gla_g, gla_lr, gla_lr_up[l], gla_lr_bias[l], gla_norm_w[l])
        o_hg = hgrn2_branch(hg_q, hg_f, hg_i, hg_g, lb_all[l].reshape(2, HGRN_KEY_WIDTH), hgrn_norm_w[l])
        g_na, g_gla, g_hg = jnp.split(jax.nn.sigmoid(gates), N_BRANCHES, axis=-1)
        merged = (g_na * (o_na @ w_proj_na[l]) + g_gla * (o_gla @ w_proj_gla[l])
                  + g_hg * (o_hg @ w_proj_hgrn[l]))
        x = x + gate1 * (merged @ w_out[l])
        h = rmsnorm(x, norm2_w[l]) * (1.0 + scale2) + shift2
        ff = (jax.nn.silu(h @ w_ffn_gate[l]) * (h @ w_ffn_up[l])) @ w_ffn_down[l]
        x = x + gate2 * ff
    return rmsnorm(x, final_norm_w)


_drawn_inputs = setup_inputs


def setup_inputs(seed=0):
    import zlib

    import numpy as np

    out = dict(_drawn_inputs(seed))
    spreads = {}
    factors = {'norm1_w': 4.489,
     'na_rpb': 79.175,
     'gla_lr_bias': 22.076,
     'gla_norm_w': 25.45,
     'hgrn_norm_w': 26.31,
     'norm2_w': 17.354,
     'final_norm_w': 24.605}
    for name, (base, spread) in spreads.items():
        noise = np.random.default_rng([zlib.crc32(name.encode()), seed]).standard_normal(out[name].shape)
        drawn = base * np.exp(spread * noise) if base else spread * noise
        out[name] = __import__('jax').numpy.asarray(drawn.astype(out[name].dtype))
    for name, factor in factors.items():
        out[name] = (out[name] * factor).astype(out[name].dtype)
    return out
```

```python
import concourse.bass as bass
from concourse import mybir
from contextlib import ExitStack

F32 = mybir.dt.float32
F32R = mybir.dt.float32r
U8 = mybir.dt.uint8
ACT = mybir.ActivationFunctionType
ALU = mybir.AluOpType

P = 128
D_MODEL = 1024
T = 1024
KD = 8
HALF = 512
NC = 8
LEVELS = [64, 32, 16, 8, 4, 2, 1]
NQ = 2 * len(LEVELS)
NADA = 16
EPS = 1e-6
F_FLOOR = 1e-30
LN_SPLIT = 2.0 ** -50
KF = 11
NEG_INF = -1e30

PC_C, PC_BADA, PC_N1, PC_N2, PC_NF, PC_GN, PC_HN, PC_LB, PC_ZB = 0, 8, 56, 64, 72, 80, 81, 82, 90
NPRM = 94

TRIPS = dict(pre=1, hgrn=4, gla=2, na=4, mid=1, merge=4, mid2=1, out=4, n2=1, up0=11, dn0=4, up1=11, dn1=4, fin=1)
TILES = dict(pre=2, hgrn=8, gla=6, na=6, merge=6, out=2, up0=2, dn0=2, up1=2, dn1=2)
PLAN = {
    "tile": (0, TILES),
    "gram_done": (0, dict(hgrn=32, gla=64)),
    "gram_free0": (1, dict(hgrn=16, gla=32)),
    "gram_free1": (1, dict(hgrn=16, gla=32)),
    "misc_done": (0, dict(pre=4, hgrn=10, gla=10, na=1)),
    "misc_free": (1, dict(pre=1, hgrn=10, gla=10, na=1)),
    "dve_own": (0, dict(pre=19, hgrn=55, gla=50, na=33, merge=2, n2=10)),
    "act_own": (0, dict(pre=4, hgrn=23, gla=22, n2=1, fin=1)),
    "param_ready": (0, dict(pre=1)),
    "cact_ready": (0, dict(pre=1)),
    "sig_ready": (0, dict(hgrn=2, gla=2)),
    "ln_in": (0, dict(hgrn=2, gla=2)),
    "ln_out": (0, dict(hgrn=2, gla=2)),
    "diff_ready": (0, dict(hgrn=2 + NQ, gla=2 + NQ)),
    "exp_ready": (0, dict(hgrn=2 + NQ, gla=2 + NQ)),
    "ksum_ready": (0, dict(hgrn=1)),
    "kdec_ready": (0, dict(hgrn=2, gla=2)),
    "x_ready": (0, dict(hgrn=NQ, gla=NQ)),
    "attn_ready": (0, dict(hgrn=1, gla=2)),
    "osq_ready": (0, dict(hgrn=1, gla=2)),
    "orstd_ready": (0, dict(hgrn=1, gla=2)),
    "o_ready": (0, dict(hgrn=1, gla=2, na=1)),
    "sq_ready": (0, dict(pre=8, n2=8, fin=8)),
    "sq_used": (0, dict(pre=8, n2=8, fin=8)),
    "rstd_ready": (0, dict(pre=1, n2=1, fin=1)),
    "norm_ready": (0, dict(pre=8, n2=8, fin=8)),
    "hi_ready": (0, dict(pre=8, mid=12, mid2=8, n2=8, up0=1, up1=1)),
    "lo_ready": (0, dict(pre=8, mid=12, mid2=8, n2=8, up0=1, up1=1)),
    "merged": (0, dict(merge=2)),
    "s_done": (0, dict(na=18)),
    "s_free": (1, dict(na=18)),
    "max_ready": (0, dict(na=16)),
    "p_exp": (0, dict(na=16)),
    "p_norm": (0, dict(na=16)),
    "pt_done": (0, dict(na=16)),
    "pt_ready": (0, dict(na=16)),
    "ada_ld": (0, dict(hgrn=4)),
    "lup_ld": (0, dict(gla=1)),
    "bias_ld": (0, dict(na=1)),
    "o_st": (0, dict(hgrn=1, gla=2, na=1)),
    "gate_st0": (1, dict(hgrn=1, na=1)),
    "gate_st1": (1, dict(hgrn=1, na=1)),
    "gate_st2": (1, dict(hgrn=1, na=1)),
    "in_ld0": (0, dict(mid=6, merge=3, out=1, dn0=1, dn1=1)),
    "in_ld1": (0, dict(mid=6, merge=3, out=1, dn0=1, dn1=1)),
    "y_st0": (0, dict(out=1, dn0=1)),
    "y_st1": (0, dict(out=1, dn0=1)),
    "out_st": (0, dict(fin=8)),
}
TALLY = {}


def trunk(nc, prm, masks, cmat, cmask, xt, w_ada, w_lr, w_in, w_proj, w_out, w_up, w_dn, lup, rpb, out):
    base = {}
    for name, (first, per) in PLAN.items():
        n, base[name] = first, {}
        for st in TRIPS:
            base[name][st] = n
            n += TRIPS[st] * per.get(st, 0)

    ctx = ExitStack()
    with ctx:
        sems = {k: ctx.enter_context(nc.semaphore(k)) for k in PLAN if k != "tile"}
        sem = lambda name: ctx.enter_context(nc.semaphore(name))
        w_raw = [sem("w_raw0"), sem("w_raw1")]
        w_hi = sem("w_hi")
        w_ready = sem("w_ready")
        tile_done = sem("tile_done")
        tile_free = [sem("tile_free0"), sem("tile_free1")]
        const_ld = sem("const_ld")
        x_ld = sem("x_ld")
        ada_pre = [sem(f"ada_pre{k}") for k in range(4)]
        rpb_st = sem("rpb_st")
        lr_st = sem("lr_st")
        pool_step, dve_step = sem("pool_step"), sem("dve_step")
        lr_ld = sem("lr_ld")
        cmask_ld = sem("cmask_ld")

        class Pass:

            def __init__(self, e, stage, i=0):
                self.e, self.st, self.i, self.n = e, stage, i, {}

            def at(self, name, n):
                return base[name][self.st] + PLAN[name][1].get(self.st, 0) * self.i + n

            def up(self, name):
                self.n[name] = self.n.get(name, 0) + 1
                return sems[name]

            def wait(self, name, n):
                v = self.at(name, n)
                if isinstance(v, int) and v <= 0:
                    return
                self.e.wait_ge(sems[name], v)

            def wait_dma(self, name, n):
                v = self.at(name, n) * 16
                if isinstance(v, int) and v <= 0:
                    return
                self.e.wait_ge(sems[name], v)

            def tile(self, j):
                return self.at("tile", j)

            def tile_half(self, j):
                b, k = base["tile"][self.st], TILES[self.st]
                return b // 2 + (k // 2) * self.i + j // 2

            def wait_evac(self, j):
                self.e.wait_ge(tile_free[j % 2], self.tile_half(j) + 1)

            def wait_tile(self, j):
                self.e.wait_ge(tile_done, self.tile(j) + 1)

            def free_tile(self, ins, j):
                ins.then_inc(tile_free[j % 2], 1)
                self.wait_evac(j)

            def own(self, ins, name):
                ins.then_inc(self.up(name), 1)
                self.e.wait_ge(sems[name], self.at(name, self.n[name]))

            def free(self, ins, name, use):
                ins.then_inc(sems[name], 1)
                self.e.wait_ge(sems[name], self.at(name, use + 1))

            def end(self):
                for k, v in self.n.items():
                    TALLY[(k, self.st)] = v

        start = -(-nc.sbuf_base // 32) * 32
        fence = ctx.enter_context(nc.sbuf_tensor("fence", [P, (nc.sbuf_usable_end - start) // 4 - 16], F32))
        del fence
        place = [start]

        def at(name, offset, shape, dt=F32):
            return nc.alloc_sbuf_tensor_at(name, shape, dt, offset=offset)

        def sb(name, shape, dt=F32):
            n = 1 if dt == U8 else 4
            for k in shape[1:]:
                n *= k
            place[0] += -(-n // 32) * 32
            return at(name, place[0] - -(-n // 32) * 32, shape, dt)

        WR = sb("WR", [P, 2, 2, KF, P], F32R)
        RAW = sb("RAW", [P, 2, KF, P])
        hs_at = place[0]
        HS = sb("HS", [P, 16, T], F32R)
        H2 = at("H2", hs_at, [P, 16, T])
        z_at = place[0]
        ZT = sb("ZT", [P, 26, T])
        BIG = at("BIG", z_at, [P, 24, T], F32R)
        ADA = at("ADA", z_at, [P, NADA, KD, P])
        px_at = z_at + 22 * T * 4
        PX = at("PX", px_at, [P, 2, NC, P + 1])
        ADX = at("ADX", px_at + 2 * NC * (P + 1) * 4, [P, 2, KD, P])
        LR = at("LR", px_at + 2 * NC * (P + 1) * 4, [32, T])
        sb("rest_of_ADX", [P, 16])
        PRM = sb("PRM", [P, NPRM])
        MOD = sb("MOD", [P, 48])
        SCL = sb("SCL", [P, 2, KD])
        CA = sb("CA", [P, KD])
        LB = sb("LB", [P, 2, 8])
        EP = sb("EP", [P, 2])
        MASK = sb("MASK", [P, NQ, P], U8)
        CM = sb("CM", [P, 2, P])
        LUP = sb("LUP", [32, 2, P])
        AN = sb("AN", [P, 2, NC])
        SM = sb("SM", [P, 16])
        MASKF = at("MASKF", z_at + 24 * T * 4, [P, NQ, P])
        ONES, IDENT = CM[:, 0, :], CM[:, 1, :]
        zt = lambda k: ZT[:, k, :]

        PD = [ctx.enter_context(nc.psum_tensor(f"PD{j}", [P, T], F32)) for j in range(2)]
        PG = ctx.enter_context(nc.psum_tensor("PG", [P, T], F32))
        PM = ctx.enter_context(nc.psum_tensor("PM", [P, T], F32))

        gates_dr = nc.dram_tensor("gates_scratch", [24, P, T], F32).ap()
        o_dr = nc.dram_tensor("o_scratch", [12, P, T], F32).ap()
        y_dr = nc.dram_tensor("y_scratch", [8, P, T], F32).ap()
        lr_dr = nc.dram_tensor("lr_scratch", [32, T], F32).ap()
        bias_dr = nc.dram_tensor("bias_scratch", [8, P, 14 * 64], F32).ap()

        Q, K0, K1, F0, F1, V, G = range(7)
        XB = [7, 8, 9, 10]
        A0, VT0, KT0, KT1, QD0, QD1, S0, S1, GB = 11, 12, 13, 14, 15, 16, 17, 18, 19
        gV = [K1, V]
        gG = [G, 19]
        gA = [A0, 20]
        gVT = [VT0, 21]

        def blocks(ap, s):
            return ap.rearrange("p (b t) -> p b t", t=2 * s)

        def px_view(d, s):
            lo = 1 - d
            nb = P // (2 * s)
            v = PX[:, d, :, lo:lo + P].rearrange("p c (b t) -> p c b t", t=2 * s)
            r = PX[:, d, :, s:s + 2 * s * (nb - 1) + 1:2 * s] if nb > 1 else PX[:, d, :, s:s + 1]
            r = r.rearrange("p c (b o) -> p c b o", o=1).to_broadcast([P, NC, nb, 2 * s])
            return v, r

        def px_last(d):
            return PX[:, d, :, P:P + 1].to_broadcast([P, NC, P])

        NQT, NK, NV, NVT, NO = range(5)
        NS = [ZT[:, 5, :], ZT[:, 6, :]]
        NPT = [ZT[:, 7, :], ZT[:, 8, :]]
        NTR = at("NTR", z_at + 9 * T * 4, [P, 2, 14 * 64])
        NTI = at("NTI", z_at + 11 * T * 4, [P, 2, 5 * P])
        NCM = at("NCM", z_at + 13 * T * 4, [P, 64 + 5 * P])
        OCOL = 768

        def na_step(k):
            t = k % 8
            us = range(0, 4) if t < 2 else range(4, 8) if t > 5 else range(t - 2, t + 3)
            return k // 8, t, list(us)

        chunked = lambda ap: ap.rearrange("p (c t) -> p c t", t=P)

        block = ctx.enter_context(nc.Block())

        @block.sync
        def _(sp):
            sp.dma_start(PRM[:, :], prm).then_inc(const_ld, 16)
            sp.dma_start(CM[:, :, :], cmat).then_inc(const_ld, 16)
            sp.dma_start(MASKF[:, :, :], masks).then_inc(const_ld, 16)
            for k in range(4):
                sp.dma_start(ADA[:, 4 * k:4 * k + 4, :, :], w_ada[:, 4 * k:4 * k + 4, :, :]).then_inc(ada_pre[k], 16)
                if k == 0:
                    sp.dma_start(ZT[:, 16:24, :], xt).then_inc(x_ld, 16)
                    sp.dma_start(RAW[:, 1, 0:KD, :], w_lr).then_inc(w_raw[1], 16)

            def load(c, j, src):
                sp.wait_ge(w_ready, c.tile(j) - 1)
                sp.dma_start(RAW[:, j % 2, 0:src.shape[2], :], src.rearrange("n p k m -> p (n k) m")
                             ).then_inc(w_raw[j % 2], 16)

            Pass(sp, "pre").wait("lo_ready", 8)
            with sp.Fori(0, TRIPS["hgrn"]) as i:
                c = Pass(sp, "hgrn", i)
                for j in range(8):
                    load(c, j, w_in[bass.ds(i * 8 + j, 1)])
                    if j % 2:
                        a = j // 2
                        c.wait("misc_done", [-1, 1, 2, 4][a])
                        sp.dma_start(ADX[:, :, :, :], w_ada[:, bass.ds(i * 8 + (NADA + 2 * a), 2), :, :]
                                     ).then_inc(sems["ada_ld"], 16)
            for st, first in (("gla", 32), ("na", 44)):
                with sp.Fori(0, TRIPS[st]) as i:
                    c = Pass(sp, st, i)
                    for j in range(6):
                        load(c, j, w_in[bass.ds(i * 6 + (first + j), 1)])
            for st, src, per in (("merge", w_proj, 6), ("out", w_out, 2), ("up0", w_up[0], 2), ("dn0", w_dn[0], 2),
                                 ("up1", w_up[1], 2), ("dn1", w_dn[1], 2)):
                with sp.Fori(0, TRIPS[st]) as i:
                    c = Pass(sp, st, i)
                    for j in range(per):
                        load(c, j, src[bass.ds(i * per + j, 1)])

        @block.gpsimd
        def _(pool):
            pool.sem_inc(w_raw[0], 16)
            for h in range(8):
                for r in range(2):
                    src = bass.AP(rpb.tensor, h * 15 * P + (1 - r) * P + 63, [[P, 14], [-1, 64], [1, 64]])
                    dst = bass.AP(bias_dr.tensor, (h * P + 64 * r) * 896, [[64, 14], [896, 64], [1, 64]])
                    pool.dma_start(dst, src).then_inc(rpb_st, 16)

            def split(slot, kt, n, half, inc):
                pool.wait_ge(w_raw[slot], 16 * (half + 1))
                if not (isinstance(n, int) and n - 1 <= 0):
                    pool.wait_ge(tile_done, n - 1)
                pool.sem_inc(pool_step, 1)
                raw, hi, lo = RAW[:, slot, 0:kt, :], WR[:, slot, 0, 0:kt, :], WR[:, slot, 1, 0:kt, :]
                pool.tensor_copy(hi, raw).then_inc(w_hi, inc)
                pool.wait_ge(w_hi, n + 1)
                pool.tensor_tensor(lo, raw, hi.bitcast(F32), ALU.subtract).then_inc(w_ready, inc)

            split(1, KD, 1, 0, 2)
            for st, kt in (("hgrn", 8), ("gla", 8), ("na", 8), ("merge", 4), ("out", 8), ("up0", 8), ("dn0", KF),
                           ("up1", 8), ("dn1", KF)):
                with pool.Fori(0, TRIPS[st] * TILES[st] // 2) as i:
                    b = base["tile"][st]
                    for j in range(2):
                        split(j, kt, i * 2 + (b + j), i + b // 2, 1)

        @block.tensor
        def _(pe):
            def dense(c, j, kt, mov, lo_at):
                pe.wait_ge(w_ready, c.tile(j) + 1)
                pe.wait_ge(tile_free[j % 2], c.tile_half(j))
                s = j % 2
                for k in range(kt):
                    for n, (w, x) in enumerate(((0, 0), (0, lo_at), (1, 0))):
                        for h in range(2):
                            last = pe.matmul(PD[s][:, h * HALF:(h + 1) * HALF], WR[:, s, w, k, :],
                                             mov[:, k + x, h * HALF:(h + 1) * HALF],
                                             start=(k == 0 and n == 0), stop=(k == kt - 1 and n == 2))
                last.then_inc(tile_done, 1)

            def sum_squares(c, src):
                for ct in range(KD):
                    c.wait("sq_ready", ct + 1)
                    for h in range(2):
                        last = pe.matmul(PG[:, h * HALF:(h + 1) * HALF], ONES, src(ct)[:, h * HALF:(h + 1) * HALF],
                                         start=(ct == 0), stop=(ct == KD - 1))
                    last.then_inc(c.up("sq_used"), 1)

            c = Pass(pe, "pre")
            c.wait("cact_ready", 1)
            for k4 in range(4):
                pe.wait_ge(ada_pre[k4], 16)
                for t in range(4 * k4, 4 * k4 + 4):
                    for k in range(KD):
                        last = pe.matmul(PM[:, t:t + 1], ADA[:, t, k, :], CA[:, k:k + 1], start=(k == 0), stop=(k == KD - 1))
                last.then_inc(c.up("misc_done"), 1)
                if k4 == 0:
                    sum_squares(c, lambda ct: zt(24 + ct % 2))
            c.wait("lo_ready", 8)
            pe.wait_ge(w_ready, 2)
            for k in range(KD):
                for n, (w, x) in enumerate(((0, 0), (0, KD), (1, 0))):
                    for h in range(2):
                        last = pe.matmul(PD[1][:, h * HALF:(h + 1) * HALF], WR[:, 1, w, k, :],
                                         HS[:, k + x, h * HALF:(h + 1) * HALF],
                                         start=(k == 0 and n == 0), stop=(k == KD - 1 and n == 2))
            last.then_inc(tile_done, 2)
            c.end()

            def turn(c, src, use):
                c.wait("misc_free", use)
                for n in range(NC):
                    last = pe.transpose(PM[:, n * P:(n + 1) * P], src[:, n * P:(n + 1) * P], IDENT)
                last.then_inc(c.up("misc_done"), 1)

            def ada_part(c, a, use):
                c.wait_dma("ada_ld", a + 1)
                c.wait("misc_free", use)
                for t in range(2):
                    for k in range(KD):
                        last = pe.matmul(PM[:, t:t + 1], ADX[:, t, k, :], CA[:, k:k + 1], start=(k == 0), stop=(k == KD - 1))
                last.then_inc(c.up("misc_done"), 1)

            def gram(c, use, lhs, rhs, rows):
                for h in range(2):
                    c.wait(f"gram_free{h}", use)
                    for n in range(4 * h, 4 * h + 4):
                        last = pe.matmul(PG[:, n * P:(n + 1) * P], lhs[rows, n * P:(n + 1) * P],
                                         rhs[rows, n * P:(n + 1) * P], start=True, stop=True)
                    last.then_inc(c.up("gram_done"), 1)

            def states(c, use, d, heads):
                c.wait("misc_free", use)
                KT = zt(KT0 + d)
                for n in (range(0, 7) if d == 0 else range(1, 8)):
                    for m, (rows, vt) in enumerate(heads):
                        last = pe.matmul(PM[rows, n * P:(n + 1) * P], KT[:, n * P + rows.start:n * P + rows.stop],
                                         zt(vt)[:, n * P:(n + 1) * P], start=True, stop=True)
                last.then_inc(c.up("misc_done"), 1)

            def outputs(c, use, rows, vt, a):
                c.wait("misc_free", use)
                for n in range(NC):
                    cols = slice(n * P, (n + 1) * P)
                    terms = [(zt(vt)[:, cols], zt(a)[:, cols])]
                    if n > 0:
                        terms.append((zt(S0)[rows, cols], zt(QD0)[rows, cols]))
                    if n < NC - 1:
                        terms.append((zt(S1)[rows, cols], zt(QD1)[rows, cols]))
                    for m, (l, r) in enumerate(terms):
                        last = pe.matmul(PM[:, cols], l, r, start=(m == 0), stop=(m == len(terms) - 1))
                last.then_inc(c.up("misc_done"), 1)

            def head_sums(c, use, nth, sq):
                c.wait("osq_ready", nth + 1)
                for h in range(2):
                    c.wait(f"gram_free{h}", use)
                    pe.matmul(PG[:, h * HALF:(h + 1) * HALF], ONES, zt(sq)[:, h * HALF:(h + 1) * HALF],
                              start=True, stop=True).then_inc(c.up("gram_done"), 1)

            ALL = slice(0, P)
            with pe.Fori(0, TRIPS["hgrn"]) as i:
                c = Pass(pe, "hgrn", i)
                dense(c, 0, KD, HS, KD)
                dense(c, 1, KD, HS, KD)
                ada_part(c, 0, 0)
                dense(c, 2, KD, HS, KD)
                dense(c, 3, KD, HS, KD)
                ada_part(c, 1, 1)
                c.wait_evac(3)
                turn(c, zt(V), 2)
                dense(c, 4, KD, HS, KD)
                dense(c, 5, KD, HS, KD)
                ada_part(c, 2, 3)
                c.wait("kdec_ready", 1)
                turn(c, zt(F0), 4)
                c.wait("kdec_ready", 2)
                turn(c, zt(F1), 5)
                c.wait("misc_free", 6)
                states(c, 6, 0, [(ALL, VT0)])
                states(c, 7, 1, [(ALL, VT0)])
                c.wait("ksum_ready", 1)
                gram(c, 0, zt(V), zt(Q), ALL)
                for q in range(NQ):
                    c.wait("x_ready", q + 1)
                    gram(c, 1 + q, zt(XB[q % 4]), zt(XB[q % 4]), ALL)
                    if q == 4:
                        dense(c, 6, KD, HS, KD)
                    if q == 9:
                        dense(c, 7, KD, HS, KD)
                        ada_part(c, 3, 8)
                c.wait("attn_ready", 1)
                outputs(c, 9, ALL, VT0, A0)
                head_sums(c, 15, 0, F1)
                c.end()

            ROWS = [slice(0, 64), slice(64, 128)]
            with pe.Fori(0, TRIPS["gla"]) as i:
                c = Pass(pe, "gla", i)
                c.wait_dma("lup_ld", 1)
                pe.wait_ge(lr_ld, 16)
                for d in range(2):
                    c.wait("misc_free", d)
                    for h in range(2):
                        last = pe.matmul(PM[:, h * HALF:(h + 1) * HALF], LUP[:, d, :], LR[:, h * HALF:(h + 1) * HALF],
                                         start=True, stop=True)
                    last.then_inc(c.up("misc_done"), 1)
                for j in range(4):
                    dense(c, j, KD, HS, KD)
                for hh in range(2):
                    c.wait_evac(2 + hh)
                    turn(c, zt(gV[hh]), 2 + hh)
                dense(c, 4, KD, HS, KD)
                for d in range(2):
                    c.wait("kdec_ready", d + 1)
                    turn(c, zt(F0 + d), 4 + d)
                c.wait("misc_free", 6)
                for d in range(2):
                    states(c, 6 + d, d, list(zip(ROWS, gVT)))
                for hh in range(2):
                    gram(c, hh, zt(K0), zt(Q), ROWS[hh])
                for q in range(NQ):
                    c.wait("x_ready", q + 1)
                    for hh in range(2):
                        gram(c, 2 + 2 * q + hh, zt(XB[q % 4]), zt(XB[q % 4]), ROWS[hh])
                    if q == 4:
                        dense(c, 5, KD, HS, KD)
                for hh in range(2):
                    c.wait("attn_ready", hh + 1)
                    outputs(c, 8 + hh, ROWS[hh], gVT[hh], gA[hh])
                    head_sums(c, 30 + hh, hh, XB[2 + hh])
                c.end()

            with pe.Fori(0, TRIPS["na"]) as i:
                c = Pass(pe, "na", i)
                for j in range(3):
                    dense(c, j, KD, HS, KD)
                c.wait_evac(2)
                turn(c, zt(NV), 0)
                for j in range(3, 6):
                    dense(c, j, KD, HS, KD)
                c.wait("misc_free", 1)
                c.wait("gram_free0", 0)
                c.wait("gram_free1", 0)
                for k in range(18):
                    c.wait("s_free", k)
                    if k >= 2:
                        c.wait("pt_ready", k - 1)
                        head, t, us = na_step(k - 2)
                        rows = ROWS[head]
                        for m, u in enumerate(us):
                            last = pe.matmul(PG[rows, OCOL:OCOL + P], zt(NVT)[:, u * P + rows.start:u * P + rows.stop],
                                             NPT[(k - 2) % 2][:, m * P:(m + 1) * P],
                                             start=(m == 0), stop=(m == len(us) - 1))
                    if k < 16:
                        head, t, us = na_step(k)
                        rows = ROWS[head]
                        n = len(us) * P
                        for lo in range(0, n, HALF):
                            hi = min(n, lo + HALF)
                            last = pe.matmul(PG[:, lo:hi], zt(NQT)[rows, t * P:(t + 1) * P],
                                             zt(NK)[rows, us[0] * P + lo:us[0] * P + hi], start=True, stop=True)
                    last.then_inc(c.up("s_done"), 1)
                    if 1 <= k <= 16:
                        c.wait("p_norm", k)
                        if k >= 2:
                            c.wait("pt_ready", k - 1)
                        for m in range(len(na_step(k - 1)[2])):
                            last = pe.transpose(PM[:, m * P:(m + 1) * P], NS[(k - 1) % 2][:, m * P:(m + 1) * P], IDENT)
                        last.then_inc(c.up("pt_done"), 1)
                c.end()

            c = Pass(pe, "mid")
            c.wait("lo_ready", 12)
            with pe.Fori(0, TRIPS["merge"]) as i:
                c = Pass(pe, "merge", i)
                for j in range(6):
                    dense(c, j, 4, BIG[:, 8 * (j % 3):8 * (j % 3) + 8, :], 4)
            c = Pass(pe, "mid2")
            c.wait("lo_ready", 8)
            with pe.Fori(0, TRIPS["out"]) as i:
                c = Pass(pe, "out", i)
                for j in range(2):
                    dense(c, j, KD, BIG, KD)
            c = Pass(pe, "n2")
            sum_squares(c, lambda ct: zt(24 + ct % 2))
            c.wait("lo_ready", 8)
            for g in range(2):
                with pe.Fori(0, TRIPS[f"up{g}"]) as i:
                    c = Pass(pe, f"up{g}", i)
                    for j in range(2):
                        dense(c, j, KD, HS, KD)
                c = Pass(pe, f"up{g}", TRIPS[f"up{g}"])
                c.wait("lo_ready", 0)
                with pe.Fori(0, TRIPS[f"dn{g}"]) as i:
                    c = Pass(pe, f"dn{g}", i)
                    for j in range(2):
                        dense(c, j, KF, BIG, KF)
            c = Pass(pe, "fin")
            sum_squares(c, lambda ct: H2[:, 8 + ct % 2, :])

        @block.scalar
        def _(act):
            act.sem_inc(sems["gram_free0"], 1)
            act.sem_inc(sems["gram_free1"], 1)
            act.sem_inc(sems["misc_free"], 1)
            act.sem_inc(sems["s_free"], 1)
            for m in range(3):
                act.sem_inc(sems[f"gate_st{m}"], 16)
            act.sem_inc(tile_free[0], 1)
            A = act.activation

            def squares(c, src, dst, first_free=True):
                for ct in range(KD):
                    if ct >= 2:
                        c.wait("sq_used", ct - 1)
                    c.own(A(dst(ct), src(ct), ACT.Square), "sq_ready")

            def rstd(c, dst, ps, width, name):
                c.own(A(dst, ps, ACT.Ln, bias=EP[:, 0:1], scale=1.0 / width), "act_own")
                c.own(A(dst, dst, ACT.Exp, scale=-0.5), name)

            c = Pass(act, "pre")
            act.wait_ge(const_ld, 48)
            c.own(A(CA[:, :], PRM[:, PC_C:PC_C + KD], ACT.Sigmoid), "act_own")
            c.wait("param_ready", 1)
            c.own(A(LB[:, 0, :], LB[:, 0, :], ACT.Exp), "act_own")
            act.wait_ge(x_ld, 16)
            squares(c, lambda ct: zt(16 + ct), lambda ct: zt(24 + ct % 2))
            c.wait("sq_used", 8)
            rstd(c, zt(24), PG[:, :], 1024.0, "rstd_ready")
            for ct in range(KD):
                c.wait("norm_ready", ct + 1)
                c.own(A(HS[:, ct, :], zt(16 + ct), ACT.Identity, bias=MOD[:, ct:ct + 1], scale=SCL[:, 0, ct:ct + 1]), "hi_ready")
            act.wait_ge(tile_done, 2)
            c.own(A(zt(0)[0:32, :], PD[1][0:32, :], ACT.Copy), "act_own")
            act.sem_inc(tile_free[1], 1)
            act.dma_start(lr_dr, zt(0)[0:32, :]).then_inc(lr_st, 16)
            act.wait_ge(lr_st, 16)
            c.end()

            def evac_turned(c, dst, use, nth):
                c.wait("misc_done", nth)
                c.free(A(dst, PM[:, :], ACT.Copy), "misc_free", use)

            def decays(c, d):
                c.wait("diff_ready", d + 1)
                x, lo = zt(XB[d]), 1 - d
                dst = zt(QD0) if d == 0 else zt(F1)
                c.own(A(chunked(dst), PX[:, d, :, lo:lo + P], ACT.Exp), "act_own")
                c.own(A(AN[:, d, :], PX[:, d, :, P], ACT.Exp), "act_own")
                c.own(A(x, x, ACT.Exp, scale=-1.0), "exp_ready")

            def level_exp(c, q):
                s = LEVELS[q // 2]
                c.wait("diff_ready", 2 + q + 1)
                x = blocks(zt(XB[q % 4]), s)
                c.own(A(x[:, :, 0:s], x[:, :, 0:s], ACT.Exp, scale=-1.0), "act_own")
                c.own(A(x[:, :, s:], x[:, :, s:], ACT.Exp), "exp_ready")

            def store_gate(c, j, m, first):
                c.wait_tile(j)
                c.wait_dma(f"gate_st{m}", 0)
                c.free_tile(A(zt(GB + m), PD[j % 2][:, :], ACT.Sigmoid), j)
                act.dma_start(gates_dr[bass.ds(c.i * 3 + (first + m), 1)].rearrange("n p t -> (n p) t"), zt(GB + m)
                              ).then_inc(c.up(f"gate_st{m}"), 16)

            def head_out(c, use, nth, ob, sq, rb, gu):
                c.wait("misc_done", use + MD[c.st])
                c.free(A(zt(ob), PM[:, :], ACT.Copy), "misc_free", use)
                c.own(A(zt(sq), zt(ob), ACT.Square), "osq_ready")
                c.wait("gram_done", 2 * gu + 2)
                c.own(A(zt(rb), PG[:, :], ACT.Ln, bias=EP[:, 0:1], scale=1.0 / P), "act_own")
                act.sem_inc(sems["gram_free0"], 1)
                act.sem_inc(sems["gram_free1"], 1)
                c.own(A(zt(rb), zt(rb), ACT.Exp, scale=-0.5), "orstd_ready")

            def store_o(c, nth, row, ob):
                c.wait("o_ready", nth + 1)
                act.dma_start(o_dr[bass.ds(row, 1)].rearrange("n p t -> (n p) t"), zt(ob)).then_inc(c.up("o_st"), 16)

            MD = {"hgrn": 1, "gla": 1}
            with act.Fori(0, TRIPS["hgrn"]) as i:
                c = Pass(act, "hgrn", i)
                c.wait_tile(0)
                c.own(A(zt(Q), PD[0][:, :], ACT.Sigmoid), "sig_ready")
                for d in range(2):
                    c.wait_tile(1 + d)
                    ps = PD[(1 + d) % 2]
                    c.own(A(zt(F0 + d), ps[:, :], ACT.Sigmoid), "act_own")
                    c.free_tile(A(zt(K0 + d), ps[:, :], ACT.Sigmoid, scale=-1.0), 1 + d)
                c.wait_tile(3)
                c.free_tile(A(zt(V), PD[1][:, :], ACT.Copy), 3)
                for d in range(2):
                    c.wait("ln_in", d + 1)
                    c.own(A(zt(XB[2 * d]), zt(XB[2 * d]), ACT.Ln), "act_own")
                    c.own(A(zt(XB[2 * d + 1]), zt(XB[2 * d + 1]), ACT.Ln), "ln_out")
                evac_turned(c, zt(VT0), 2, 3)
                for d in range(2):
                    decays(c, d)
                c.wait_tile(4)
                c.own(A(zt(G), PD[0][:, :], ACT.Sigmoid), "sig_ready")
                store_gate(c, 5, 0, 0)
                for d in range(2):
                    evac_turned(c, zt(KT0 + d), 4 + d, 5 + d)
                for h in range(2):
                    c.wait("gram_done", h + 1)
                    c.free(A(zt(A0)[:, h * HALF:(h + 1) * HALF], PG[:, h * HALF:(h + 1) * HALF], ACT.Copy), f"gram_free{h}", 0)
                for q in range(NQ):
                    level_exp(c, q)
                    if q == 8:
                        store_gate(c, 6, 1, 0)
                store_gate(c, 7, 2, 0)
                head_out(c, 9, 0, F0, F1, XB[0], 15)
                store_o(c, 0, i + 8, F0)
                c.wait_dma("o_st", 1)
                c.end()

            act.dma_start(LR[:, :], lr_dr).then_inc(lr_ld, 16)
            for m in range(3):
                Pass(act, "gla").wait_dma(f"gate_st{m}", 0)
            with act.Fori(0, TRIPS["gla"]) as i:
                c = Pass(act, "gla", i)
                act.dma_start(LUP[:, :, :], lup[bass.ds(i, 1)].rearrange("n r d m -> (n r) d m")
                              ).then_inc(c.up("lup_ld"), 16)
                for d in range(2):
                    c.wait("misc_done", d + 1)
                    c.free(A(zt(F0 + d), PM[:, :], ACT.Identity, bias=PRM[:, bass.ds(i + (PC_ZB + 2 * d), 1)]), "misc_free", d)
                c.wait_tile(0)
                c.free_tile(A(zt(Q), PD[0][:, :], ACT.Copy, scale=0.125), 0)
                c.wait_tile(1)
                c.free_tile(A(zt(K0), PD[1][:, :], ACT.Copy), 1)
                for d in range(2):
                    c.wait("ln_in", d + 1)
                    x = zt(XB[d])
                    c.own(A(x, x, ACT.Exp, scale=-1.0), "act_own")
                    c.own(A(x, x, ACT.Ln, bias=EP[:, 1:2]), "ln_out")
                for hh in range(2):
                    c.wait_tile(2 + hh)
                    c.free_tile(A(zt(gV[hh]), PD[hh][:, :], ACT.Copy), 2 + hh)
                for hh in range(2):
                    evac_turned(c, zt(gVT[hh]), 2 + hh, 3 + hh)
                for d in range(2):
                    decays(c, d)
                c.wait_tile(4)
                c.own(A(zt(gG[0]), PD[0][:, :], ACT.Sigmoid), "sig_ready")
                for d in range(2):
                    evac_turned(c, zt(KT0 + d), 4 + d, 5 + d)
                for hh in range(2):
                    for h in range(2):
                        c.wait("gram_done", 2 * hh + h + 1)
                        c.free(A(zt(gA[hh])[:, h * HALF:(h + 1) * HALF], PG[:, h * HALF:(h + 1) * HALF], ACT.Copy, scale=2.0),
                               f"gram_free{h}", hh)
                for q in range(NQ):
                    level_exp(c, q)
                    if q == 8:
                        c.wait_tile(5)
                        c.own(A(zt(gG[1]), PD[1][:, :], ACT.Sigmoid), "sig_ready")
                for hh in range(2):
                    head_out(c, 8 + hh, hh, F0 + hh, XB[2 + hh], XB[hh], 30 + hh)
                    store_o(c, hh, i * 2 + (4 + hh), F0 + hh)
                c.wait_dma("o_st", 2)
                c.end()

            act.wait_ge(rpb_st, 16 * 16)
            act.dma_start(NCM[:, :], cmask).then_inc(cmask_ld, 16)
            with act.Fori(0, TRIPS["na"]) as i:
                c = Pass(act, "na", i)
                act.dma_start(NTR[:, :, :], bias_dr[bass.ds(i * 2, 2)].rearrange("e p x -> p e x")).then_inc(c.up("bias_ld"), 16)
                c.wait_tile(0)
                c.free_tile(A(zt(NQT), PD[0][:, :], ACT.Copy, scale=0.125), 0)
                c.wait_tile(1)
                c.free_tile(A(zt(NK), PD[1][:, :], ACT.Copy), 1)
                c.wait_tile(2)
                c.free_tile(A(zt(NV), PD[0][:, :], ACT.Copy), 2)
                evac_turned(c, zt(NVT), 0, 1)
                for m in range(3):
                    store_gate(c, 3 + m, m, 12)
                for k in range(17):
                    if k < 16:
                        n = len(na_step(k)[2]) * P
                        c.wait("max_ready", k + 1)
                        s = NS[k % 2][:, 0:n]
                        c.own(A(s, s, ACT.Exp, bias=SM[:, 4 + k % 2:5 + k % 2], accum_out=SM[:, 8 + k % 2:9 + k % 2]), "p_exp")
                    if k >= 1:
                        n = len(na_step(k - 1)[2]) * P
                        c.wait("pt_done", k)
                        c.own(A(NPT[(k - 1) % 2][:, 0:n], PM[:, 0:n], ACT.Copy), "pt_ready")
                store_o(c, 0, i, NO)
                c.wait_dma("o_st", 1)
                c.end()
            for m in range(3):
                Pass(act, "mid").wait_dma(f"gate_st{m}", 0)

            c = Pass(act, "mid")
            def load_o(n):
                act.dma_start(H2[:, n % 2, :], o_dr[n]).then_inc(c.up(f"in_ld{n % 2}"), 16)
            load_o(0)
            for n in range(12):
                if n + 1 < 12:
                    if n >= 1:
                        c.wait("lo_ready", n)
                    load_o(n + 1)
                c.wait_dma(f"in_ld{n % 2}", n // 2 + 1)
                c.own(A(BIG[:, 8 * (n // 4) + n % 4, :], H2[:, n % 2, :], ACT.Copy), "hi_ready")
            c.end()
            with act.Fori(0, TRIPS["merge"]) as i:
                c = Pass(act, "merge", i)
                for j in range(6):
                    act.wait_ge(tile_free[j % 2], c.tile_half(j))
                    act.dma_start(zt(24 + j % 2), gates_dr[bass.ds(i * 6 + j, 1)].rearrange("n p t -> (n p) t")
                                  ).then_inc(c.up(f"in_ld{j % 2}"), 16)
                c.end()
            c = Pass(act, "mid2")
            c.wait("merged", 0)
            for ct in range(KD):
                c.own(A(BIG[:, ct, :], H2[:, 4 + ct, :], ACT.Copy), "hi_ready")
            c.end()
            with act.Fori(0, TRIPS["out"]) as i:
                c = Pass(act, "out", i)
                for j in range(2):
                    act.wait_ge(tile_free[j], c.tile_half(j))
                    act.dma_start(zt(24 + j), xt[:, bass.ds(i * 2 + j, 1), :].rearrange("p n t -> p (n t)")
                                  ).then_inc(c.up(f"in_ld{j}"), 16)
                for j in range(2):
                    c.wait_evac(j)
                    act.dma_start(y_dr[bass.ds(i * 2 + j, 1)].rearrange("n p t -> (n p) t"),
                                  ZT[:, bass.ds(i * 2 + (16 + j), 1), :].rearrange("p n t -> p (n t)")
                                  ).then_inc(c.up(f"y_st{j}"), 16)
                c.end()
            c = Pass(act, "n2")
            squares(c, lambda ct: zt(16 + ct), lambda ct: zt(24 + ct % 2))
            c.wait("sq_used", 8)
            for j in range(2):
                c.wait_dma(f"y_st{j}", 0)
            rstd(c, zt(0), PG[:, :], 1024.0, "rstd_ready")
            for ct in range(KD):
                c.wait("norm_ready", ct + 1)
                c.own(A(HS[:, ct, :], zt(16 + ct), ACT.Identity, bias=MOD[:, 24 + ct:25 + ct], scale=SCL[:, 1, ct:ct + 1]), "hi_ready")
            c.wait("lo_ready", 8)
            c.end()
            for g in range(2):
                with act.Fori(0, TRIPS["up0"]) as i:
                    c = Pass(act, f"up{g}", i)
                    c.wait_tile(0)
                    c.free_tile(A(zt(24), PD[0][:, :], ACT.Silu), 0)
                    c.wait_evac(1)
                    c.own(A(BIG[:, bass.ds(i, 1), :].rearrange("p n t -> p (n t)"), zt(25), ACT.Copy), "hi_ready")
                    c.end()
                c = Pass(act, f"up{g}", TRIPS["up0"])
                c.wait("lo_ready", 0)
                with act.Fori(0, TRIPS["dn0"]) as i:
                    c = Pass(act, f"dn{g}", i)
                    for j in range(2):
                        if g == 0:
                            c.wait_dma(f"y_st{j}", 0)
                        else:
                            act.wait_ge(tile_free[j], c.tile_half(j))
                        act.dma_start(zt(24 + j), y_dr[bass.ds(i * 2 + j, 1)].rearrange("n p t -> (n p) t")
                                      ).then_inc(c.up(f"in_ld{j}"), 16)
                    if g == 0:
                        for j in range(2):
                            c.wait_evac(j)
                            act.dma_start(y_dr[bass.ds(i * 2 + j, 1)].rearrange("n p t -> (n p) t"), zt(24 + j)
                                          ).then_inc(c.up(f"y_st{j}"), 16)
                    c.end()
                if g == 0:
                    for j in range(2):
                        Pass(act, "up1").wait_dma(f"y_st{j}", 0)
            c = Pass(act, "fin")
            for j in range(2):
                act.wait_ge(tile_free[j], base["tile"]["fin"] // 2)
            squares(c, lambda ct: H2[:, ct, :], lambda ct: H2[:, 8 + ct % 2, :])
            c.wait("sq_used", 8)
            rstd(c, H2[:, 10, :], PG[:, :], 1024.0, "rstd_ready")
            for ct in range(KD):
                c.wait("norm_ready", ct + 1)
                act.dma_start(out[ct], H2[:, ct, :]).then_inc(c.up("out_st"), 16)
            c.wait_dma("out_st", 8)
            c.end()

        @block.vector
        def _(dve):
            tt, ts, stt = dve.tensor_tensor, dve.tensor_scalar, dve.scalar_tensor_tensor

            def scaled_split(c, x, a, b, ct):
                c.wait("hi_ready", ct + 1)
                c.own(ts(x, x, a, b, ALU.mult, ALU.add), "dve_own")
                c.own(tt(HS[:, KD + ct, :], x, HS[:, ct, :].bitcast(F32), ALU.subtract), "lo_ready")

            c = Pass(dve, "pre")
            own = lambda ins: c.own(ins, "dve_own")
            own(dve.memset(EP[:, 0:1], EPS))
            own(dve.memset(EP[:, 1:2], 1.0))
            dve.wait_ge(const_ld, 48)
            own(dve.tensor_copy(MASK[:, :, :], MASKF[:, :, :]))
            lb, lg = LB[:, 0, :], PRM[:, PC_LB:PC_LB + 8]
            c.own(tt(lb, lg, lg, ALU.subtract), "param_ready")
            c.wait("act_own", 1)
            c.own(tt(CA[:, :], CA[:, :], PRM[:, PC_C:PC_C + KD], ALU.mult), "cact_ready")
            c.wait("act_own", 2)
            own(dve.reciprocal(LB[:, 1, :], lb))
            own(tt(lb, lb, LB[:, 1, :], ALU.mult))
            own(tt(lb, lb, lb, ALU.subtract))
            own(ts(lb, lb, 0.0, 1.0, ALU.max, ALU.min))
            own(ts(LB[:, 1, :], lb, -1.0, 1.0, ALU.mult, ALU.add))
            c.wait("misc_done", 4)
            c.free(tt(MOD[:, 0:NADA], PM[:, 0:NADA], PRM[:, PC_BADA:PC_BADA + NADA], ALU.add), "misc_free", 0)
            own(ts(SCL[:, 0, :], MOD[:, 8:16], 1.0, None, ALU.add))
            own(tt(SCL[:, 0, :], SCL[:, 0, :], PRM[:, PC_N1:PC_N1 + KD], ALU.mult))

            def norm(c, first, rb, w, s):
                c.wait("rstd_ready", 1)
                for ct in range(KD + 1):
                    if ct < KD:
                        c.own(tt(zt(first + ct), zt(first + ct), rb, ALU.mult), "norm_ready")
                    if ct > 0:
                        scaled_split(c, zt(first + ct - 1), SCL[:, s, ct - 1:ct], MOD[:, w + ct - 1:w + ct], ct - 1)

            norm(c, 16, zt(24), 0, 0)
            dve.wait_ge(lr_st, 16)
            own(dve.memset(PX[:, :, :, 0:1], 0.0))
            c.end()

            def add_ada(c, a, use, nth):
                c.wait("misc_done", nth)
                c.free(tt(MOD[:, bass.ds(c.i * 8 + (NADA + 2 * a), 2)], PM[:, 0:2],
                          PRM[:, bass.ds(c.i * 8 + (PC_BADA + NADA + 2 * a), 2)], ALU.add), "misc_free", use)

            def cumulate(c, d):
                for n in range(NC):
                    ins = dve.tensor_tensor_scan(PX[:, d, n, 1:P + 1], ONES, zt(F0 + d)[:, n * P:(n + 1) * P], 0.0,
                                                 ALU.mult, ALU.add)
                    c.own(ins, "dve_own")
                lo = 1 - d
                c.own(tt(chunked(zt(XB[d])), PX[:, d, :, lo:lo + P], px_last(d), ALU.subtract), "diff_ready")

            def decayed(c, k0, k1):
                c.wait("exp_ready", 1)
                c.own(tt(zt(F0), zt(k0), zt(XB[0]), ALU.mult), "kdec_ready")
                c.own(tt(zt(QD0), zt(QD0), zt(Q), ALU.mult), "dve_own")
                c.wait("exp_ready", 2)
                c.own(tt(zt(F1), zt(k1), zt(F1), ALU.mult), "kdec_ready")
                c.own(tt(zt(QD1), zt(Q), zt(XB[1]), ALU.mult), "dve_own")

            def level_diff(c, q):
                s, d = LEVELS[q // 2], q % 2
                v, r = px_view(d, s)
                o = zt(XB[q % 4]).rearrange("p (c b t) -> p c b t", c=NC, t=2 * s)
                c.own(tt(o, v, r, ALU.subtract), "diff_ready")

            def level_products(c, q, k0, k1):
                s, d = LEVELS[q // 2], q % 2
                c.wait("exp_ready", 2 + q + 1)
                x = blocks(zt(XB[q % 4]), s)
                a, b = (k0, Q) if d == 0 else (Q, k1)
                c.own(tt(x[:, :, 0:s], x[:, :, 0:s], blocks(zt(a), s)[:, :, 0:s], ALU.mult), "dve_own")
                c.own(tt(x[:, :, s:], x[:, :, s:], blocks(zt(b), s)[:, :, s:], ALU.mult), "x_ready")

            def level_select(c, q, a, use, name=None):
                for h in range(2):
                    c.wait("gram_done", 2 * use + h + 1)
                    dve.sem_inc(dve_step, 1)
                    ins = dve.copy_predicated(chunked(zt(a)[:, h * HALF:(h + 1) * HALF]),
                                              MASK[:, q:q + 1, :].to_broadcast([P, 4, P]),
                                              chunked(PG[:, h * HALF:(h + 1) * HALF]))
                    c.free(ins, f"gram_free{h}", use)

            def carry(c, use, d):
                c.wait("misc_done", use + 1)
                S = chunked(zt(S0 + d))
                ps = chunked(PM[:, :])
                order = list(range(0, 7)) if d == 0 else list(range(7, 0, -1))
                for m, n in enumerate(order):
                    to = S[:, n + 1 if d == 0 else n - 1, :]
                    if m == 0:
                        ins = dve.tensor_copy(to, ps[:, n, :])
                    else:
                        ins = stt(to, S[:, n, :], AN[:, d, n:n + 1], ps[:, n, :], ALU.mult, ALU.add)
                    if m == len(order) - 1:
                        c.free(ins, "misc_free", use)
                    else:
                        c.own(ins, "dve_own")

            def finish_head(c, nth, ob, rb, g, w):
                c.wait("orstd_ready", nth + 1)
                c.own(stt(zt(ob), zt(ob), PRM[:, w:w + 1], zt(rb), ALU.mult, ALU.mult), "dve_own")
                c.own(tt(zt(ob), zt(ob), zt(g), ALU.mult), "o_ready")

            with dve.Fori(0, TRIPS["hgrn"]) as i:
                c = Pass(dve, "hgrn", i)
                own = lambda ins: c.own(ins, "dve_own")
                c.wait("sig_ready", 1)
                c.free_tile(tt(zt(Q), zt(Q), PD[0][:, :], ALU.mult), 0)
                add_ada(c, 0, 0, 1)
                for d in range(2):
                    c.wait_evac(1 + d)
                    f, k, x0, x1 = zt(F0 + d), zt(K0 + d), zt(XB[2 * d]), zt(XB[2 * d + 1])
                    lbc, oml = LB[:, 0, bass.ds(i + 4 * d, 1)], LB[:, 1, bass.ds(i + 4 * d, 1)]
                    own(ts(f, f, oml, lbc, ALU.mult, ALU.add))
                    own(ts(k, k, oml, None, ALU.mult))
                    own(ts(x0, f, LN_SPLIT, None, ALU.max))
                    own(ts(x1, f, 1.0 / LN_SPLIT, F_FLOOR / LN_SPLIT, ALU.mult, ALU.max))
                    c.own(ts(x1, x1, 1.0, None, ALU.min), "ln_in")
                for d in range(2):
                    c.wait("ln_out", d + 1)
                    own(tt(zt(F0 + d), zt(XB[2 * d]), zt(XB[2 * d + 1]), ALU.add))
                    cumulate(c, d)
                add_ada(c, 1, 1, 2)
                decayed(c, K0, K1)
                c.wait("sig_ready", 2)
                c.free_tile(tt(zt(G), zt(G), PD[0][:, :], ALU.mult), 4)
                level_diff(c, 0)
                level_diff(c, 1)
                add_ada(c, 2, 3, 4)
                c.wait("misc_done", 3)
                c.own(tt(zt(V), zt(K0), zt(K1), ALU.add), "ksum_ready")
                carry(c, 6, 0)
                carry(c, 7, 1)
                c.wait("gram_free0", 1)
                c.wait("gram_free1", 1)
                for q in range(NQ + 1):
                    if q < NQ:
                        level_products(c, q, K0, K1)
                    if q + 2 < NQ:
                        if q >= 2:
                            c.wait("gram_done", 2 * q)
                        level_diff(c, q + 2)
                    if q >= 1:
                        level_select(c, q - 1, A0, q)
                    if q == 10:
                        add_ada(c, 3, 8, 9)
                c.own(dve.memset(SM[:, 15:16], 0.0), "attn_ready")
                finish_head(c, 0, F0, XB[0], G, PC_HN)
                c.end()

            with dve.Fori(0, TRIPS["gla"]) as i:
                c = Pass(dve, "gla", i)
                own = lambda ins: c.own(ins, "dve_own")
                for d in range(2):
                    c.wait("misc_free", d + 1)
                    f, x = zt(F0 + d), zt(XB[d])
                    c.own(stt(x, f, -1.0, f, ALU.mult, ALU.max), "ln_in")
                for d in range(2):
                    c.wait("ln_out", d + 1)
                    f = zt(F0 + d)
                    own(stt(f, f, 0.0, zt(XB[d]), ALU.min, ALU.subtract))
                    own(ts(f, f, 1.0 / 16.0, None, ALU.mult))
                    cumulate(c, d)
                c.wait_evac(0)
                c.wait_evac(1)
                decayed(c, K0, K0)
                c.wait("sig_ready", 1)
                c.free_tile(tt(zt(gG[0]), zt(gG[0]), PD[0][:, :], ALU.mult), 4)
                level_diff(c, 0)
                level_diff(c, 1)
                carry(c, 6, 0)
                carry(c, 7, 1)
                c.wait("gram_free0", 2)
                c.wait("gram_free1", 2)
                for q in range(NQ + 1):
                    if q < NQ:
                        level_products(c, q, K0, K0)
                    if q + 2 < NQ:
                        if q >= 2:
                            c.wait("gram_done", 4 * q)
                        level_diff(c, q + 2)
                    if q >= 1:
                        for hh in range(2):
                            level_select(c, q - 1, gA[hh], 2 * q + hh)
                    if q == 9:
                        c.wait("sig_ready", 2)
                        c.free_tile(tt(zt(gG[1]), zt(gG[1]), PD[1][:, :], ALU.mult), 5)
                for hh in range(2):
                    c.own(dve.memset(SM[:, 15:16], 0.0), "attn_ready")
                for hh in range(2):
                    finish_head(c, hh, F0 + hh, XB[hh], gG[hh], PC_GN)
                c.end()

            dve.wait_ge(cmask_ld, 16)
            with dve.Fori(0, TRIPS["na"]) as i:
                c = Pass(dve, "na", i)
                own = lambda ins: c.own(ins, "dve_own")
                c.wait_dma("bias_ld", 1)
                tr = NTR[:, :, :].rearrange("p e (r k) -> p (e r) k", k=64)
                cm = NCM[:, 0:64].rearrange("p (o k) -> p o k", o=1).to_broadcast([P, 28, 64])
                own(tt(tr, tr, cm, ALU.add))
                for e in range(2):
                    own(tt(NTI[:, e, :], NTR[:, e, P:6 * P], NCM[:, 64:64 + 5 * P], ALU.add))
                for k in range(18):
                    c.wait("s_done", k + 1)
                    if k < 16:
                        head, t, us = na_step(k)
                        n = len(us) * P
                        at = (us[0] - t + 3) * P
                        bias = NTI[:, head, 0:n] if len(us) == 5 else NTR[:, head, at:at + n]
                        dve.sem_inc(dve_step, 1)
                        ins = dve.tensor_tensor_reduce(NS[k % 2][:, 0:n], PG[:, 0:n], bias, 1.0, -3.0e38, ALU.add, ALU.max,
                                                       SM[:, k % 2:k % 2 + 1])
                        if k < 2:
                            c.own(ins, "s_free")
                        else:
                            own(ins)
                    if k >= 2:
                        head, t, us = na_step(k - 2)
                        rows = slice(64 * head, 64 * head + 64)
                        ins = dve.tensor_copy(zt(NO)[rows, t * P:(t + 1) * P], PG[rows, OCOL:OCOL + P])
                        c.own(ins, "s_free")
                    if k < 16:
                        c.own(ts(SM[:, 4 + k % 2:5 + k % 2], SM[:, k % 2:k % 2 + 1], -1.0, None, ALU.mult), "max_ready")
                    if 1 <= k <= 16:
                        m = (k - 1) % 2
                        n = len(na_step(k - 1)[2]) * P
                        c.wait("p_exp", k)
                        own(dve.reciprocal(SM[:, 12 + m:13 + m], SM[:, 8 + m:9 + m]))
                        c.own(ts(NS[m][:, 0:n], NS[m][:, 0:n], SM[:, 12 + m:13 + m], None, ALU.mult), "p_norm")
                c.own(dve.memset(SM[:, 15:16], 0.0), "o_ready")
                c.end()

            c = Pass(dve, "mid")
            for n in range(12):
                at = 8 * (n // 4) + n % 4
                c.wait("hi_ready", n + 1)
                c.own(tt(BIG[:, at + 4, :], H2[:, n % 2, :], BIG[:, at, :].bitcast(F32), ALU.subtract), "lo_ready")
            c.end()
            with dve.Fori(0, TRIPS["merge"]) as i:
                c = Pass(dve, "merge", i)
                for j in range(6):
                    m = H2[:, bass.ds(i * 2 + (4 + j // 3), 1), :].rearrange("p n t -> p (n t)")
                    c.wait_dma(f"in_ld{j % 2}", j // 2 + 1)
                    c.wait_tile(j)
                    to = m if j % 3 == 0 else H2[:, 2, :]
                    c.free_tile(tt(to, zt(24 + j % 2), PD[j % 2][:, :], ALU.mult), j)
                    if j % 3:
                        c.own(tt(m, m, H2[:, 2, :], ALU.add), "dve_own" if j % 3 == 1 else "merged")
                c.end()
            c = Pass(dve, "mid2")
            for ct in range(KD):
                c.wait("hi_ready", ct + 1)
                c.own(tt(BIG[:, KD + ct, :], H2[:, 4 + ct, :], BIG[:, ct, :].bitcast(F32), ALU.subtract), "lo_ready")
            c.end()
            with dve.Fori(0, TRIPS["out"]) as i:
                c = Pass(dve, "out", i)
                for j in range(2):
                    x1 = ZT[:, bass.ds(i * 2 + (16 + j), 1), :].rearrange("p n t -> p (n t)")
                    c.wait_dma(f"in_ld{j}", 1)
                    c.wait_tile(j)
                    c.free_tile(stt(x1, PD[j][:, :], MOD[:, bass.ds(i * 2 + (16 + j), 1)], zt(24 + j), ALU.mult, ALU.add), j)
                c.end()
            c = Pass(dve, "n2")
            own = lambda ins: c.own(ins, "dve_own")
            own(ts(SCL[:, 1, :], MOD[:, 32:40], 1.0, None, ALU.add))
            own(tt(SCL[:, 1, :], SCL[:, 1, :], PRM[:, PC_N2:PC_N2 + KD], ALU.mult))
            norm(c, 16, zt(0), 24, 1)
            c.end()
            for g in range(2):
                with dve.Fori(0, TRIPS["up0"]) as i:
                    c = Pass(dve, f"up{g}", i)
                    c.wait_evac(0)
                    c.wait_tile(1)
                    c.free_tile(tt(zt(25), zt(24), PD[1][:, :], ALU.mult), 1)
                    c.wait("hi_ready", 1)
                    hi = BIG[:, bass.ds(i, 1), :].rearrange("p n t -> p (n t)")
                    lo = BIG[:, bass.ds(i + KF, 1), :].rearrange("p n t -> p (n t)")
                    c.own(tt(lo, zt(25), hi.bitcast(F32), ALU.subtract), "lo_ready")
                    c.end()
                with dve.Fori(0, TRIPS["dn0"]) as i:
                    c = Pass(dve, f"dn{g}", i)
                    for j in range(2):
                        y = zt(24 + j) if g == 0 else H2[:, bass.ds(i * 2 + j, 1), :].rearrange("p n t -> p (n t)")
                        c.wait_dma(f"in_ld{j}", 1)
                        c.wait_tile(j)
                        c.free_tile(stt(y, PD[j][:, :], MOD[:, bass.ds(i * 2 + (40 + j), 1)], zt(24 + j), ALU.mult, ALU.add), j)
                    c.end()
            c = Pass(dve, "fin")
            c.wait("rstd_ready", 1)
            for ct in range(KD):
                y = H2[:, ct, :]
                c.own(stt(y, y, PRM[:, PC_NF + ct:PC_NF + ct + 1], H2[:, 10, :], ALU.mult, ALU.mult), "norm_ready")
            c.end()


_NAMES = ["x", "c", "w_ada", "b_ada", "norm1_w", "w_in", "na_rpb", "gla_lr_up", "gla_lr_bias", "gla_norm_w",
          "hgrn_lb_logits", "hgrn_norm_w", "w_proj_na", "w_proj_gla", "w_proj_hgrn", "w_out", "norm2_w",
          "w_ffn_gate", "w_ffn_up", "w_ffn_down", "final_norm_w"]


def kernel(**inputs):
    import numpy as np
    import concourse.bacc as _bacc
    from concourse import mybir as _mybir
    from concourse.bass_utils import run_bass_kernel_spmd as _run

    a = {k: np.asarray(inputs[k]) for k in _NAMES}

    cols = lambda v: v.reshape(-1, P).T
    lrb = a["gla_lr_bias"][0].reshape(2, 2, P).reshape(4, P).T
    prm = np.concatenate([cols(a["c"][0]), cols(a["b_ada"][0]), cols(a["norm1_w"][0]), cols(a["norm2_w"][0]),
                          cols(a["final_norm_w"]), cols(a["gla_norm_w"][0]), cols(a["hgrn_norm_w"][0]),
                          cols(a["hgrn_lb_logits"][0]), lrb], axis=1)
    xt = a["x"][0].T.reshape(KD, P, T).transpose(1, 0, 2)
    pieces = lambda w: w.reshape(w.shape[0] // P, P, w.shape[1] // P, P).transpose(2, 1, 0, 3)
    w_ada = pieces(a["w_ada"][0]).transpose(1, 0, 2, 3)
    w = a["w_in"][0]
    w_lr = np.concatenate([w[:, 3072:3104], np.zeros((D_MODEL, P - 32), w.dtype)], axis=1)
    w_lr = pieces(w_lr)[0]
    order = []
    gate = [5664 + (g % 3) * D_MODEL + (g // 3) * P for g in range(24)]
    for h in range(4):
        order += [3104 + P * h, 3616 + P * h, 4128 + P * h, 4640 + P * h, 5152 + P * h] + gate[3 * h:3 * h + 3]
    for p in range(2):
        order += [1536 + P * p, 1792 + P * p, 2048 + 2 * P * p, 2048 + 2 * P * p + P, 2560 + 2 * P * p, 2560 + 2 * P * p + P]
    for p in range(4):
        order += [P * p, 512 + P * p, 1024 + P * p] + gate[12 + 3 * p:15 + 3 * p]
    w_in = pieces(np.concatenate([w[:, o:o + P] for o in order], axis=1))
    pr = [pieces(a[f"w_proj_{b}"][0]) for b in ("na", "gla", "hgrn")]
    w_proj = np.stack([pr[n % 3][n // 3] for n in range(24)])
    w_out = pieces(a["w_out"][0])
    wg, wu, wd = pieces(a["w_ffn_gate"][0]), pieces(a["w_ffn_up"][0]), pieces(a["w_ffn_down"][0])
    w_up = np.stack([wg, wu], axis=1).reshape(2, 2 * KF, P, KD, P)
    w_dn = np.stack([wd[:, :, 0:KF], wd[:, :, KF:2 * KF]])
    lup = np.zeros((2, 32, 2, P), w.dtype)
    for s in range(2):
        for p in range(2):
            lup[p, 16 * s:16 * s + 16, s, :] = a["gla_lr_up"][0, s, :, p * P:(p + 1) * P]
    rpb = np.zeros((8, 15, P), w.dtype)
    rpb[:, :, 48:79] = a["na_rpb"][0]

    masks = np.zeros((P, NQ, P), np.float32)
    j, i = np.arange(P)[:, None], np.arange(P)[None, :]
    for n, s in enumerate(LEVELS):
        same = (j // (2 * s)) == (i // (2 * s))
        masks[:, 2 * n, :] = same & (j % (2 * s) < s) & (i % (2 * s) >= s)
        masks[:, 2 * n + 1, :] = same & (j % (2 * s) >= s) & (i % (2 * s) < s)
    cmat = np.stack([np.ones((P, P), np.float32), np.eye(P, dtype=np.float32)], axis=1)
    qr, qc = np.arange(P) // 64, np.arange(P) % 64
    start = np.clip(qc - 8, 0, 48)
    kc = np.arange(64)
    cmask = np.zeros((P, 64 + 5 * P), np.float32)
    cmask[:, 0:64][(kc[None, :] < start[:, None]) | (kc[None, :] >= start[:, None] + 16)] = NEG_INF
    kr = np.arange(5 * P) // 64 - 4
    off = kr[None, :] - qr[:, None]
    cmask[:, 64:][(off < -4) | (off > 3)] = NEG_INF

    nc = _bacc.Bacc("TRN2", target_bir_lowering=False, num_devices=1)
    arrays, args = {}, []
    for name, v in (("prm", prm), ("masks", masks), ("cmat", cmat), ("cmask", cmask), ("xt", xt), ("w_ada", w_ada),
                    ("w_lr", w_lr), ("w_in", w_in), ("w_proj", w_proj), ("w_out", w_out), ("w_up", w_up),
                    ("w_dn", w_dn), ("lup", lup), ("rpb", rpb)):
        v = np.ascontiguousarray(v)
        arrays[f"in_{name}_dram"] = v
        args.append(nc.dram_tensor(f"in_{name}_dram", v.shape, _mybir.dt.from_np(v.dtype), kind="ExternalInput").ap())
    args.append(nc.dram_tensor("out_0_dram", (KD, P, T), _mybir.dt.float32, kind="ExternalOutput").ap())
    trunk(nc, *args)
    r = _run(nc, [arrays], core_ids=[0])
    got = r.results[0]["out_0_dram"]
    return got.transpose(2, 0, 1).reshape(1, T, D_MODEL)
```

```python
import concourse.bass as bass
from concourse import mybir
from contextlib import ExitStack

F32 = mybir.dt.float32
F32R = mybir.dt.float32r
U8 = mybir.dt.uint8
ACT = mybir.ActivationFunctionType
ALU = mybir.AluOpType

P = 128
D_MODEL = 1024
T = 1024
KD = 8
HALF = 512
NC = 8
LEVELS = [64, 32, 16, 8, 4, 2, 1]
NQ = 2 * len(LEVELS)
NADA = 16
EPS = 1e-6
F_FLOOR = 1e-30
LN_SPLIT = 2.0 ** -50
KF = 11
NEG_INF = -1e30

PC_C, PC_BADA, PC_N1, PC_N2, PC_NF, PC_GN, PC_HN, PC_LB, PC_ZB = 0, 8, 56, 64, 72, 80, 81, 82, 90
NPRM = 94

TRIPS = dict(pre=1, hgrn_in=1, hgrn=3, hgrn_last=1, gla=2, na=4, mid=1, merge=4, mid2=1, out=4, n2=1, up0=11, dn0=4, up1=11, dn1=4, fin=1)
TILES = dict(pre=2, hgrn_in=4, hgrn=8, hgrn_last=8, gla=8, na=4, merge=6, out=2, up0=2, dn0=2, up1=2, dn1=2)
PLAN = {
    "tile": (0, TILES),
    "gram_done": (0, dict(hgrn=18, gla=36)),
    "gram_free0": (1, dict(hgrn=9, gla=18, na=1)),
    "gram_free1": (1, dict(hgrn=9, gla=18)),
    "misc_done": (0, dict(hgrn=6, gla=10, na=1)),
    "misc_free": (1, dict(hgrn=6, gla=10, na=1)),
    "dve_own": (0, dict(pre=37, hgrn_in=26, hgrn=56, hgrn_last=30, gla=50, na=27, merge=2, mid2=1, n2=10)),
    "act_own": (0, dict(pre=4, hgrn_in=4, hgrn=23, hgrn_last=19, gla=22, n2=1, fin=1)),
    "param_ready": (0, dict(pre=1)),
    "sig_ready": (0, dict(hgrn=2, gla=2)),
    "f_ready": (0, dict(hgrn_in=2, hgrn=2, hgrn_last=0)),
    "ln_in": (0, dict(hgrn_in=2, hgrn=2, hgrn_last=0, gla=2)),
    "ln_out": (0, dict(hgrn_in=2, hgrn=2, hgrn_last=0, gla=2)),
    "diff_ready": (0, dict(hgrn_in=2, hgrn=NQ + 2, hgrn_last=NQ, gla=2 + NQ)),
    "exp_ready": (0, dict(hgrn=2 + NQ, gla=2 + NQ)),
    "ksum_ready": (0, dict(hgrn=1)),
    "kdec_ready": (0, dict(hgrn=2, gla=2)),
    "x_ready": (0, dict(hgrn=NQ, gla=NQ)),
    "attn_ready": (0, dict(hgrn=1, gla=2)),
    "osq_ready": (0, dict(hgrn=1, gla=2)),
    "orstd_ready": (0, dict(hgrn=1, gla=2)),
    "o_ready": (0, dict(hgrn=1, gla=2)),
    "sq_ready": (0, dict(pre=8, out=2, dn1=2)),
    "sq_used": (0, dict(pre=8)),
    "acc_ready": (0, dict(out=2, dn1=2)),
    "sum_done": (0, dict(n2=1, fin=1)),
    "rstd_ready": (0, dict(pre=1, n2=1, fin=1)),
    "norm_ready": (0, dict(pre=8, n2=8, fin=8)),
    "hi_ready": (0, dict(pre=8, mid=12, mid2=8, n2=8, up0=1, up1=1)),
    "lo_ready": (0, dict(pre=8, mid=12, mid2=8, n2=8, up0=1, up1=1)),
    "merged": (0, dict(merge=2)),
    "s_done": (0, dict(na=16)),
    "s_read": (0, dict(na=16)),
    "pv_done": (0, dict(na=1)),
    "max_ready": (0, dict(na=16)),
    "p_exp": (0, dict(na=16)),
    "p_norm": (0, dict(na=16)),
    "pt_done": (0, dict(na=16)),
    "pt_ready": (0, dict(na=16)),
    "ada_ld0": (0, dict(na=1)),
    "ada_ld1": (0, dict(na=1)),
    "mod_ready": (1, dict(na=1)),
    "lup_ld": (0, dict(gla=1)),
    "bias_ld": (0, dict(na=1)),
    "o_st": (1, dict(hgrn=1, gla=2, na=1)),
    "gate_st0": (1, dict(hgrn=1, hgrn_last=3, gla=1, na=1)),
    "gate_st1": (1, dict(hgrn=1, hgrn_last=2, gla=1)),
    "gate_st2": (1, dict(hgrn=1, hgrn_last=2)),
    "in_ld0": (0, dict(merge=3, out=1, dn0=1, dn1=1)),
    "in_ld1": (0, dict(merge=3, out=1, dn0=1, dn1=1)),
    "y_st0": (0, dict(out=1, dn0=1)),
    "y_st1": (0, dict(out=1, dn0=1)),
    "out_st": (0, dict(fin=8)),
}
for _, per in PLAN.values():
    if "hgrn" in per:
        per.setdefault("hgrn_last", per["hgrn"])
TALLY = {}


def trunk(nc, cvec, prm, masks, cmat, cmask, xt, w_ada, w_lr, w_in, w_proj, w_out, w_up, w_dn, lup, rpb, out):
    base = {}
    for name, (first, per) in PLAN.items():
        n, base[name] = first, {}
        for st in TRIPS:
            base[name][st] = n
            n += TRIPS[st] * per.get(st, 0)

    ctx = ExitStack()
    with ctx:
        sems = {k: ctx.enter_context(nc.semaphore(k)) for k in PLAN if k != "tile"}
        sem = lambda name: ctx.enter_context(nc.semaphore(name))
        w_raw = [sem("w_raw0"), sem("w_raw1")]
        w_hi = sem("w_hi")
        w_ready = sem("w_ready")
        tile_done = sem("tile_done")
        tile_free = [sem("tile_free0"), sem("tile_free1")]
        const_ld = sem("const_ld")
        x_ld = sem("x_ld")
        ada_pre = [sem(f"ada_pre{k}") for k in range(4)]
        o_ld = [sem(f"o_ld{b}") for b in range(3)]
        rpb_st = sem("rpb_st")
        lr_st = sem("lr_st")
        acc_zero = sem("acc_zero")
        pool_step, dve_step = sem("pool_step"), sem("dve_step")
        lr_ld = sem("lr_ld")
        cmask_ld = sem("cmask_ld")

        class Pass:

            def __init__(self, e, stage, i=0):
                self.e, self.st, self.i, self.n = e, stage, i, {}

            def at(self, name, n):
                return base[name][self.st] + PLAN[name][1].get(self.st, 0) * self.i + n

            def up(self, name):
                self.n[name] = self.n.get(name, 0) + 1
                return sems[name]

            def wait(self, name, n):
                v = self.at(name, n)
                if isinstance(v, int) and v <= 0:
                    return
                self.e.wait_ge(sems[name], v)

            def wait_dma(self, name, n):
                v = self.at(name, n) * 16
                if isinstance(v, int) and v <= 0:
                    return
                self.e.wait_ge(sems[name], v)

            def tile(self, j):
                return self.at("tile", j)

            def tile_half(self, j):
                b, k = base["tile"][self.st], TILES[self.st]
                return b // 2 + (k // 2) * self.i + j // 2

            def wait_evac(self, j):
                self.e.wait_ge(tile_free[j % 2], self.tile_half(j) + 1)

            def wait_tile(self, j):
                self.e.wait_ge(tile_done, self.tile(j) + 1)

            def free_tile(self, ins, j):
                ins.then_inc(tile_free[j % 2], 1)
                self.wait_evac(j)

            def own(self, ins, name):
                ins.then_inc(self.up(name), 1)
                self.e.wait_ge(sems[name], self.at(name, self.n[name]))

            def free(self, ins, name, use):
                ins.then_inc(sems[name], 1)
                self.e.wait_ge(sems[name], self.at(name, use + 1))

            def end(self):
                for k, v in self.n.items():
                    TALLY[(k, self.st)] = v

        start = -(-nc.sbuf_base // 32) * 32
        fence = ctx.enter_context(nc.sbuf_tensor("fence", [P, (nc.sbuf_usable_end - start) // 4 - 16], F32))
        del fence
        place = [start]

        def at(name, offset, shape, dt=F32):
            return nc.alloc_sbuf_tensor_at(name, shape, dt, offset=offset)

        def sb(name, shape, dt=F32):
            n = 1 if dt == U8 else 4
            for k in shape[1:]:
                n *= k
            place[0] += -(-n // 32) * 32
            return at(name, place[0] - -(-n // 32) * 32, shape, dt)

        WR = sb("WR", [P, 2, 2, KF, P], F32R)
        RAW = sb("RAW", [P, 2, KF, P])
        hs_at = place[0]
        HS = sb("HS", [P, 16, T], F32R)
        H2 = at("H2", hs_at, [P, 16, T])
        z_at = place[0]
        ZT = sb("ZT", [P, 26, T])
        BIG = at("BIG", z_at, [P, 24, T], F32R)
        px_at = z_at + 22 * T * 4
        PX = at("PX", px_at, [P, 2, NC, P + 1])
        CB = at("CB", px_at + 2 * NC * (P + 1) * 4, [P, T])
        LR = at("LR", px_at + (2 * NC * (P + 1) + T) * 4, [32, T])
        sb("rest_of_LR", [P, 16])
        PRM = sb("PRM", [P, NPRM])
        MOD = sb("MOD", [P, 48])
        SCL = sb("SCL", [P, 2, KD])
        MT = sb("MT", [P, 8])
        LB = sb("LB", [P, 2, 8])
        EP = sb("EP", [P, 2])
        MASK = sb("MASK", [P, len(LEVELS), P], U8)
        CM = sb("CM", [P, 2, P])
        LUP = sb("LUP", [32, 2, P])
        AN = sb("AN", [P, 2, NC])
        SM = sb("SM", [P, 16])
        MASKF = at("MASKF", hs_at + 10 * T * 4, [P, len(LEVELS), P])
        ONES, IDENT = CM[:, 0, :], CM[:, 1, :]
        zt = lambda k: ZT[:, k, :]

        PD = [ctx.enter_context(nc.psum_tensor(f"PD{j}", [P, T], F32)) for j in range(2)]
        PG = ctx.enter_context(nc.psum_tensor("PG", [P, T], F32))
        PM = ctx.enter_context(nc.psum_tensor("PM", [P, T], F32))

        gates_dr = nc.dram_tensor("gates_scratch", [24, P, T], F32).ap()
        o_dr = nc.dram_tensor("o_scratch", [12, P, T], F32).ap()
        y_dr = nc.dram_tensor("y_scratch", [8, P, T], F32).ap()
        lr_dr = nc.dram_tensor("lr_scratch", [32, T], F32).ap()
        bias_dr = nc.dram_tensor("bias_scratch", [8, P, 14 * 64], F32).ap()

        Q, K0, K1, F0, F1, V, G = range(7)
        XB = [7, 8, 9, 10]
        A0, VT0, KT0, KT1, QD0, QD1, S0, S1, GB = 11, 12, 13, 14, 15, 16, 17, 18, 19
        LNX = KT1
        QRAW = KT0
        gV = [K1, V]
        gG = [G, 19]
        gA = [A0, 20]
        gVT = [VT0, 21]

        def blocks(ap, s):
            return ap.rearrange("p (b t) -> p b t", t=2 * s)

        def px_view(d, s):
            lo = 1 - d
            nb = P // (2 * s)
            v = PX[:, d, :, lo:lo + P].rearrange("p c (b t) -> p c b t", t=2 * s)
            r = PX[:, d, :, s:s + 2 * s * (nb - 1) + 1:2 * s] if nb > 1 else PX[:, d, :, s:s + 1]
            r = r.rearrange("p c (b o) -> p c b o", o=1).to_broadcast([P, NC, nb, 2 * s])
            return v, r

        def px_last(d):
            return PX[:, d, :, P:P + 1].to_broadcast([P, NC, P])

        NQT, NK, NV, NVT, NGB, NW = 0, 1, 2, 3, 11, 14
        NS = at("NS", z_at + 4 * T * 4, [P, 3, 5 * P])
        NPT = at("NPT", z_at + 6 * T * 4, [P, 2, 5 * P])
        NTR = at("NTR", z_at + 7424 * 4, [P, 2, 14 * 64])
        NTI = at("NTI", z_at + 9216 * 4, [P, 2, 5 * P])
        NCM = at("NCM", z_at + 10496 * 4, [P, 64 + 5 * P])

        def na_step(k):
            t = k % 8
            us = range(0, 4) if t < 2 else range(4, 8) if t > 5 else range(t - 2, t + 3)
            return k // 8, t, list(us)

        chunked = lambda ap: ap.rearrange("p (c t) -> p c t", t=P)

        block = ctx.enter_context(nc.Block())

        @block.sync
        def _(sp):
            sp.dma_start(PRM[:, :], prm).then_inc(const_ld, 16)
            sp.dma_start(CM[:, :, :], cmat).then_inc(const_ld, 16)
            sp.dma_start(MASKF[:, :, :], masks).then_inc(const_ld, 16)
            sp.dma_start(CB[:, :], cvec.to_broadcast([P, T])).then_inc(const_ld, 16)
            for k in range(4):
                sp.dma_start(ZT[:, 4 * k:4 * k + 4, :], w_ada[:, 4 * k:4 * k + 4, :]).then_inc(ada_pre[k], 16)
                if k == 0:
                    sp.dma_start(ZT[:, 16:24, :], xt).then_inc(x_ld, 16)
                    sp.dma_start(RAW[:, 1, 0:KD, :], w_lr).then_inc(w_raw[1], 16)

            def load(c, j, src):
                sp.wait_ge(w_ready, c.tile(j) - 1)
                sp.dma_start(RAW[:, j % 2, 0:src.shape[2], :], src.rearrange("n p k m -> p (n k) m")
                             ).then_inc(w_raw[j % 2], 16)

            for st in ("hgrn_in", "hgrn", "hgrn_last", "gla", "na"):
                per, first = TILES[st], base["tile"][st] - TILES["pre"]
                with sp.Fori(0, TRIPS[st]) as i:
                    c = Pass(sp, st, i)
                    for j in range(per):
                        load(c, j, w_in[bass.ds(i * per + (first + j), 1)])
                        if st == "na" and j == 3:
                            c.wait("mod_ready", 0)
                            c.wait_evac(0)
                            for a in range(2):
                                sp.dma_start(ZT[:, NW + 4 * a:NW + 4 * a + 4, :],
                                             w_ada[:, bass.ds(i * 8 + (NADA + 4 * a), 4), :]).then_inc(sems[f"ada_ld{a}"], 16)
            for st, src, per in (("merge", w_proj, 6), ("out", w_out, 2), ("up0", w_up[0], 2), ("dn0", w_dn[0], 2),
                                 ("up1", w_up[1], 2), ("dn1", w_dn[1], 2)):
                with sp.Fori(0, TRIPS[st]) as i:
                    c = Pass(sp, st, i)
                    for j in range(per):
                        load(c, j, src[bass.ds(i * per + j, 1)])

        @block.gpsimd
        def _(pool):
            pool.sem_inc(w_raw[0], 16)
            for h in range(8):
                for r in range(2):
                    src = bass.AP(rpb.tensor, h * 15 * P + (1 - r) * P + 63, [[P, 14], [-1, 64], [1, 64]])
                    dst = bass.AP(bias_dr.tensor, (h * P + 64 * r) * 896, [[64, 14], [896, 64], [1, 64]])
                    pool.dma_start(dst, src).then_inc(rpb_st, 16)

            def split(slot, kt, n, half, inc):
                pool.wait_ge(w_raw[slot], 16 * (half + 1))
                if not (isinstance(n, int) and n - 1 <= 0):
                    pool.wait_ge(tile_done, n - 1)
                pool.sem_inc(pool_step, 1)
                raw, hi, lo = RAW[:, slot, 0:kt, :], WR[:, slot, 0, 0:kt, :], WR[:, slot, 1, 0:kt, :]
                pool.tensor_copy(hi, raw).then_inc(w_hi, inc)
                pool.wait_ge(w_hi, n + 1)
                pool.tensor_tensor(lo, raw, hi.bitcast(F32), ALU.subtract).then_inc(w_ready, inc)

            split(1, KD, 1, 0, 2)
            for st, kt in (("hgrn_in", 8), ("hgrn", 8), ("hgrn_last", 8), ("gla", 8), ("na", 8), ("merge", 4), ("out", 8), ("up0", 8), ("dn0", KF),
                           ("up1", 8), ("dn1", KF)):
                with pool.Fori(0, TRIPS[st] * TILES[st] // 2) as i:
                    b = base["tile"][st]
                    for j in range(2):
                        split(j, kt, i * 2 + (b + j), i + b // 2, 1)

        @block.tensor
        def _(pe):
            def dense(c, j, kt, mov, lo_at, each=None):
                pe.wait_ge(w_ready, c.tile(j) + 1)
                pe.wait_ge(tile_free[j % 2], c.tile_half(j))
                s = j % 2
                for k in range(kt):
                    if each is not None:
                        Pass(pe, each[0]).wait("lo_ready", each[1] + k + 1)
                    for n, (w, x) in enumerate(((0, 0), (0, lo_at), (1, 0))):
                        for h in range(2):
                            last = pe.matmul(PD[s][:, h * HALF:(h + 1) * HALF], WR[:, s, w, k, :],
                                             mov[:, k + x, h * HALF:(h + 1) * HALF],
                                             start=(k == 0 and n == 0), stop=(k == kt - 1 and n == 2))
                last.then_inc(tile_done, 1)

            def sum_squares(c, src):
                for ct in range(KD):
                    c.wait("sq_ready", ct + 1)
                    for h in range(2):
                        last = pe.matmul(PG[:, h * HALF:(h + 1) * HALF], ONES, src(ct)[:, h * HALF:(h + 1) * HALF],
                                         start=(ct == 0), stop=(ct == KD - 1))
                    last.then_inc(c.up("sq_used"), 1)

            def total(c, acc):
                for h in range(2):
                    last = pe.matmul(PG[:, h * HALF:(h + 1) * HALF], ONES, acc[:, h * HALF:(h + 1) * HALF],
                                     start=True, stop=True)
                last.then_inc(c.up("sum_done"), 1)

            c = Pass(pe, "pre")
            pe.wait_ge(const_ld, 64)
            sum_squares(c, lambda ct: H2[:, 8 + ct % 2, :])
            pe.wait_ge(w_ready, 2)
            for k in range(KD):
                c.wait("lo_ready", k + 1)
                for n, (w, x) in enumerate(((0, 0), (0, KD), (1, 0))):
                    for h in range(2):
                        last = pe.matmul(PD[1][:, h * HALF:(h + 1) * HALF], WR[:, 1, w, k, :],
                                         HS[:, k + x, h * HALF:(h + 1) * HALF],
                                         start=(k == 0 and n == 0), stop=(k == KD - 1 and n == 2))
            last.then_inc(tile_done, 2)
            c.end()

            def turn(c, src, use):
                c.wait("misc_free", use)
                for n in range(NC):
                    last = pe.transpose(PM[:, n * P:(n + 1) * P], src[:, n * P:(n + 1) * P], IDENT)
                last.then_inc(c.up("misc_done"), 1)

            def gram(c, use, lhs, rhs, rows):
                for h in range(2):
                    c.wait(f"gram_free{h}", use)
                    for n in range(4 * h, 4 * h + 4):
                        last = pe.matmul(PG[:, n * P:(n + 1) * P], lhs[rows, n * P:(n + 1) * P],
                                         rhs[rows, n * P:(n + 1) * P], start=True, stop=True)
                    last.then_inc(c.up("gram_done"), 1)

            def level(c, use, l, rows):
                s = LEVELS[l]
                xf, xb = zt(XB[2 * l % 4])[rows, :], zt(XB[2 * l % 4 + 1])[rows, :]
                for h in range(2):
                    c.wait(f"gram_free{h}", use)
                    for n in range(4 * h, 4 * h + 4):
                        cols = slice(n * P, (n + 1) * P)
                        to = blocks(PG[:, cols], s)
                        pe.matmul(to[:, :, s:], xf[:, cols], blocks(xf[:, cols], s)[:, :, s:], start=True, stop=True)
                        last = pe.matmul(to[:, :, 0:s], xb[:, cols], blocks(xb[:, cols], s)[:, :, 0:s],
                                         start=True, stop=True)
                    last.then_inc(c.up("gram_done"), 1)

            def states(c, use, d, heads):
                c.wait("misc_free", use)
                KT = zt(KT0 + d)
                for n in (range(0, 7) if d == 0 else range(1, 8)):
                    for m, (rows, vt) in enumerate(heads):
                        last = pe.matmul(PM[rows, n * P:(n + 1) * P], KT[:, n * P + rows.start:n * P + rows.stop],
                                         zt(vt)[:, n * P:(n + 1) * P], start=True, stop=True)
                last.then_inc(c.up("misc_done"), 1)

            def outputs(c, use, rows, vt, a):
                c.wait("misc_free", use)
                for n in range(NC):
                    cols = slice(n * P, (n + 1) * P)
                    terms = [(zt(vt)[:, cols], zt(a)[:, cols])]
                    if n > 0:
                        terms.append((zt(S0)[rows, cols], zt(QD0)[rows, cols]))
                    if n < NC - 1:
                        terms.append((zt(S1)[rows, cols], zt(QD1)[rows, cols]))
                    for m, (l, r) in enumerate(terms):
                        last = pe.matmul(PM[:, cols], l, r, start=(m == 0), stop=(m == len(terms) - 1))
                last.then_inc(c.up("misc_done"), 1)

            def head_sums(c, use, nth, sq):
                c.wait("osq_ready", nth + 1)
                for h in range(2):
                    c.wait(f"gram_free{h}", use)
                    pe.matmul(PG[:, h * HALF:(h + 1) * HALF], ONES, zt(sq)[:, h * HALF:(h + 1) * HALF],
                              start=True, stop=True).then_inc(c.up("gram_done"), 1)

            ALL = slice(0, P)
            c = Pass(pe, "hgrn_in")
            for j in range(4):
                dense(c, j, KD, HS, KD)
            c.end()

            def hgrn_head(c):
                c.wait_evac(-1)
                turn(c, zt(V), 0)
                dense(c, 0, KD, HS, KD)
                dense(c, 1, KD, HS, KD)
                for d in range(2):
                    c.wait("kdec_ready", d + 1)
                    turn(c, zt(F0 + d), 1 + d)
                c.wait("misc_free", 3)
                states(c, 3, 0, [(ALL, VT0)])
                c.wait("ksum_ready", 1)
                gram(c, 0, zt(V), zt(Q), ALL)
                states(c, 4, 1, [(ALL, VT0)])
                for l in range(len(LEVELS)):
                    c.wait("x_ready", 2 * l + 2)
                    level(c, 1 + l, l, ALL)
                    if l < 6:
                        dense(c, 2 + l, KD, HS, KD)
                c.wait("attn_ready", 1)
                outputs(c, 5, ALL, VT0, A0)
                head_sums(c, 8, 0, A0)
                c.end()

            with pe.Fori(0, TRIPS["hgrn"]) as i:
                hgrn_head(Pass(pe, "hgrn", i))
            hgrn_head(Pass(pe, "hgrn_last"))

            ROWS = [slice(0, 64), slice(64, 128)]
            with pe.Fori(0, TRIPS["gla"]) as i:
                c = Pass(pe, "gla", i)
                c.wait_dma("lup_ld", 1)
                pe.wait_ge(lr_ld, 16)
                for d in range(2):
                    c.wait("misc_free", d)
                    for h in range(2):
                        last = pe.matmul(PM[:, h * HALF:(h + 1) * HALF], LUP[:, d, :], LR[:, h * HALF:(h + 1) * HALF],
                                         start=True, stop=True)
                    last.then_inc(c.up("misc_done"), 1)
                for j in range(4):
                    dense(c, j, KD, HS, KD)
                for hh in range(2):
                    c.wait_evac(2 + hh)
                    turn(c, zt(gV[hh]), 2 + hh)
                dense(c, 4, KD, HS, KD)
                for d in range(2):
                    c.wait("kdec_ready", d + 1)
                    turn(c, zt(F0 + d), 4 + d)
                c.wait("misc_free", 6)
                for d in range(2):
                    states(c, 6 + d, d, list(zip(ROWS, gVT)))
                    gram(c, d, zt(K0), zt(Q), ROWS[d])
                for l in range(len(LEVELS)):
                    c.wait("x_ready", 2 * l + 2)
                    for hh in range(2):
                        level(c, 2 + 2 * l + hh, l, ROWS[hh])
                    if l in (1, 3, 5):
                        dense(c, 5 + l // 2, KD, HS, KD)
                for hh in range(2):
                    c.wait("attn_ready", hh + 1)
                    outputs(c, 8 + hh, ROWS[hh], gVT[hh], gA[hh])
                    head_sums(c, 16 + hh, hh, XB[2 + hh])
                c.end()

            with pe.Fori(0, TRIPS["na"]) as i:
                c = Pass(pe, "na", i)
                for j in range(3):
                    dense(c, j, KD, HS, KD)
                c.wait_evac(2)
                turn(c, zt(NV), 0)
                dense(c, 3, KD, HS, KD)
                c.wait("misc_free", 1)
                c.wait_evac(2)
                c.wait_evac(3)
                c.wait("gram_free0", 0)
                c.wait("gram_free1", 0)
                for k in range(19):
                    if k < 16:
                        if k >= 2:
                            c.wait("s_read", k - 1)
                        head, t, us = na_step(k)
                        rows, n = ROWS[head], len(us) * P
                        for lo in range(0, n, HALF):
                            hi = min(n, lo + HALF)
                            last = pe.matmul(PD[k % 2][:, lo:hi], zt(NQT)[rows, t * P:(t + 1) * P],
                                             zt(NK)[rows, us[0] * P + lo:us[0] * P + hi], start=True, stop=True)
                        last.then_inc(c.up("s_done"), 1)
                    if 2 <= k <= 17:
                        c.wait("p_norm", k - 1)
                        if k >= 3:
                            c.wait("pt_ready", k - 2)
                        for m in range(len(na_step(k - 2)[2])):
                            last = pe.transpose(PM[:, m * P:(m + 1) * P], NS[:, (k - 2) % 3, m * P:(m + 1) * P], IDENT)
                        last.then_inc(c.up("pt_done"), 1)
                    if k >= 3:
                        c.wait("pt_ready", k - 2)
                        head, t, us = na_step(k - 3)
                        rows = ROWS[head]
                        for m, u in enumerate(us):
                            last = pe.matmul(PG[rows, t * P:(t + 1) * P], zt(NVT)[:, u * P + rows.start:u * P + rows.stop],
                                             NPT[:, (k - 3) % 2, m * P:(m + 1) * P],
                                             start=(m == 0), stop=(m == len(us) - 1))
                last.then_inc(c.up("pv_done"), 1)
                c.end()

            with pe.Fori(0, TRIPS["merge"]) as i:
                c = Pass(pe, "merge", i)
                for j in range(6):
                    dense(c, j, 4, BIG[:, 8 * (j % 3):8 * (j % 3) + 8, :], 4, ("mid", 4 * (j % 3)))
            with pe.Fori(0, TRIPS["out"]) as i:
                c = Pass(pe, "out", i)
                dense(c, 0, KD, BIG, KD, ("mid2", 0))
                dense(c, 1, KD, BIG, KD)
            c = Pass(pe, "n2")
            c.wait("acc_ready", 0)
            total(c, H2[:, 2, :])
            c.end()
            for g in range(2):
                with pe.Fori(0, TRIPS[f"up{g}"]) as i:
                    c = Pass(pe, f"up{g}", i)
                    dense(c, 0, KD, HS, KD, ("n2", 0))
                    dense(c, 1, KD, HS, KD)
                with pe.Fori(0, TRIPS[f"dn{g}"]) as i:
                    c = Pass(pe, f"dn{g}", i)
                    dense(c, 0, KF, BIG, KF, (f"up{g}", 0))
                    dense(c, 1, KF, BIG, KF)
            c = Pass(pe, "fin")
            c.wait("acc_ready", 0)
            total(c, H2[:, 11, :])
            c.end()

        @block.scalar
        def _(act):
            act.sem_inc(sems["gram_free0"], 1)
            act.sem_inc(sems["gram_free1"], 1)
            act.sem_inc(sems["misc_free"], 1)
            act.sem_inc(sems["mod_ready"], 1)
            for m in range(3):
                act.sem_inc(sems[f"gate_st{m}"], 16)
            act.sem_inc(sems["o_st"], 16)
            act.sem_inc(tile_free[0], 1)
            A = act.activation

            def squares(c, src, dst, first_free=True):
                for ct in range(KD):
                    if ct >= 2:
                        c.wait("sq_used", ct - 1)
                    c.own(A(dst(ct), src(ct), ACT.Square), "sq_ready")

            def rstd(c, dst, ps, width, name):
                c.own(A(dst, ps, ACT.Ln, bias=EP[:, 0:1], scale=1.0 / width), "act_own")
                c.own(A(dst, dst, ACT.Exp, scale=-0.5), name)

            c = Pass(act, "pre")
            act.wait_ge(const_ld, 64)
            c.own(A(H2[:, 12, :], CB[:, :], ACT.Sigmoid), "act_own")
            c.wait("param_ready", 1)
            c.own(A(LB[:, 0, :], LB[:, 0, :], ACT.Exp), "act_own")
            act.wait_ge(x_ld, 16)
            squares(c, lambda ct: zt(16 + ct), lambda ct: H2[:, 8 + ct % 2, :])
            c.wait("sq_used", 8)
            rstd(c, H2[:, 15, :], PG[:, :], 1024.0, "rstd_ready")
            for ct in range(KD):
                c.wait("norm_ready", ct + 1)
                c.own(A(HS[:, ct, :], zt(16 + ct), ACT.Identity, bias=MOD[:, ct:ct + 1], scale=SCL[:, 0, ct:ct + 1]), "hi_ready")
            act.wait_ge(tile_done, 2)
            c.own(A(zt(0)[0:32, :], PD[1][0:32, :], ACT.Copy), "act_own")
            act.sem_inc(tile_free[1], 1)
            act.dma_start(lr_dr, zt(0)[0:32, :]).then_inc(lr_st, 16)
            act.wait_ge(lr_st, 16)
            c.end()

            EARLY = dict(hgrn=-2, hgrn_last=-2, gla=0)

            def evac_turned(c, dst, use, nth):
                c.wait("misc_done", nth)
                c.free(A(dst, PM[:, :], ACT.Copy), "misc_free", use)

            def decays(c, d):
                c.wait("diff_ready", EARLY[c.st] + d + 1)
                x, lo = zt(XB[d]), 1 - d
                dst = zt(QD0) if d == 0 else zt(F1)
                c.own(A(chunked(dst), PX[:, d, :, lo:lo + P], ACT.Exp), "act_own")
                c.own(A(AN[:, d, :], PX[:, d, :, P], ACT.Exp), "act_own")
                c.own(A(x, x, ACT.Exp, scale=-1.0), "exp_ready")

            def level_exp(c, q):
                s = LEVELS[q // 2]
                c.wait("diff_ready", EARLY[c.st] + 2 + q + 1)
                x = blocks(zt(XB[q % 4]), s)
                c.own(A(x[:, :, 0:s], x[:, :, 0:s], ACT.Exp, scale=-1.0), "act_own")
                c.own(A(x[:, :, s:], x[:, :, s:], ACT.Exp), "exp_ready")

            def store_gate(c, j, m, row, gb):
                c.wait_tile(j)
                c.wait_dma(f"gate_st{m}", c.n.get(f"gate_st{m}", 0))
                c.free_tile(A(zt(gb), PD[j % 2][:, :], ACT.Sigmoid), j)
                act.dma_start(gates_dr[bass.ds(row, 1)].rearrange("n p t -> (n p) t"), zt(gb)
                              ).then_inc(c.up(f"gate_st{m}"), 16)

            def head_out(c, use, nth, ob, sq, rb, gu):
                c.wait("misc_done", use + 1)
                c.free(A(zt(ob), PM[:, :], ACT.Copy), "misc_free", use)
                c.own(A(zt(sq), zt(ob), ACT.Square), "osq_ready")
                c.wait("gram_done", 2 * gu + 2)
                c.own(A(zt(rb), PG[:, :], ACT.Ln, bias=EP[:, 0:1], scale=1.0 / P), "act_own")
                act.sem_inc(sems["gram_free0"], 1)
                act.sem_inc(sems["gram_free1"], 1)
                c.own(A(zt(rb), zt(rb), ACT.Exp, scale=-0.5), "orstd_ready")

            def store_o(c, nth, row, ob):
                c.wait("o_ready", nth + 1)
                act.dma_start(o_dr[bass.ds(row, 1)].rearrange("n p t -> (n p) t"), zt(ob)).then_inc(c.up("o_st"), 16)

            def raw_tile(c, j, dst):
                c.wait_tile(j)
                c.free_tile(A(zt(dst), PD[j % 2][:, :], ACT.Copy), j)

            def hgrn_head(c, i, fill):
                c.own(A(zt(Q), zt(QRAW), ACT.Sigmoid), "sig_ready")
                evac_turned(c, zt(VT0), 0, 1)
                for d in range(2):
                    decays(c, d)
                c.wait_tile(0)
                c.own(A(zt(G), PD[0][:, :], ACT.Sigmoid), "sig_ready")
                store_gate(c, 1, 0, i * 3, GB)
                c.wait_dma("o_st", 0)
                for d in range(2):
                    evac_turned(c, zt(KT0 + d), 1 + d, 2 + d)
                for h in range(2):
                    c.wait("gram_done", h + 1)
                    c.free(A(zt(A0)[:, h * HALF:(h + 1) * HALF], PG[:, h * HALF:(h + 1) * HALF], ACT.Copy), f"gram_free{h}", 0)
                for q in range(NQ):
                    level_exp(c, q)
                    if q >= 5 and q % 2:
                        fill(c, q // 2)
                fill(c, 7)
                head_out(c, 5, 0, KT1, A0, S0, 8)
                store_o(c, 0, i, KT1)
                c.end()

            def decay_tile(c, j, d):
                c.wait_tile(j)
                c.own(A(zt(GB + d), PD[j % 2][:, :], ACT.Sigmoid, scale=-1.0), "act_own")
                c.free_tile(A(zt(F0 + d), PD[j % 2][:, :], ACT.Sigmoid), j)
                act.sem_inc(c.up("f_ready"), 1)

            def decay_ln(c, d):
                c.wait("ln_in", d + 1)
                c.own(A(zt(F0 + d), zt(F0 + d), ACT.Ln), "act_own")
                c.own(A(zt(LNX), zt(LNX), ACT.Ln), "ln_out")

            def fill_head(c, j):
                if j < 4:
                    store_gate(c, j, j - 1, c.i * 3 + (j - 1), GB + j - 1)
                elif j < 6:
                    if j == 5:
                        decay_ln(c, 0)
                    c.wait_dma(f"gate_st{j - 4}", 1)
                    decay_tile(c, j, j - 4)
                else:
                    if j == 6:
                        decay_ln(c, 1)
                    raw_tile(c, j, (QRAW, V)[j - 6])

            c = Pass(act, "hgrn_in")
            for d in range(2):
                decay_tile(c, d, d)
                decay_ln(c, d)
            raw_tile(c, 2, QRAW)
            raw_tile(c, 3, V)
            c.end()
            with act.Fori(0, TRIPS["hgrn"]) as i:
                hgrn_head(Pass(act, "hgrn", i), i, fill_head)
            hgrn_head(Pass(act, "hgrn_last"), 3, lambda c, j: store_gate(c, j, (j - 1) % 3, 9 + (j - 1), GB + (j - 1) % 3))

            act.dma_start(LR[:, :], lr_dr).then_inc(lr_ld, 16)
            for m in range(3):
                Pass(act, "gla").wait_dma(f"gate_st{m}", 0)
            Pass(act, "gla").wait_dma("o_st", 0)
            with act.Fori(0, TRIPS["gla"]) as i:
                c = Pass(act, "gla", i)
                act.dma_start(LUP[:, :, :], lup[bass.ds(i, 1)].rearrange("n r d m -> (n r) d m")
                              ).then_inc(c.up("lup_ld"), 16)
                for d in range(2):
                    c.wait("misc_done", d + 1)
                    c.free(A(zt(F0 + d), PM[:, :], ACT.Identity, bias=PRM[:, bass.ds(i + (PC_ZB + 2 * d), 1)]), "misc_free", d)
                c.wait_tile(0)
                c.free_tile(A(zt(Q), PD[0][:, :], ACT.Copy, scale=0.125), 0)
                c.wait_tile(1)
                c.free_tile(A(zt(K0), PD[1][:, :], ACT.Copy), 1)
                for d in range(2):
                    c.wait("ln_in", d + 1)
                    x = zt(XB[d])
                    c.own(A(x, x, ACT.Exp, scale=-1.0), "act_own")
                    c.own(A(x, x, ACT.Ln, bias=EP[:, 1:2]), "ln_out")
                for hh in range(2):
                    c.wait_dma(f"gate_st{hh}", 0)
                    c.wait_tile(2 + hh)
                    c.free_tile(A(zt(gV[hh]), PD[hh][:, :], ACT.Copy), 2 + hh)
                for hh in range(2):
                    evac_turned(c, zt(gVT[hh]), 2 + hh, 3 + hh)
                for d in range(2):
                    decays(c, d)
                c.wait_tile(4)
                c.own(A(zt(gG[0]), PD[0][:, :], ACT.Sigmoid), "sig_ready")
                for d in range(2):
                    evac_turned(c, zt(KT0 + d), 4 + d, 5 + d)
                for hh in range(2):
                    for h in range(2):
                        c.wait("gram_done", 2 * hh + h + 1)
                        c.free(A(zt(gA[hh])[:, h * HALF:(h + 1) * HALF], PG[:, h * HALF:(h + 1) * HALF], ACT.Copy, scale=2.0),
                               f"gram_free{h}", hh)
                for q in range(NQ):
                    level_exp(c, q)
                    if q == 6:
                        c.wait_tile(5)
                        c.own(A(zt(gG[1]), PD[1][:, :], ACT.Sigmoid), "sig_ready")
                    if q == 10:
                        store_gate(c, 6, 0, i * 2 + 16, gV[0])
                store_gate(c, 7, 1, i * 2 + 17, gV[1])
                for hh in range(2):
                    head_out(c, 8 + hh, hh, F0 + hh, XB[2 + hh], XB[hh], 16 + hh)
                    store_o(c, hh, i * 2 + (4 + hh), F0 + hh)
                c.wait_dma("o_st", 2)
                c.end()

            for m in range(2):
                Pass(act, "na").wait_dma(f"gate_st{m}", 0)
            act.wait_ge(rpb_st, 16 * 16)
            act.dma_start(NCM[:, :], cmask).then_inc(cmask_ld, 16)
            with act.Fori(0, TRIPS["na"]) as i:
                c = Pass(act, "na", i)
                act.dma_start(NTR[:, :, :], bias_dr[bass.ds(i * 2, 2)].rearrange("e p x -> p e x")).then_inc(c.up("bias_ld"), 16)
                c.wait_tile(0)
                c.free_tile(A(zt(NQT), PD[0][:, :], ACT.Copy, scale=0.125), 0)
                c.wait_tile(1)
                c.free_tile(A(zt(NK), PD[1][:, :], ACT.Copy), 1)
                c.wait_tile(2)
                c.free_tile(A(zt(NV), PD[0][:, :], ACT.Copy), 2)
                evac_turned(c, zt(NVT), 0, 1)
                store_gate(c, 3, 0, i + 20, NGB)
                for k in range(18):
                    if k < 16:
                        n = len(na_step(k)[2]) * P
                        c.wait("max_ready", k + 1)
                        p = NS[:, k % 3, 0:n]
                        c.own(A(p, p, ACT.Exp, bias=SM[:, 4 + k % 2:5 + k % 2], accum_out=SM[:, 8 + k % 2:9 + k % 2]), "p_exp")
                    if k >= 2:
                        n = len(na_step(k - 2)[2]) * P
                        c.wait("pt_done", k - 1)
                        c.own(A(NPT[:, (k - 2) % 2, 0:n], PM[:, 0:n], ACT.Copy), "pt_ready")
                c.wait("pv_done", 1)
                c.free(A(zt(NV), PG[:, :], ACT.Copy), "gram_free0", 0)
                act.dma_start(o_dr[bass.ds(i + 8, 1)].rearrange("n p t -> (n p) t"), zt(NV)).then_inc(c.up("o_st"), 16)
                c.wait_dma("o_st", 1)
                c.end()
            for m in range(3):
                Pass(act, "mid").wait_dma(f"gate_st{m}", 0)

            c = Pass(act, "mid")
            for b in range(3):
                act.dma_start(H2[:, 4 * b:4 * b + 4, :], o_dr[4 * b:4 * b + 4].rearrange("n p t -> p n t")).then_inc(o_ld[b], 16)
            for n in range(12):
                if n % 4 == 0:
                    act.wait_ge(o_ld[n // 4], 16)
                c.own(A(BIG[:, 8 * (n // 4) + n % 4, :], H2[:, n, :], ACT.Copy), "hi_ready")
            c.end()
            with act.Fori(0, TRIPS["merge"]) as i:
                c = Pass(act, "merge", i)
                for j in range(6):
                    act.wait_ge(tile_free[j % 2], c.tile_half(j))
                    act.dma_start(zt(24 + j % 2), gates_dr[bass.ds(i * 6 + j, 1)].rearrange("n p t -> (n p) t")
                                  ).then_inc(c.up(f"in_ld{j % 2}"), 16)
                c.end()
            c = Pass(act, "mid2")
            c.wait("merged", 0)
            for ct in range(KD):
                c.own(A(BIG[:, ct, :], H2[:, 4 + ct, :], ACT.Copy), "hi_ready")
            c.end()
            with act.Fori(0, TRIPS["out"]) as i:
                c = Pass(act, "out", i)
                for j in range(2):
                    act.wait_ge(tile_free[j], c.tile_half(j))
                    act.dma_start(zt(24 + j), xt[:, bass.ds(i * 2 + j, 1), :].rearrange("p n t -> p (n t)")
                                  ).then_inc(c.up(f"in_ld{j}"), 16)
                for j in range(2):
                    x1 = ZT[:, bass.ds(i * 2 + (16 + j), 1), :].rearrange("p n t -> p (n t)")
                    c.wait_evac(j)
                    act.dma_start(y_dr[bass.ds(i * 2 + j, 1)].rearrange("n p t -> (n p) t"), x1
                                  ).then_inc(c.up(f"y_st{j}"), 16)
                    c.own(A(H2[:, j, :], x1, ACT.Square), "sq_ready")
                c.end()
            c = Pass(act, "n2")
            c.wait("sum_done", 1)
            for j in range(2):
                c.wait_dma(f"y_st{j}", 0)
            rstd(c, zt(0), PG[:, :], 1024.0, "rstd_ready")
            for ct in range(KD):
                c.wait("norm_ready", ct + 1)
                c.own(A(HS[:, ct, :], zt(16 + ct), ACT.Identity, bias=MOD[:, 24 + ct:25 + ct], scale=SCL[:, 1, ct:ct + 1]), "hi_ready")
            c.wait("lo_ready", 8)
            c.end()
            for g in range(2):
                with act.Fori(0, TRIPS["up0"]) as i:
                    c = Pass(act, f"up{g}", i)
                    c.wait_tile(0)
                    c.free_tile(A(zt(24), PD[0][:, :], ACT.Silu), 0)
                    c.wait_evac(1)
                    c.own(A(BIG[:, bass.ds(i, 1), :].rearrange("p n t -> p (n t)"), zt(25), ACT.Copy), "hi_ready")
                    c.end()
                c = Pass(act, f"up{g}", TRIPS["up0"])
                c.wait("lo_ready", 0)
                with act.Fori(0, TRIPS["dn0"]) as i:
                    c = Pass(act, f"dn{g}", i)
                    for j in range(2):
                        if g == 0:
                            c.wait_dma(f"y_st{j}", 0)
                        else:
                            act.wait_ge(tile_free[j], c.tile_half(j))
                        act.dma_start(zt(24 + j), y_dr[bass.ds(i * 2 + j, 1)].rearrange("n p t -> (n p) t")
                                      ).then_inc(c.up(f"in_ld{j}"), 16)
                    if g == 0:
                        for j in range(2):
                            c.wait_evac(j)
                            act.dma_start(y_dr[bass.ds(i * 2 + j, 1)].rearrange("n p t -> (n p) t"), zt(24 + j)
                                          ).then_inc(c.up(f"y_st{j}"), 16)
                    else:
                        for j in range(2):
                            c.wait_evac(j)
                            y = H2[:, bass.ds(i * 2 + j, 1), :].rearrange("p n t -> p (n t)")
                            c.own(A(H2[:, 8 + j, :], y, ACT.Square), "sq_ready")
                    c.end()
                if g == 0:
                    for j in range(2):
                        Pass(act, "up1").wait_dma(f"y_st{j}", 0)
            c = Pass(act, "fin")
            c.wait("sum_done", 1)
            rstd(c, H2[:, 10, :], PG[:, :], 1024.0, "rstd_ready")
            for ct in range(KD):
                c.wait("norm_ready", ct + 1)
                act.dma_start(out[ct], H2[:, ct, :]).then_inc(c.up("out_st"), 16)
            c.wait_dma("out_st", 8)
            c.end()

        @block.vector
        def _(dve):
            tt, ts, stt = dve.tensor_tensor, dve.tensor_scalar, dve.scalar_tensor_tensor

            def scaled_split(c, x, a, b, ct):
                c.wait("hi_ready", ct + 1)
                c.own(ts(x, x, a, b, ALU.mult, ALU.add), "dve_own")
                c.own(tt(HS[:, KD + ct, :], x, HS[:, ct, :].bitcast(F32), ALU.subtract), "lo_ready")

            c = Pass(dve, "pre")
            own = lambda ins: c.own(ins, "dve_own")
            own(dve.memset(EP[:, 0:1], EPS))
            own(dve.memset(EP[:, 1:2], 1.0))
            dve.wait_ge(const_ld, 64)
            own(dve.tensor_copy(MASK[:, :, :], MASKF[:, :, :]))
            lb, lg = LB[:, 0, :], PRM[:, PC_LB:PC_LB + 8]
            c.own(tt(lb, lg, lg, ALU.subtract), "param_ready")
            c.wait("act_own", 1)
            own(tt(CB[:, :], CB[:, :], H2[:, 12, :], ALU.mult))
            c.wait("act_own", 2)
            own(dve.reciprocal(LB[:, 1, :], lb))
            own(tt(lb, lb, LB[:, 1, :], ALU.mult))
            own(tt(lb, lb, lb, ALU.subtract))
            own(ts(lb, lb, 0.0, 1.0, ALU.max, ALU.min))
            own(ts(LB[:, 1, :], lb, -1.0, 1.0, ALU.mult, ALU.add))
            for t in range(NADA):
                if t % 4 == 0:
                    dve.wait_ge(ada_pre[t // 4], 16)
                own(dve.tensor_tensor_reduce(zt(t), zt(t), CB[:, :], 1.0, 0.0, ALU.mult, ALU.add, MOD[:, t:t + 1]))
            own(tt(MOD[:, 0:NADA], MOD[:, 0:NADA], PRM[:, PC_BADA:PC_BADA + NADA], ALU.add))
            own(ts(SCL[:, 0, :], MOD[:, 8:16], 1.0, None, ALU.add))
            own(tt(SCL[:, 0, :], SCL[:, 0, :], PRM[:, PC_N1:PC_N1 + KD], ALU.mult))

            def norm(c, first, rb, w, s):
                c.wait("rstd_ready", 1)
                for ct in range(KD + 1):
                    if ct < KD:
                        c.own(tt(zt(first + ct), zt(first + ct), rb, ALU.mult), "norm_ready")
                    if ct > 0:
                        scaled_split(c, zt(first + ct - 1), SCL[:, s, ct - 1:ct], MOD[:, w + ct - 1:w + ct], ct - 1)

            norm(c, 16, H2[:, 15, :], 0, 0)
            dve.wait_ge(lr_st, 16)
            own(dve.memset(PX[:, :, :, 0:1], 0.0))
            c.end()

            def cumulate(c, d):
                for n in range(NC):
                    ins = dve.tensor_tensor_scan(PX[:, d, n, 1:P + 1], ONES, zt(F0 + d)[:, n * P:(n + 1) * P], 0.0,
                                                 ALU.mult, ALU.add)
                    c.own(ins, "dve_own")
                lo = 1 - d
                c.own(tt(chunked(zt(XB[d])), PX[:, d, :, lo:lo + P], px_last(d), ALU.subtract), "diff_ready")

            def decayed(c, k0, k1):
                c.wait("exp_ready", 1)
                c.own(tt(zt(F0), zt(k0), zt(XB[0]), ALU.mult), "kdec_ready")
                c.own(tt(zt(QD0), zt(QD0), zt(Q), ALU.mult), "dve_own")
                c.wait("exp_ready", 2)
                c.own(tt(zt(F1), zt(k1), zt(F1), ALU.mult), "kdec_ready")
                c.own(tt(zt(QD1), zt(Q), zt(XB[1]), ALU.mult), "dve_own")

            def level_diff(c, q):
                s, d = LEVELS[q // 2], q % 2
                v, r = px_view(d, s)
                o = zt(XB[q % 4]).rearrange("p (c b t) -> p c b t", c=NC, t=2 * s)
                c.own(tt(o, v, r, ALU.subtract), "diff_ready")

            def level_products(c, q, k0, k1):
                s, d = LEVELS[q // 2], q % 2
                c.wait("exp_ready", 2 + q + 1)
                x = blocks(zt(XB[q % 4]), s)
                a, b = (k0, Q) if d == 0 else (Q, k1)
                c.own(tt(x[:, :, 0:s], x[:, :, 0:s], blocks(zt(a), s)[:, :, 0:s], ALU.mult), "dve_own")
                c.own(tt(x[:, :, s:], x[:, :, s:], blocks(zt(b), s)[:, :, s:], ALU.mult), "x_ready")

            def level_select(c, l, a, use):
                for h in range(2):
                    c.wait("gram_done", 2 * use + h + 1)
                    dve.sem_inc(dve_step, 1)
                    ins = dve.copy_predicated(chunked(zt(a)[:, h * HALF:(h + 1) * HALF]),
                                              MASK[:, l:l + 1, :].to_broadcast([P, 4, P]),
                                              chunked(PG[:, h * HALF:(h + 1) * HALF]))
                    c.free(ins, f"gram_free{h}", use)

            def carry(c, use, d):
                c.wait("misc_done", use + 1)
                S = chunked(zt(S0 + d))
                ps = chunked(PM[:, :])
                order = list(range(0, 7)) if d == 0 else list(range(7, 0, -1))
                for m, n in enumerate(order):
                    to = S[:, n + 1 if d == 0 else n - 1, :]
                    if m == 0:
                        ins = dve.tensor_copy(to, ps[:, n, :])
                    else:
                        ins = stt(to, S[:, n, :], AN[:, d, n:n + 1], ps[:, n, :], ALU.mult, ALU.add)
                    if m == len(order) - 1:
                        c.free(ins, "misc_free", use)
                    else:
                        c.own(ins, "dve_own")

            def finish_head(c, nth, ob, rb, g, w):
                c.wait("orstd_ready", nth + 1)
                c.own(stt(zt(ob), zt(ob), PRM[:, w:w + 1], zt(rb), ALU.mult, ALU.mult), "dve_own")
                c.own(tt(zt(ob), zt(ob), zt(g), ALU.mult), "o_ready")

            def decay_in(c, d, head):
                f, x = zt(F0 + d), zt(LNX)
                c.wait("f_ready", d + 1)
                c.own(ts(f, f, LB[:, 1, bass.ds(head + 4 * d, 1)], LB[:, 0, bass.ds(head + 4 * d, 1)], ALU.mult, ALU.add), "dve_own")
                c.own(ts(x, f, 1.0 / LN_SPLIT, F_FLOOR / LN_SPLIT, ALU.mult, ALU.max), "dve_own")
                c.own(ts(x, x, 1.0, None, ALU.min), "dve_own")
                c.own(ts(f, f, LN_SPLIT, None, ALU.max), "ln_in")

            def decay_out(c, d):
                c.wait("ln_out", d + 1)
                c.own(tt(zt(F0 + d), zt(F0 + d), zt(LNX), ALU.add), "dve_own")

            def keys(c, head):
                for d in range(2):
                    c.own(ts(zt(K0 + d), zt(GB + d), LB[:, 1, bass.ds(head + 4 * d, 1)], None, ALU.mult), "dve_own")

            def hgrn_head(c, i, last):
                c.wait("sig_ready", 1)
                c.own(tt(zt(Q), zt(Q), zt(QRAW), ALU.mult), "dve_own")
                decayed(c, K0, K1)
                level_diff(c, 0)
                level_diff(c, 1)
                c.wait("sig_ready", 2)
                c.free_tile(tt(zt(G), zt(G), PD[0][:, :], ALU.mult), 0)
                c.wait("misc_done", 1)
                c.own(tt(zt(V), zt(K0), zt(K1), ALU.add), "ksum_ready")
                carry(c, 3, 0)
                for q in range(NQ):
                    level_products(c, q, K0, K1)
                    if q == 0:
                        carry(c, 4, 1)
                        c.wait("gram_free0", 1)
                        c.wait("gram_free1", 1)
                    if q + 2 < NQ:
                        if q >= 2:
                            c.wait("gram_done", 2 * (q // 2 + 1))
                        level_diff(c, q + 2)
                    if q % 2 and q > 1:
                        level_select(c, q // 2 - 1, A0, q // 2)
                    if not last:
                        if q == 9:
                            decay_in(c, 0, i + 1)
                        if q == 11:
                            decay_out(c, 0)
                            decay_in(c, 1, i + 1)
                        if q == 13:
                            decay_out(c, 1)
                            keys(c, i + 1)
                level_select(c, NQ // 2 - 1, A0, NQ // 2)
                c.own(dve.memset(SM[:, 15:16], 0.0), "attn_ready")
                if not last:
                    cumulate(c, 0)
                    cumulate(c, 1)
                finish_head(c, 0, KT1, S0, G, PC_HN)
                c.end()

            c = Pass(dve, "hgrn_in")
            for d in range(2):
                decay_in(c, d, 0)
                decay_out(c, d)
            keys(c, 0)
            cumulate(c, 0)
            cumulate(c, 1)
            c.end()
            with dve.Fori(0, TRIPS["hgrn"]) as i:
                hgrn_head(Pass(dve, "hgrn", i), i, False)
            hgrn_head(Pass(dve, "hgrn_last"), 3, True)

            with dve.Fori(0, TRIPS["gla"]) as i:
                c = Pass(dve, "gla", i)
                own = lambda ins: c.own(ins, "dve_own")
                for d in range(2):
                    c.wait("misc_free", d + 1)
                    f, x = zt(F0 + d), zt(XB[d])
                    c.own(stt(x, f, -1.0, f, ALU.mult, ALU.max), "ln_in")
                for d in range(2):
                    c.wait("ln_out", d + 1)
                    f = zt(F0 + d)
                    own(stt(f, f, 0.0, zt(XB[d]), ALU.min, ALU.subtract))
                    own(ts(f, f, 1.0 / 16.0, None, ALU.mult))
                    cumulate(c, d)
                c.wait_evac(0)
                c.wait_evac(1)
                decayed(c, K0, K0)
                c.wait("sig_ready", 1)
                c.free_tile(tt(zt(gG[0]), zt(gG[0]), PD[0][:, :], ALU.mult), 4)
                level_diff(c, 0)
                level_diff(c, 1)
                carry(c, 6, 0)
                carry(c, 7, 1)
                c.wait("gram_free0", 2)
                c.wait("gram_free1", 2)
                for q in range(NQ + 2):
                    if q < NQ:
                        level_products(c, q, K0, K0)
                    if q >= 2 and q % 2 == 0:
                        level_select(c, q // 2 - 1, gA[0], q)
                    if q + 2 < NQ:
                        if q >= 2:
                            c.wait("gram_done", 4 * (q // 2 + 1))
                        level_diff(c, q + 2)
                    if q >= 2 and q % 2:
                        level_select(c, q // 2 - 1, gA[1], q)
                    if q == 7:
                        c.wait("sig_ready", 2)
                        c.free_tile(tt(zt(gG[1]), zt(gG[1]), PD[1][:, :], ALU.mult), 5)
                for hh in range(2):
                    c.own(dve.memset(SM[:, 15:16], 0.0), "attn_ready")
                for hh in range(2):
                    finish_head(c, hh, F0 + hh, XB[hh], gG[hh], PC_GN)
                c.end()

            dve.wait_ge(cmask_ld, 16)
            with dve.Fori(0, TRIPS["na"]) as i:
                c = Pass(dve, "na", i)
                own = lambda ins: c.own(ins, "dve_own")
                c.wait_dma("bias_ld", 1)
                tr = NTR[:, :, :].rearrange("p e (r k) -> p (e r) k", k=64)
                cm = NCM[:, 0:64].rearrange("p (o k) -> p o k", o=1).to_broadcast([P, 28, 64])
                own(tt(tr, tr, cm, ALU.add))
                for e in range(2):
                    own(tt(NTI[:, e, :], NTR[:, e, P:6 * P], NCM[:, 64:64 + 5 * P], ALU.add))
                for k in range(17):
                    if k < 16:
                        head, t, us = na_step(k)
                        n = len(us) * P
                        at = (us[0] - t + 3) * P
                        bias = NTI[:, head, 0:n] if len(us) == 5 else NTR[:, head, at:at + n]
                        c.wait("s_done", k + 1)
                        dve.sem_inc(dve_step, 1)
                        c.own(dve.tensor_tensor_reduce(NS[:, k % 3, 0:n], PD[k % 2][:, 0:n], bias, 1.0, -3.0e38, ALU.add,
                                                       ALU.max, SM[:, k % 2:k % 2 + 1]), "s_read")
                        c.own(ts(SM[:, 4 + k % 2:5 + k % 2], SM[:, k % 2:k % 2 + 1], -1.0, None, ALU.mult), "max_ready")
                    if k >= 1:
                        m, p = (k - 1) % 2, NS[:, (k - 1) % 3, 0:len(na_step(k - 1)[2]) * P]
                        c.wait("p_exp", k)
                        own(dve.reciprocal(SM[:, 12 + m:13 + m], SM[:, 8 + m:9 + m]))
                        c.own(ts(p, p, SM[:, 12 + m:13 + m], None, ALU.mult), "p_norm")
                    if 8 <= k < 16:
                        t = k - 8
                        if t % 4 == 0:
                            c.wait_dma(f"ada_ld{t // 4}", 1)
                            dve.sem_inc(dve_step, 1)
                        own(dve.tensor_tensor_reduce(zt(NW + t), zt(NW + t), CB[:, :], 1.0, 0.0, ALU.mult, ALU.add, MT[:, t:t + 1]))
                c.own(tt(MOD[:, bass.ds(i * 8 + NADA, 8)], MT[:, :], PRM[:, bass.ds(i * 8 + (PC_BADA + NADA), 8)], ALU.add),
                      "mod_ready")
                c.end()

            c = Pass(dve, "mid")
            for n in range(12):
                at = 8 * (n // 4) + n % 4
                c.wait("hi_ready", n + 1)
                c.own(tt(BIG[:, at + 4, :], H2[:, n, :], BIG[:, at, :].bitcast(F32), ALU.subtract), "lo_ready")
            c.end()
            with dve.Fori(0, TRIPS["merge"]) as i:
                c = Pass(dve, "merge", i)
                for j in range(6):
                    m = H2[:, bass.ds(i * 2 + (4 + j // 3), 1), :].rearrange("p n t -> p (n t)")
                    c.wait_dma(f"in_ld{j % 2}", j // 2 + 1)
                    c.wait_tile(j)
                    to = m if j % 3 == 0 else H2[:, 2, :]
                    c.free_tile(tt(to, zt(24 + j % 2), PD[j % 2][:, :], ALU.mult), j)
                    if j % 3:
                        c.own(tt(m, m, H2[:, 2, :], ALU.add), "dve_own" if j % 3 == 1 else "merged")
                c.end()
            c = Pass(dve, "mid2")
            for ct in range(KD):
                c.wait("hi_ready", ct + 1)
                c.own(tt(BIG[:, KD + ct, :], H2[:, 4 + ct, :], BIG[:, ct, :].bitcast(F32), ALU.subtract), "lo_ready")
            c.own(dve.memset(H2[:, 2, :], 0.0), "dve_own")
            c.end()

            def add_square(c, j, sq, acc):
                c.wait("sq_ready", j + 1)
                c.own(tt(acc, acc, sq, ALU.add), "acc_ready")

            with dve.Fori(0, TRIPS["out"]) as i:
                c = Pass(dve, "out", i)
                for j in range(2):
                    x1 = ZT[:, bass.ds(i * 2 + (16 + j), 1), :].rearrange("p n t -> p (n t)")
                    c.wait_dma(f"in_ld{j}", 1)
                    c.wait_tile(j)
                    c.free_tile(stt(x1, PD[j][:, :], MOD[:, bass.ds(i * 2 + (16 + j), 1)], zt(24 + j), ALU.mult, ALU.add), j)
                for j in range(2):
                    add_square(c, j, H2[:, j, :], H2[:, 2, :])
                c.end()
            c = Pass(dve, "n2")
            own = lambda ins: c.own(ins, "dve_own")
            own(ts(SCL[:, 1, :], MOD[:, 32:40], 1.0, None, ALU.add))
            own(tt(SCL[:, 1, :], SCL[:, 1, :], PRM[:, PC_N2:PC_N2 + KD], ALU.mult))
            norm(c, 16, zt(0), 24, 1)
            c.end()
            for g in range(2):
                with dve.Fori(0, TRIPS["up0"]) as i:
                    c = Pass(dve, f"up{g}", i)
                    c.wait_evac(0)
                    c.wait_tile(1)
                    c.free_tile(tt(zt(25), zt(24), PD[1][:, :], ALU.mult), 1)
                    c.wait("hi_ready", 1)
                    hi = BIG[:, bass.ds(i, 1), :].rearrange("p n t -> p (n t)")
                    lo = BIG[:, bass.ds(i + KF, 1), :].rearrange("p n t -> p (n t)")
                    c.own(tt(lo, zt(25), hi.bitcast(F32), ALU.subtract), "lo_ready")
                    c.end()
                if g == 1:
                    c = Pass(dve, "up1", TRIPS["up1"])
                    dve.memset(H2[:, 11, :], 0.0).then_inc(acc_zero, 1)
                    dve.wait_ge(acc_zero, 1)
                with dve.Fori(0, TRIPS["dn0"]) as i:
                    c = Pass(dve, f"dn{g}", i)
                    for j in range(2):
                        y = zt(24 + j) if g == 0 else H2[:, bass.ds(i * 2 + j, 1), :].rearrange("p n t -> p (n t)")
                        c.wait_dma(f"in_ld{j}", 1)
                        c.wait_tile(j)
                        c.free_tile(stt(y, PD[j][:, :], MOD[:, bass.ds(i * 2 + (40 + j), 1)], zt(24 + j), ALU.mult, ALU.add), j)
                    if g == 1:
                        for j in range(2):
                            add_square(c, j, H2[:, 8 + j, :], H2[:, 11, :])
                    c.end()
            c = Pass(dve, "fin")
            c.wait("rstd_ready", 1)
            for ct in range(KD):
                y = H2[:, ct, :]
                c.own(stt(y, y, PRM[:, PC_NF + ct:PC_NF + ct + 1], H2[:, 10, :], ALU.mult, ALU.mult), "norm_ready")
            c.end()


_NAMES = ["x", "c", "w_ada", "b_ada", "norm1_w", "w_in", "na_rpb", "gla_lr_up", "gla_lr_bias", "gla_norm_w",
          "hgrn_lb_logits", "hgrn_norm_w", "w_proj_na", "w_proj_gla", "w_proj_hgrn", "w_out", "norm2_w",
          "w_ffn_gate", "w_ffn_up", "w_ffn_down", "final_norm_w"]


def kernel(**inputs):
    import numpy as np
    import concourse.bacc as _bacc
    from concourse import mybir as _mybir
    from concourse.bass_utils import run_bass_kernel_spmd as _run

    a = {k: np.asarray(inputs[k]) for k in _NAMES}

    cols = lambda v: v.reshape(-1, P).T
    lrb = a["gla_lr_bias"][0].reshape(2, 2, P).reshape(4, P).T
    prm = np.concatenate([cols(a["c"][0]), cols(a["b_ada"][0]), cols(a["norm1_w"][0]), cols(a["norm2_w"][0]),
                          cols(a["final_norm_w"]), cols(a["gla_norm_w"][0]), cols(a["hgrn_norm_w"][0]),
                          cols(a["hgrn_lb_logits"][0]), lrb], axis=1)
    xt = a["x"][0].T.reshape(KD, P, T).transpose(1, 0, 2)
    pieces = lambda w: w.reshape(w.shape[0] // P, P, w.shape[1] // P, P).transpose(2, 1, 0, 3)
    w_ada = a["w_ada"][0].T.reshape(48, P, D_MODEL).transpose(1, 0, 2)
    w = a["w_in"][0]
    w_lr = np.concatenate([w[:, 3072:3104], np.zeros((D_MODEL, P - 32), w.dtype)], axis=1)
    w_lr = pieces(w_lr)[0]
    order = []
    gate = [5664 + (2 - g % 3) * D_MODEL + (g // 3) * P for g in range(24)]
    head = [[3616 + P * h, 4128 + P * h, 3104 + P * h, 4640 + P * h] for h in range(4)]
    order += head[0]
    for h in range(4):
        order += [5152 + P * h] + (gate[3 * h:3 * h + 3] + head[h + 1] if h < 3 else gate[9:16])
    for p in range(2):
        order += [1536 + P * p, 1792 + P * p, 2048 + 2 * P * p, 2048 + 2 * P * p + P, 2560 + 2 * P * p, 2560 + 2 * P * p + P]
        order += gate[16 + 2 * p:18 + 2 * p]
    for p in range(4):
        order += [P * p, 512 + P * p, 1024 + P * p] + [gate[20 + p]]
    w_in = pieces(np.concatenate([w[:, o:o + P] for o in order], axis=1))
    pr = [pieces(a[f"w_proj_{b}"][0]) for b in ("hgrn", "gla", "na")]
    w_proj = np.stack([pr[n % 3][n // 3] for n in range(24)])
    w_out = pieces(a["w_out"][0])
    wg, wu, wd = pieces(a["w_ffn_gate"][0]), pieces(a["w_ffn_up"][0]), pieces(a["w_ffn_down"][0])
    w_up = np.stack([wg, wu], axis=1).reshape(2, 2 * KF, P, KD, P)
    w_dn = np.stack([wd[:, :, 0:KF], wd[:, :, KF:2 * KF]])
    lup = np.zeros((2, 32, 2, P), w.dtype)
    for s in range(2):
        for p in range(2):
            lup[p, 16 * s:16 * s + 16, s, :] = a["gla_lr_up"][0, s, :, p * P:(p + 1) * P]
    rpb = np.zeros((8, 15, P), w.dtype)
    rpb[:, :, 48:79] = a["na_rpb"][0]

    masks = np.zeros((P, len(LEVELS), P), np.float32)
    j, i = np.arange(P)[:, None], np.arange(P)[None, :]
    for n, s in enumerate(LEVELS):
        same = (j // (2 * s)) == (i // (2 * s))
        masks[:, n, :] = same & ((j % (2 * s) < s) != (i % (2 * s) < s))
    cmat = np.stack([np.ones((P, P), np.float32), np.eye(P, dtype=np.float32)], axis=1)
    qr, qc = np.arange(P) // 64, np.arange(P) % 64
    start = np.clip(qc - 8, 0, 48)
    kc = np.arange(64)
    cmask = np.zeros((P, 64 + 5 * P), np.float32)
    cmask[:, 0:64][(kc[None, :] < start[:, None]) | (kc[None, :] >= start[:, None] + 16)] = NEG_INF
    kr = np.arange(5 * P) // 64 - 4
    off = kr[None, :] - qr[:, None]
    cmask[:, 64:][(off < -4) | (off > 3)] = NEG_INF

    nc = _bacc.Bacc("TRN2", target_bir_lowering=False, num_devices=1)
    arrays, args = {}, []
    for name, v in (("c", a["c"]), ("prm", prm), ("masks", masks), ("cmat", cmat), ("cmask", cmask), ("xt", xt), ("w_ada", w_ada),
                    ("w_lr", w_lr), ("w_in", w_in), ("w_proj", w_proj), ("w_out", w_out), ("w_up", w_up),
                    ("w_dn", w_dn), ("lup", lup), ("rpb", rpb)):
        v = np.ascontiguousarray(v)
        arrays[f"in_{name}_dram"] = v
        args.append(nc.dram_tensor(f"in_{name}_dram", v.shape, _mybir.dt.from_np(v.dtype), kind="ExternalInput").ap())
    args.append(nc.dram_tensor("out_0_dram", (KD, P, T), _mybir.dt.float32, kind="ExternalOutput").ap())
    trunk(nc, *args)
    r = _run(nc, [arrays], core_ids=[0])
    got = r.results[0]["out_0_dram"]
    return got.transpose(2, 0, 1).reshape(1, T, D_MODEL)
```

```python
import concourse.bass as bass
from concourse import mybir
from contextlib import ExitStack

F32 = mybir.dt.float32
F32R = mybir.dt.float32r
U8 = mybir.dt.uint8
ACT = mybir.ActivationFunctionType
ALU = mybir.AluOpType

P = 128
D_MODEL = 1024
T = 1024
KD = 8
HALF = 512
NC = 8
LEVELS = [64, 32, 16, 8, 4, 2, 1]
NQ = 2 * len(LEVELS)
NADA = 16
EPS = 1e-6
F_FLOOR = 1e-30
LN_SPLIT = 2.0 ** -50
KF = 11
NEG_INF = -1e30

PC_BADA, PC_N1, PC_N2, PC_NF, PC_GN, PC_HN, PC_LB, PC_ZB = 0, 48, 56, 64, 72, 73, 74, 82
NPRM = 86

TRIPS = dict(pre=1, hgrn_in=1, hgrn=3, hgrn_last=1, gla0=1, gla1=1, na=2, mid=1, merge=4, mid2=1, out=4, n2=1,
             up0=11, dn0=4, up1=11, dn1=4, fin=1)
TILES = dict(pre=2, hgrn_in=4, hgrn=8, hgrn_last=8, gla0=10, gla1=10, na=6, merge=6, out=2, up0=2, dn0=2, up1=2, dn1=2)
PLAN = {
    "tile": (0, TILES),
    "gram_done": (0, dict(hgrn=18, gla=36)),
    "gram_free0": (1, dict(hgrn=9, gla=18, na=2)),
    "gram_free1": (1, dict(hgrn=9, gla=18)),
    "misc_done": (0, dict(hgrn=6, hgrn_last=8, gla0=10, gla1=8, na=2)),
    "misc_free": (1, dict(hgrn=6, hgrn_last=8, gla0=10, gla1=8, na=2)),
    "z_ready": (0, dict(hgrn_last=2, gla0=2)),
    "dve_own": (0, dict(pre=34, hgrn_in=26, hgrn=56, hgrn_last=30, gla=50, na=54, merge=2, mid2=1, n2=1)),
    "act_own": (0, dict(pre=4, hgrn_in=4, hgrn=23, hgrn_last=19, gla=22, n2=1, fin=1)),
    "param_ready": (0, dict(pre=1)),
    "sig_ready": (0, dict(hgrn=2, gla=2)),
    "qk_ready": (0, dict(gla1=2)),
    "f_ready": (0, dict(hgrn_in=2, hgrn=2, hgrn_last=0)),
    "ln_in": (0, dict(hgrn_in=2, hgrn=2, hgrn_last=0, gla=2)),
    "ln_out": (0, dict(hgrn_in=2, hgrn=2, hgrn_last=0, gla=2)),
    "diff_ready": (0, dict(hgrn_in=2, hgrn=NQ + 2, hgrn_last=NQ, gla=2 + NQ)),
    "exp_ready": (0, dict(hgrn=2 + NQ, gla=2 + NQ)),
    "ksum_ready": (0, dict(hgrn=1)),
    "kdec_ready": (0, dict(hgrn=2, gla=2)),
    "x_ready": (0, dict(hgrn=NQ, gla=NQ)),
    "attn_ready": (0, dict(hgrn=1, gla=2)),
    "osq_ready": (0, dict(hgrn=1, gla=2)),
    "orstd_ready": (0, dict(hgrn=1, gla=2)),
    "o_ready": (0, dict(hgrn=1, gla=2)),
    "sq_ready": (0, dict(pre=8, out=2, dn1=2)),
    "sq_used": (0, dict(pre=8)),
    "acc_ready": (0, dict(out=2, dn1=2)),
    "sum_done": (0, dict(n2=1, fin=1)),
    "rstd_ready": (0, dict(pre=1, n2=1, fin=1)),
    "norm_ready": (0, dict(pre=8, n2=8, fin=8)),
    "hi_ready": (0, dict(pre=8, mid=12, mid2=8, n2=8, up0=1, up1=1)),
    "lo_ready": (0, dict(pre=8, mid=12, mid2=8, n2=8, up0=1, up1=1)),
    "merged": (0, dict(merge=2)),
    "s_done": (0, dict(na=32)),
    "s_read": (0, dict(na=32)),
    "pv_done": (0, dict(na=2)),
    "max_ready": (0, dict(na=32)),
    "p_exp": (0, dict(na=32)),
    "p_norm": (0, dict(na=32)),
    "pt_done": (0, dict(na=32)),
    "pt_ready": (0, dict(na=32)),
    "ada_ld0": (0, dict(na=2)),
    "ada_ld1": (0, dict(na=2)),
    "mod_ready": (1, dict(na=2)),
    "bias_ld": (0, dict(na=2)),
    "o_st": (1, dict(hgrn=1, gla=2, na=2)),
    "gate_st0": (1, dict(hgrn=1, hgrn_last=3, gla0=1, gla1=2)),
    "gate_st1": (1, dict(hgrn=1, hgrn_last=2, gla0=1, gla1=2)),
    "gate_st2": (1, dict(hgrn=1, hgrn_last=2, gla1=2)),
    "in_ld0": (0, dict(merge=3, out=1, dn0=1, dn1=1)),
    "in_ld1": (0, dict(merge=3, out=1, dn0=1, dn1=1)),
    "y_st0": (0, dict(out=1, dn0=1)),
    "y_st1": (0, dict(out=1, dn0=1)),
    "out_st": (0, dict(fin=8)),
}
for _, per in PLAN.values():
    if "hgrn" in per:
        per.setdefault("hgrn_last", per["hgrn"])
    if "gla" in per:
        per["gla0"] = per["gla1"] = per.pop("gla")


def trunk(nc, cvec, prm, masks, cmat, cmask, xt, w_ada, w_lr, w_in, w_proj, w_out, w_up, w_dn, lup, rpb, out):
    base = {}
    for name, (first, per) in PLAN.items():
        n, base[name] = first, {}
        for st in TRIPS:
            base[name][st] = n
            n += TRIPS[st] * per.get(st, 0)

    ctx = ExitStack()
    with ctx:
        sems = {k: ctx.enter_context(nc.semaphore(k)) for k in PLAN if k != "tile"}
        sem = lambda name: ctx.enter_context(nc.semaphore(name))
        w_raw = [sem("w_raw0"), sem("w_raw1")]
        w_hi = sem("w_hi")
        w_ready = sem("w_ready")
        tile_done = sem("tile_done")
        tile_free = [sem("tile_free0"), sem("tile_free1")]
        const_ld = sem("const_ld")
        x_ld = [sem(f"x_ld{k}") for k in range(2)]
        ada_pre = [sem(f"ada_pre{k}") for k in range(4)]
        o_ld = [sem(f"o_ld{b}") for b in range(4)]
        rpb_st = sem("rpb_st")
        lr_st, lr_ld = sem("lr_st"), sem("lr_ld")
        lup_ld = sem("lup_ld")
        cmask_ld = sem("cmask_ld")
        acc_zero = sem("acc_zero")
        pool_step, dve_step = sem("pool_step"), sem("dve_step")

        class Pass:

            def __init__(self, e, stage, i=0):
                self.e, self.st, self.i, self.n = e, stage, i, {}

            def at(self, name, n):
                return base[name][self.st] + PLAN[name][1].get(self.st, 0) * self.i + n

            def up(self, name):
                self.n[name] = self.n.get(name, 0) + 1
                return sems[name]

            def tile(self, j):
                return self.at("tile", j)

            def tile_half(self, j):
                b, k = base["tile"][self.st], TILES[self.st]
                return b // 2 + (k // 2) * self.i + j // 2

            def free_tile(self, ins, j):
                ins.then_inc(tile_free[j % 2], 1)
                self.e.wait_ge(tile_free[j % 2], self.tile_half(j) + 1)

            def own(self, ins, name):
                ins.then_inc(self.up(name), 1)
                self.e.wait_ge(sems[name], self.at(name, self.n[name]))

            def free(self, ins, name, use):
                ins.then_inc(sems[name], 1)
                self.e.wait_ge(sems[name], self.at(name, use + 1))

            def end(self):
                for k, v in self.n.items():
                    assert v == PLAN[k][1].get(self.st, 0), (k, self.st, v)

        start = -(-nc.sbuf_base // 32) * 32
        fence = ctx.enter_context(nc.sbuf_tensor("fence", [P, (nc.sbuf_usable_end - start) // 4 - 16], F32))
        del fence
        place = [start]

        def at(name, offset, shape, dt=F32):
            return nc.alloc_sbuf_tensor_at(name, shape, dt, offset=offset)

        def sb(name, shape, dt=F32):
            n = 1 if dt == U8 else 4
            for k in shape[1:]:
                n *= k
            place[0] += -(-n // 32) * 32
            return at(name, place[0] - -(-n // 32) * 32, shape, dt)

        WR = sb("WR", [P, 2, 2, KF, P], F32R)
        RAW = sb("RAW", [P, 2, KF, P])
        hs_at = place[0]
        HS = sb("HS", [P, 16, T], F32R)
        H2 = at("H2", hs_at, [P, 16, T])
        z_at = place[0]
        ZT = sb("ZT", [P, 26, T])
        BIG = at("BIG", z_at, [P, 24, T], F32R)
        px_at = z_at + 22 * T * 4
        PX = at("PX", px_at, [P, 2, NC, P + 1])
        CB = at("CB", px_at + 2 * NC * (P + 1) * 4, [P, T])
        LR = at("LR", px_at + (2 * NC * (P + 1) + T) * 4, [32, T])
        sb("rest_of_LR", [P, 16])
        PRM = sb("PRM", [P, NPRM])
        MOD = sb("MOD", [P, 48])
        SCL = sb("SCL", [P, 2, KD])
        MT = sb("MT", [P, 8])
        LB = sb("LB", [P, 2, 8])
        EP = sb("EP", [P, 2])
        MASK = sb("MASK", [P, len(LEVELS), P], U8)
        CM = sb("CM", [P, 2, P])
        LUP = sb("LUP", [32, 2, 2, P])
        AN = sb("AN", [P, 2, NC])
        SM = sb("SM", [P, 16])
        MASKF = at("MASKF", hs_at + 10 * T * 4, [P, len(LEVELS), P])
        ONES, IDENT = CM[:, 0, :], CM[:, 1, :]
        zt = lambda k: ZT[:, k, :]

        PD = [ctx.enter_context(nc.psum_tensor(f"PD{j}", [P, T], F32)) for j in range(2)]
        PG = ctx.enter_context(nc.psum_tensor("PG", [P, T], F32))
        PM = ctx.enter_context(nc.psum_tensor("PM", [P, T], F32))

        gates_dr = nc.dram_tensor("gates_scratch", [24, P, T], F32).ap()
        o_dr = nc.dram_tensor("o_scratch", [12, P, T], F32).ap()
        y_dr = nc.dram_tensor("y_scratch", [8, P, T], F32).ap()
        lr_dr = nc.dram_tensor("lr_scratch", [32, T], F32).ap()
        bias_dr = nc.dram_tensor("bias_scratch", [8, P, 14 * 64], F32).ap()

        Q, K0, K1, F0, F1, V, G = range(7)
        XB = [7, 8, 9, 10]
        A0, VT0, KT0, KT1, QD0, QD1, S0, S1, GB = 11, 12, 13, 14, 15, 16, 17, 18, 19
        LNX = KT1
        QRAW = KT0
        gV = [K1, V]
        gG = [G, 19]
        gA = [A0, 20]
        gVT = [VT0, 21]

        def blocks(ap, s):
            return ap.rearrange("p (b t) -> p b t", t=2 * s)

        def px_view(d, s):
            lo = 1 - d
            nb = P // (2 * s)
            v = PX[:, d, :, lo:lo + P].rearrange("p c (b t) -> p c b t", t=2 * s)
            r = PX[:, d, :, s:s + 2 * s * (nb - 1) + 1:2 * s] if nb > 1 else PX[:, d, :, s:s + 1]
            r = r.rearrange("p c (b o) -> p c b o", o=1).to_broadcast([P, NC, nb, 2 * s])
            return v, r

        def px_last(d):
            return PX[:, d, :, P:P + 1].to_broadcast([P, NC, P])

        NQT, NK, NV, NVT, NW = 0, 1, 2, 3, 14
        NS = at("NS", z_at + 4 * T * 4, [P, 3, 5 * P])
        NPT = at("NPT", z_at + 6 * T * 4, [P, 2, 5 * P])
        NTR = at("NTR", z_at + 7424 * 4, [P, 2, 14 * 64])
        NTI = at("NTI", z_at + 9216 * 4, [P, 2, 5 * P])
        NCM = at("NCM", z_at + 10496 * 4, [P, 64 + 5 * P])

        def na_step(k):
            t = k % 8
            us = range(0, 4) if t < 2 else range(4, 8) if t > 5 else range(t - 2, t + 3)
            return k // 8, t, list(us)

        chunked = lambda ap: ap.rearrange("p (c t) -> p c t", t=P)

        block = ctx.enter_context(nc.Block())

        @block.sync
        def _(sp):
            sp.dma_start(PRM[:, :], prm).then_inc(const_ld, 16)
            sp.dma_start(CM[:, :, :], cmat).then_inc(const_ld, 16)
            sp.dma_start(MASKF[:, :, :], masks).then_inc(const_ld, 16)
            sp.dma_start(CB[:, :], cvec.to_broadcast([P, T])).then_inc(const_ld, 16)
            for k in range(2):
                sp.dma_start(ZT[:, 16 + 4 * k:20 + 4 * k, :], xt[:, 4 * k:4 * k + 4, :]).then_inc(x_ld[k], 16)
            for k in range(4):
                sp.dma_start(ZT[:, 4 * k:4 * k + 4, :], w_ada[:, 4 * k:4 * k + 4, :]).then_inc(ada_pre[k], 16)
                if k == 1:
                    sp.dma_start(RAW[:, 1, 0:KD, :], w_lr).then_inc(w_raw[1], 16)

            def load(c, j, src):
                sp.wait_ge(w_ready, c.tile(j) - 1)
                sp.dma_start(RAW[:, j % 2, 0:src.shape[2], :], src.rearrange("n p k m -> p (n k) m")
                             ).then_inc(w_raw[j % 2], 16)

            for st in ("hgrn_in", "hgrn", "hgrn_last", "gla0", "gla1", "na"):
                per, first = TILES[st], base["tile"][st] - TILES["pre"]
                with sp.Fori(0, TRIPS[st]) as i:
                    c = Pass(sp, st, i)
                    for j in range(per):
                        load(c, j, w_in[bass.ds(i * per + (first + j), 1)])
                        if st == "na" and j % 3 == 2:
                            sp.wait_ge(sems["mod_ready"], c.at("mod_ready", j // 3))
                            sp.wait_ge(tile_free[0], c.tile_half(0) + 1)
                            for a in range(2):
                                sp.dma_start(ZT[:, NW + 4 * a:NW + 4 * a + 4, :],
                                             w_ada[:, bass.ds(i * 16 + (NADA + 8 * (j // 3) + 4 * a), 4), :]
                                             ).then_inc(sems[f"ada_ld{a}"], 16)
            c = Pass(sp, "merge")
            sp.wait_ge(tile_done, c.tile(0))
            for b, rows in enumerate((range(0, 4), range(4, 8), range(8, 11))):
                if b == 2:
                    sp.wait_ge(sems["o_st"], c.at("o_st", -1) * 16)
                else:
                    sp.wait_ge(sems["o_st"], Pass(sp, "na").at("o_st", 0) * 16)
                sp.dma_start(H2[:, rows.start:rows.stop, :], o_dr[rows.start:rows.stop].rearrange("n p t -> p n t")
                             ).then_inc(o_ld[b], 16)
            for st, src, per in (("merge", w_proj, 6), ("out", w_out, 2), ("up0", w_up[0], 2), ("dn0", w_dn[0], 2),
                                 ("up1", w_up[1], 2), ("dn1", w_dn[1], 2)):
                with sp.Fori(0, TRIPS[st]) as i:
                    c = Pass(sp, st, i)
                    for j in range(per):
                        load(c, j, src[bass.ds(i * per + j, 1)])

        @block.gpsimd
        def _(pool):
            pool.sem_inc(w_raw[0], 16)
            for h in range(8):
                for r in range(2):
                    src = bass.AP(rpb.tensor, h * 15 * P + (1 - r) * P + 63, [[P, 14], [-1, 64], [1, 64]])
                    dst = bass.AP(bias_dr.tensor, (h * P + 64 * r) * 896, [[64, 14], [896, 64], [1, 64]])
                    pool.dma_start(dst, src).then_inc(rpb_st, 16)

            def split(slot, kt, n, half, inc):
                pool.wait_ge(w_raw[slot], 16 * (half + 1))
                if not (isinstance(n, int) and n - 1 <= 0):
                    pool.wait_ge(tile_done, n - 1)
                pool.sem_inc(pool_step, 1)
                raw, hi, lo = RAW[:, slot, 0:kt, :], WR[:, slot, 0, 0:kt, :], WR[:, slot, 1, 0:kt, :]
                pool.tensor_copy(hi, raw).then_inc(w_hi, inc)
                pool.wait_ge(w_hi, n + 1)
                pool.tensor_tensor(lo, raw, hi.bitcast(F32), ALU.subtract).then_inc(w_ready, inc)

            split(1, KD, 1, 0, 2)
            for st, kt in (("hgrn_in", 8), ("hgrn", 8), ("hgrn_last", 8), ("gla0", 8), ("gla1", 8), ("na", 8),
                           ("merge", 4), ("out", 8), ("up0", 8), ("dn0", KF),
                           ("up1", 8), ("dn1", KF)):
                with pool.Fori(0, TRIPS[st] * TILES[st] // 2) as i:
                    b = base["tile"][st]
                    for j in range(2):
                        split(j, kt, i * 2 + (b + j), i + b // 2, 1)

        @block.tensor
        def _(pe):
            def dense(c, j, kt, mov, lo_at, each=None):
                pe.wait_ge(w_ready, c.tile(j) + 1)
                pe.wait_ge(tile_free[j % 2], c.tile_half(j))
                s = j % 2
                for k in range(kt):
                    if each is not None:
                        pe.wait_ge(sems["lo_ready"], Pass(pe, each[0]).at("lo_ready", each[1] + k + 1))
                    for n, (w, x) in enumerate(((0, 0), (0, lo_at), (1, 0))):
                        for h in range(2):
                            last = pe.matmul(PD[s][:, h * HALF:(h + 1) * HALF], WR[:, s, w, k, :],
                                             mov[:, k + x, h * HALF:(h + 1) * HALF],
                                             start=(k == 0 and n == 0), stop=(k == kt - 1 and n == 2))
                last.then_inc(tile_done, 1)

            def sum_squares(c, src):
                for ct in range(KD):
                    pe.wait_ge(sems["sq_ready"], c.at("sq_ready", ct + 1))
                    for h in range(2):
                        last = pe.matmul(PG[:, h * HALF:(h + 1) * HALF], ONES, src(ct)[:, h * HALF:(h + 1) * HALF],
                                         start=(ct == 0), stop=(ct == KD - 1))
                    last.then_inc(c.up("sq_used"), 1)

            def total(c, acc):
                for h in range(2):
                    last = pe.matmul(PG[:, h * HALF:(h + 1) * HALF], ONES, acc[:, h * HALF:(h + 1) * HALF],
                                     start=True, stop=True)
                last.then_inc(c.up("sum_done"), 1)

            c = Pass(pe, "pre")
            pe.wait_ge(const_ld, 64)
            sum_squares(c, lambda ct: H2[:, 8 + ct % 2, :])
            pe.wait_ge(w_ready, 2)
            for k in range(KD):
                pe.wait_ge(sems["lo_ready"], c.at("lo_ready", k + 1))
                for n, (w, x) in enumerate(((0, 0), (0, KD), (1, 0))):
                    for h in range(2):
                        last = pe.matmul(PD[1][:, h * HALF:(h + 1) * HALF], WR[:, 1, w, k, :],
                                         HS[:, k + x, h * HALF:(h + 1) * HALF],
                                         start=(k == 0 and n == 0), stop=(k == KD - 1 and n == 2))
            last.then_inc(tile_done, 1)
            c.end()

            def turn(c, src, use):
                pe.wait_ge(sems["misc_free"], c.at("misc_free", use))
                for n in range(NC):
                    last = pe.transpose(PM[:, n * P:(n + 1) * P], src[:, n * P:(n + 1) * P], IDENT)
                last.then_inc(c.up("misc_done"), 1)

            def gram(c, use, lhs, rhs, rows):
                for h in range(2):
                    pe.wait_ge(sems[f"gram_free{h}"], c.at(f"gram_free{h}", use))
                    for n in range(4 * h, 4 * h + 4):
                        last = pe.matmul(PG[:, n * P:(n + 1) * P], lhs[rows, n * P:(n + 1) * P],
                                         rhs[rows, n * P:(n + 1) * P], start=True, stop=True)
                    last.then_inc(c.up("gram_done"), 1)

            def level(c, use, l, rows):
                s = LEVELS[l]
                xf, xb = zt(XB[2 * l % 4])[rows, :], zt(XB[2 * l % 4 + 1])[rows, :]
                for h in range(2):
                    pe.wait_ge(sems[f"gram_free{h}"], c.at(f"gram_free{h}", use))
                    for n in range(4 * h, 4 * h + 4):
                        cols = slice(n * P, (n + 1) * P)
                        to = blocks(PG[:, cols], s)
                        pe.matmul(to[:, :, s:], xf[:, cols], blocks(xf[:, cols], s)[:, :, s:], start=True, stop=True)
                        last = pe.matmul(to[:, :, 0:s], xb[:, cols], blocks(xb[:, cols], s)[:, :, 0:s],
                                         start=True, stop=True)
                    last.then_inc(c.up("gram_done"), 1)

            def states(c, use, d, heads):
                pe.wait_ge(sems["misc_free"], c.at("misc_free", use))
                KT = zt(KT0 + d)
                for n in (range(0, 7) if d == 0 else range(1, 8)):
                    for m, (rows, vt) in enumerate(heads):
                        last = pe.matmul(PM[rows, n * P:(n + 1) * P], KT[:, n * P + rows.start:n * P + rows.stop],
                                         zt(vt)[:, n * P:(n + 1) * P], start=True, stop=True)
                last.then_inc(c.up("misc_done"), 1)

            def outputs(c, use, rows, vt, a):
                pe.wait_ge(sems["misc_free"], c.at("misc_free", use))
                for n in range(NC):
                    cols = slice(n * P, (n + 1) * P)
                    terms = [(zt(vt)[:, cols], zt(a)[:, cols])]
                    if n > 0:
                        terms.append((zt(S0)[rows, cols], zt(QD0)[rows, cols]))
                    if n < NC - 1:
                        terms.append((zt(S1)[rows, cols], zt(QD1)[rows, cols]))
                    for m, (l, r) in enumerate(terms):
                        last = pe.matmul(PM[:, cols], l, r, start=(m == 0), stop=(m == len(terms) - 1))
                last.then_inc(c.up("misc_done"), 1)

            def head_sums(c, use, nth, sq):
                pe.wait_ge(sems["osq_ready"], c.at("osq_ready", nth + 1))
                for h in range(2):
                    pe.wait_ge(sems[f"gram_free{h}"], c.at(f"gram_free{h}", use))
                    pe.matmul(PG[:, h * HALF:(h + 1) * HALF], ONES, zt(sq)[:, h * HALF:(h + 1) * HALF],
                              start=True, stop=True).then_inc(c.up("gram_done"), 1)

            ALL = slice(0, P)
            c = Pass(pe, "hgrn_in")
            for j in range(4):
                dense(c, j, KD, HS, KD)
            c.end()

            def low_rank(c, pair, d, use):
                pe.wait_ge(lup_ld, 16)
                pe.wait_ge(lr_ld, 16)
                pe.wait_ge(sems["misc_free"], c.at("misc_free", use))
                for h in range(2):
                    last = pe.matmul(PM[:, h * HALF:(h + 1) * HALF], LUP[:, pair, d, :], LR[:, h * HALF:(h + 1) * HALF],
                                     start=True, stop=True)
                last.then_inc(c.up("misc_done"), 1)

            def hgrn_head(c, last):
                pe.wait_ge(tile_free[1], c.tile_half(-1) + 1)
                turn(c, zt(V), 0)
                dense(c, 0, KD, HS, KD)
                dense(c, 1, KD, HS, KD)
                for d in range(2):
                    pe.wait_ge(sems["kdec_ready"], c.at("kdec_ready", d + 1))
                    turn(c, zt(F0 + d), 1 + d)
                pe.wait_ge(sems["misc_free"], c.at("misc_free", 3))
                states(c, 3, 0, [(ALL, VT0)])
                pe.wait_ge(sems["ksum_ready"], c.at("ksum_ready", 1))
                gram(c, 0, zt(V), zt(Q), ALL)
                states(c, 4, 1, [(ALL, VT0)])
                for l in range(len(LEVELS)):
                    pe.wait_ge(sems["x_ready"], c.at("x_ready", 2 * l + 2))
                    level(c, 1 + l, l, ALL)
                    if l < 6:
                        dense(c, 2 + l, KD, HS, KD)
                    if last and l in (3, 4):
                        low_rank(c, 0, l - 3, 5 + l - 3)
                pe.wait_ge(sems["attn_ready"], c.at("attn_ready", 1))
                outputs(c, 7 if last else 5, ALL, VT0, A0)
                head_sums(c, 8, 0, A0)
                c.end()

            with pe.Fori(0, TRIPS["hgrn"]) as i:
                hgrn_head(Pass(pe, "hgrn", i), False)
            hgrn_head(Pass(pe, "hgrn_last"), True)

            ROWS = [slice(0, 64), slice(64, 128)]
            def gla_pair(c, pair, first, fills):
                for j in range(first + 2):
                    dense(c, j, KD, HS, KD)
                for hh in range(2):
                    pe.wait_ge(tile_free[(first + hh) % 2], c.tile_half(first + hh) + 1)
                    turn(c, zt(gV[hh]), hh)
                dense(c, first + 2, KD, HS, KD)
                for d in range(2):
                    pe.wait_ge(sems["kdec_ready"], c.at("kdec_ready", d + 1))
                    turn(c, zt(F0 + d), 2 + d)
                pe.wait_ge(sems["misc_free"], c.at("misc_free", 4))
                for d in range(2):
                    states(c, 4 + d, d, list(zip(ROWS, gVT)))
                    gram(c, d, zt(K0), zt(Q), ROWS[d])
                for l in range(len(LEVELS)):
                    pe.wait_ge(sems["x_ready"], c.at("x_ready", 2 * l + 2))
                    for hh in range(2):
                        level(c, 2 + 2 * l + hh, l, ROWS[hh])
                    if l < fills:
                        dense(c, first + 3 + l, KD, HS, KD)
                    if pair == 0 and l in (3, 4):
                        low_rank(c, 1, l - 3, 6 + l - 3)
                for hh in range(2):
                    pe.wait_ge(sems["attn_ready"], c.at("attn_ready", hh + 1))
                    outputs(c, (8, 6)[pair] + hh, ROWS[hh], gVT[hh], gA[hh])
                for hh in range(2):
                    head_sums(c, 16 + hh, hh, XB[2 + hh])
                c.end()

            gla_pair(Pass(pe, "gla0"), 0, 2, 5)
            gla_pair(Pass(pe, "gla1"), 1, 0, 7)

            with pe.Fori(0, TRIPS["na"]) as i:
                c = Pass(pe, "na", i)
                for u in range(2):
                    for j in range(3 * u, 3 * u + 3):
                        dense(c, j, KD, HS, KD)
                    pe.wait_ge(tile_free[(3 * u + 2) % 2], c.tile_half(3 * u + 2) + 1)
                    turn(c, zt(NV), u)
                    pe.wait_ge(sems["misc_free"], c.at("misc_free", u + 1))
                    pe.wait_ge(tile_free[(3 * u + 1) % 2], c.tile_half(3 * u + 1) + 1)
                    pe.wait_ge(sems["gram_free0"], c.at("gram_free0", u))
                    if u == 0:
                        pe.wait_ge(sems["gram_free1"], c.at("gram_free1", 0))
                    for k in range(19):
                        if k < 16:
                            if k >= 2:
                                pe.wait_ge(sems["s_read"], c.at("s_read", 16 * u + k - 1))
                            head, t, us = na_step(k)
                            rows, n = ROWS[head], len(us) * P
                            for lo in range(0, n, HALF):
                                hi = min(n, lo + HALF)
                                last = pe.matmul(PD[k % 2][:, lo:hi], zt(NQT)[rows, t * P:(t + 1) * P],
                                                 zt(NK)[rows, us[0] * P + lo:us[0] * P + hi], start=True, stop=True)
                            last.then_inc(c.up("s_done"), 1)
                        if 2 <= k <= 17:
                            pe.wait_ge(sems["p_norm"], c.at("p_norm", 16 * u + k - 1))
                            if k >= 3:
                                pe.wait_ge(sems["pt_ready"], c.at("pt_ready", 16 * u + k - 2))
                            for m in range(len(na_step(k - 2)[2])):
                                last = pe.transpose(PM[:, m * P:(m + 1) * P], NS[:, (k - 2) % 3, m * P:(m + 1) * P], IDENT)
                            last.then_inc(c.up("pt_done"), 1)
                        if k >= 3:
                            pe.wait_ge(sems["pt_ready"], c.at("pt_ready", 16 * u + k - 2))
                            head, t, us = na_step(k - 3)
                            rows = ROWS[head]
                            for m, kt in enumerate(us):
                                last = pe.matmul(PG[rows, t * P:(t + 1) * P], zt(NVT)[:, kt * P + rows.start:kt * P + rows.stop],
                                                 NPT[:, (k - 3) % 2, m * P:(m + 1) * P],
                                                 start=(m == 0), stop=(m == len(us) - 1))
                    last.then_inc(c.up("pv_done"), 1)
                c.end()

            with pe.Fori(0, TRIPS["merge"]) as i:
                c = Pass(pe, "merge", i)
                for j in range(6):
                    dense(c, j, 4, BIG[:, 8 * (j % 3):8 * (j % 3) + 8, :], 4, ("mid", 4 * (j % 3)))
            with pe.Fori(0, TRIPS["out"]) as i:
                c = Pass(pe, "out", i)
                dense(c, 0, KD, BIG, KD, ("mid2", 0))
                dense(c, 1, KD, BIG, KD)
            c = Pass(pe, "n2")
            pe.wait_ge(sems["acc_ready"], c.at("acc_ready", 0))
            total(c, H2[:, 2, :])
            c.end()
            for g in range(2):
                with pe.Fori(0, TRIPS[f"up{g}"]) as i:
                    c = Pass(pe, f"up{g}", i)
                    dense(c, 0, KD, HS, KD, ("n2", 0))
                    dense(c, 1, KD, HS, KD)
                with pe.Fori(0, TRIPS[f"dn{g}"]) as i:
                    c = Pass(pe, f"dn{g}", i)
                    dense(c, 0, KF, BIG, KF, (f"up{g}", 0))
                    dense(c, 1, KF, BIG, KF)
            c = Pass(pe, "fin")
            pe.wait_ge(sems["acc_ready"], c.at("acc_ready", 0))
            total(c, H2[:, 11, :])
            c.end()

        @block.scalar
        def _(act):
            act.sem_inc(sems["gram_free0"], 1)
            act.sem_inc(sems["gram_free1"], 1)
            act.sem_inc(sems["misc_free"], 1)
            act.sem_inc(sems["mod_ready"], 1)
            for m in range(3):
                act.sem_inc(sems[f"gate_st{m}"], 16)
            act.sem_inc(sems["o_st"], 16)
            act.sem_inc(tile_free[0], 1)
            act.sem_inc(tile_done, 1)
            A = act.activation

            def squares(c, src, dst):
                for ct in range(KD):
                    if ct % 4 == 0:
                        act.wait_ge(x_ld[ct // 4], 16)
                    if ct >= 2:
                        act.wait_ge(sems["sq_used"], c.at("sq_used", ct - 1))
                    c.own(A(dst(ct), src(ct), ACT.Square), "sq_ready")

            def rstd(c, dst, ps, width, name):
                c.own(A(dst, ps, ACT.Ln, bias=EP[:, 0:1], scale=1.0 / width), "act_own")
                c.own(A(dst, dst, ACT.Exp, scale=-0.5), name)

            c = Pass(act, "pre")
            act.wait_ge(const_ld, 64)
            c.own(A(H2[:, 12, :], CB[:, :], ACT.Sigmoid), "act_own")
            act.wait_ge(sems["param_ready"], c.at("param_ready", 1))
            c.own(A(LB[:, 0, :], LB[:, 0, :], ACT.Exp), "act_own")
            squares(c, lambda ct: zt(16 + ct), lambda ct: H2[:, 8 + ct % 2, :])
            act.wait_ge(sems["sq_used"], c.at("sq_used", 8))
            rstd(c, H2[:, 15, :], PG[:, :], 1024.0, "rstd_ready")
            for ct in range(KD):
                act.wait_ge(sems["norm_ready"], c.at("norm_ready", ct + 1))
                c.own(A(HS[:, ct, :], zt(16 + ct), ACT.Identity, bias=MOD[:, ct:ct + 1]), "hi_ready")
            act.wait_ge(tile_done, 2)
            c.own(A(zt(0)[0:32, :], PD[1][0:32, :], ACT.Copy), "act_own")
            act.sem_inc(tile_free[1], 1)
            act.dma_start(lr_dr, zt(0)[0:32, :]).then_inc(lr_st, 16)
            act.wait_ge(lr_st, 16)
            act.dma_start(LR[:, :], lr_dr).then_inc(lr_ld, 16)
            act.dma_start(LUP[:, :, :, :], lup).then_inc(lup_ld, 16)
            c.end()

            EARLY = dict(hgrn=-2, hgrn_last=-2, gla0=0, gla1=0)

            def evac_turned(c, dst, use, nth):
                act.wait_ge(sems["misc_done"], c.at("misc_done", nth))
                c.free(A(dst, PM[:, :], ACT.Copy), "misc_free", use)

            def decays(c, d):
                act.wait_ge(sems["diff_ready"], c.at("diff_ready", EARLY[c.st] + d + 1))
                x, lo = zt(XB[d]), 1 - d
                dst = zt(QD0) if d == 0 else zt(F1)
                c.own(A(chunked(dst), PX[:, d, :, lo:lo + P], ACT.Exp), "act_own")
                c.own(A(AN[:, d, :], PX[:, d, :, P], ACT.Exp), "act_own")
                c.own(A(x, x, ACT.Exp, scale=-1.0), "exp_ready")

            def level_exp(c, q):
                s = LEVELS[q // 2]
                act.wait_ge(sems["diff_ready"], c.at("diff_ready", EARLY[c.st] + 2 + q + 1))
                x = blocks(zt(XB[q % 4]), s)
                c.own(A(x[:, :, 0:s], x[:, :, 0:s], ACT.Exp, scale=-1.0), "act_own")
                c.own(A(x[:, :, s:], x[:, :, s:], ACT.Exp), "exp_ready")

            def store_gate(c, j, m, row, gb):
                act.wait_ge(tile_done, c.tile(j) + 1)
                act.wait_ge(sems[f"gate_st{m}"], c.at(f"gate_st{m}", c.n.get(f"gate_st{m}", 0)) * 16)
                c.free_tile(A(zt(gb), PD[j % 2][:, :], ACT.Sigmoid), j)
                act.dma_start(gates_dr[bass.ds(row, 1)].rearrange("n p t -> (n p) t"), zt(gb)
                              ).then_inc(c.up(f"gate_st{m}"), 16)

            def head_out(c, use, ob, sq):
                act.wait_ge(sems["misc_done"], c.at("misc_done", use + 1))
                c.free(A(zt(ob), PM[:, :], ACT.Copy), "misc_free", use)
                c.own(A(zt(sq), zt(ob), ACT.Square), "osq_ready")

            def head_rstd(c, rb, gu):
                act.wait_ge(sems["gram_done"], c.at("gram_done", 2 * gu + 2))
                c.own(A(zt(rb), PG[:, :], ACT.Ln, bias=EP[:, 0:1], scale=1.0 / P), "act_own")
                act.sem_inc(sems["gram_free0"], 1)
                act.sem_inc(sems["gram_free1"], 1)
                c.own(A(zt(rb), zt(rb), ACT.Exp, scale=-0.5), "orstd_ready")

            def store_o(c, nth, row, ob):
                act.wait_ge(sems["o_ready"], c.at("o_ready", nth + 1))
                act.dma_start(o_dr[bass.ds(row, 1)].rearrange("n p t -> (n p) t"), zt(ob)).then_inc(c.up("o_st"), 16)

            def raw_tile(c, j, dst):
                act.wait_ge(tile_done, c.tile(j) + 1)
                c.free_tile(A(zt(dst), PD[j % 2][:, :], ACT.Copy), j)

            def low_rank(c, pair, d, use):
                act.wait_ge(sems["misc_done"], c.at("misc_done", use + 1))
                bias = PRM[:, pair + PC_ZB + 2 * d:pair + PC_ZB + 2 * d + 1]
                c.free(A(zt(F0 + d), PM[:, :], ACT.Identity, bias=bias), "misc_free", use)
                act.sem_inc(c.up("z_ready"), 1)

            def hgrn_head(c, i, fill, last):
                c.own(A(zt(Q), zt(QRAW), ACT.Sigmoid), "sig_ready")
                evac_turned(c, zt(VT0), 0, 1)
                for d in range(2):
                    decays(c, d)
                act.wait_ge(tile_done, c.tile(0) + 1)
                c.own(A(zt(G), PD[0][:, :], ACT.Sigmoid), "sig_ready")
                store_gate(c, 1, 0, i * 3, GB)
                act.wait_ge(sems["o_st"], c.at("o_st", 0) * 16)
                for d in range(2):
                    evac_turned(c, zt(KT0 + d), 1 + d, 2 + d)
                    level_exp(c, d)
                for h in range(2):
                    act.wait_ge(sems["gram_done"], c.at("gram_done", h + 1))
                    c.free(A(zt(A0)[:, h * HALF:(h + 1) * HALF], PG[:, h * HALF:(h + 1) * HALF], ACT.Copy), f"gram_free{h}", 0)
                for q in range(2, NQ):
                    level_exp(c, q)
                    if q >= 5 and q % 2:
                        fill(c, q // 2)
                        if last and q >= 11:
                            low_rank(c, 0, (q - 11) // 2, 5 + (q - 11) // 2)
                fill(c, 7)
                head_out(c, 7 if last else 5, KT1, A0)
                head_rstd(c, S0, 8)
                store_o(c, 0, i, KT1)
                c.end()

            def decay_tile(c, j, d):
                act.wait_ge(tile_done, c.tile(j) + 1)
                c.own(A(zt(GB + d), PD[j % 2][:, :], ACT.Sigmoid, scale=-1.0), "act_own")
                c.free_tile(A(zt(F0 + d), PD[j % 2][:, :], ACT.Sigmoid), j)
                act.sem_inc(c.up("f_ready"), 1)

            def decay_ln(c, d):
                act.wait_ge(sems["ln_in"], c.at("ln_in", d + 1))
                c.own(A(zt(F0 + d), zt(F0 + d), ACT.Ln), "act_own")
                c.own(A(zt(LNX), zt(LNX), ACT.Ln), "ln_out")

            def fill_head(c, j):
                if j < 4:
                    store_gate(c, j, j - 1, c.i * 3 + (j - 1), GB + j - 1)
                elif j < 6:
                    if j == 5:
                        decay_ln(c, 0)
                    act.wait_ge(sems[f"gate_st{j - 4}"], c.at(f"gate_st{j - 4}", 1) * 16)
                    decay_tile(c, j, j - 4)
                else:
                    if j == 6:
                        decay_ln(c, 1)
                    raw_tile(c, j, (QRAW, V)[j - 6])

            c = Pass(act, "hgrn_in")
            for d in range(2):
                decay_tile(c, d, d)
                decay_ln(c, d)
            raw_tile(c, 2, QRAW)
            raw_tile(c, 3, V)
            c.end()
            with act.Fori(0, TRIPS["hgrn"]) as i:
                hgrn_head(Pass(act, "hgrn", i), i, fill_head, False)
            hgrn_head(Pass(act, "hgrn_last"), 3,
                      lambda c, j: store_gate(c, j, (j - 1) % 3, 9 + (j - 1), GB + (j - 1) % 3), True)

            def gla_pair(c, i, first, fill):
                for d in range(2):
                    act.wait_ge(sems["ln_in"], c.at("ln_in", d + 1))
                    c.own(A(zt(XB[d]), zt(XB[d]), ACT.Exp, scale=-1.0), "act_own")
                for d in range(2):
                    c.own(A(zt(XB[d]), zt(XB[d]), ACT.Ln, bias=EP[:, 1:2]), "ln_out")
                if i == 0:
                    act.wait_ge(tile_done, c.tile(0) + 1)
                    c.free_tile(A(zt(Q), PD[0][:, :], ACT.Copy, scale=0.125), 0)
                    raw_tile(c, 1, K0)
                else:
                    c.own(A(zt(Q), zt(QRAW), ACT.Copy, scale=0.125), "qk_ready")
                    c.own(A(zt(K0), zt(V), ACT.Copy), "qk_ready")
                for m in range(3):
                    act.wait_ge(sems[f"gate_st{m}"], c.at(f"gate_st{m}", 0) * 16)
                act.wait_ge(sems["o_st"], c.at("o_st", 0) * 16)
                for d in range(2):
                    decays(c, d)
                for hh in range(2):
                    raw_tile(c, first + hh, gV[hh])
                for hh in range(2):
                    evac_turned(c, zt(gVT[hh]), hh, 1 + hh)
                act.wait_ge(tile_done, c.tile(first + 2) + 1)
                c.own(A(zt(gG[0]), PD[0][:, :], ACT.Sigmoid), "sig_ready")
                for d in range(2):
                    evac_turned(c, zt(KT0 + d), 2 + d, 3 + d)
                    level_exp(c, d)
                for hh in range(2):
                    for h in range(2):
                        act.wait_ge(sems["gram_done"], c.at("gram_done", 2 * hh + h + 1))
                        c.free(A(zt(gA[hh])[:, h * HALF:(h + 1) * HALF], PG[:, h * HALF:(h + 1) * HALF], ACT.Copy, scale=2.0),
                               f"gram_free{h}", hh)
                for q in range(2, NQ):
                    level_exp(c, q)
                    if q == 5:
                        act.wait_ge(tile_done, c.tile(first + 3) + 1)
                        c.own(A(zt(gG[1]), PD[1][:, :], ACT.Sigmoid), "sig_ready")
                    elif q > 5 and q % 2:
                        fill(c, first + 3 + (q - 5) // 2)
                    if i == 0 and q in (11, 13):
                        low_rank(c, 1, (q - 11) // 2, 6 + (q - 11) // 2)
                for j in range(first + 8, TILES[c.st]):
                    fill(c, j)
                for hh in range(2):
                    head_out(c, (8, 6)[i] + hh, gVT[hh], XB[2 + hh])
                for hh in range(2):
                    head_rstd(c, XB[hh], 16 + hh)
                for hh in range(2):
                    store_o(c, hh, i * 2 + 4 + hh, gG[hh])
                c.end()

            def fill_pair(c, j):
                if j < 8:
                    store_gate(c, j, j - 6, 16 + (j - 6), (K1, KT1)[j - 6])
                else:
                    raw_tile(c, j, (QRAW, V)[j - 8])

            gla_pair(Pass(act, "gla0"), 0, 2, fill_pair)
            gla_pair(Pass(act, "gla1"), 1, 0,
                     lambda c, j: store_gate(c, j, (j - 4) % 3, 18 + (j - 4), (K1, KT1, KT0)[(j - 4) % 3]))

            for m in range(3):
                act.wait_ge(sems[f"gate_st{m}"], Pass(act, "na").at(f"gate_st{m}", 0) * 16)
            act.wait_ge(sems["o_st"], Pass(act, "na").at("o_st", 0) * 16)
            act.wait_ge(rpb_st, 16 * 16)
            act.dma_start(NCM[:, :], cmask).then_inc(cmask_ld, 16)
            with act.Fori(0, TRIPS["na"]) as i:
                c = Pass(act, "na", i)
                for u in range(2):
                    act.dma_start(NTR[:, :, :], bias_dr[bass.ds(i * 4 + 2 * u, 2)].rearrange("e p x -> p e x")
                                  ).then_inc(c.up("bias_ld"), 16)
                    act.wait_ge(tile_done, c.tile(3 * u) + 1)
                    c.free_tile(A(zt(NQT), PD[u][:, :], ACT.Copy, scale=0.125), 3 * u)
                    raw_tile(c, 3 * u + 1, NK)
                    raw_tile(c, 3 * u + 2, NV)
                    evac_turned(c, zt(NVT), u, u + 1)
                    for k in range(18):
                        if k < 16:
                            n = len(na_step(k)[2]) * P
                            act.wait_ge(sems["max_ready"], c.at("max_ready", 16 * u + k + 1))
                            p = NS[:, k % 3, 0:n]
                            c.own(A(p, p, ACT.Exp, bias=SM[:, 4 + k % 2:5 + k % 2], accum_out=SM[:, 8 + k % 2:9 + k % 2]), "p_exp")
                        if k >= 2:
                            n = len(na_step(k - 2)[2]) * P
                            act.wait_ge(sems["pt_done"], c.at("pt_done", 16 * u + k - 1))
                            c.own(A(NPT[:, (k - 2) % 2, 0:n], PM[:, 0:n], ACT.Copy), "pt_ready")
                    act.wait_ge(sems["pv_done"], c.at("pv_done", u + 1))
                    c.free(A(zt(NV), PG[:, :], ACT.Copy), "gram_free0", u)
                    act.dma_start(o_dr[bass.ds(i * 2 + (8 + u), 1)].rearrange("n p t -> (n p) t"), zt(NV)
                                  ).then_inc(c.up("o_st"), 16)
                    act.wait_ge(sems["o_st"], c.at("o_st", u + 1) * 16)
                c.end()

            c = Pass(act, "mid")
            act.dma_start(H2[:, 11, :], o_dr[11]).then_inc(o_ld[3], 16)
            for n in range(12):
                if n % 4 == 0:
                    act.wait_ge(o_ld[n // 4], 16)
                if n == 11:
                    act.wait_ge(o_ld[3], 16)
                c.own(A(BIG[:, 8 * (n // 4) + n % 4, :], H2[:, n, :], ACT.Copy), "hi_ready")
            c.end()
            with act.Fori(0, TRIPS["merge"]) as i:
                c = Pass(act, "merge", i)
                for j in range(6):
                    act.wait_ge(tile_free[j % 2], c.tile_half(j))
                    act.dma_start(zt(24 + j % 2), gates_dr[bass.ds(i * 6 + j, 1)].rearrange("n p t -> (n p) t")
                                  ).then_inc(c.up(f"in_ld{j % 2}"), 16)
                c.end()
            c = Pass(act, "mid2")
            act.wait_ge(sems["merged"], c.at("merged", 0))
            for ct in range(KD):
                c.own(A(BIG[:, ct, :], H2[:, 4 + ct, :], ACT.Copy), "hi_ready")
            c.end()
            with act.Fori(0, TRIPS["out"]) as i:
                c = Pass(act, "out", i)
                for j in range(2):
                    act.wait_ge(tile_free[j], c.tile_half(j))
                    act.dma_start(zt(24 + j), xt[:, bass.ds(i * 2 + j, 1), :].rearrange("p n t -> p (n t)")
                                  ).then_inc(c.up(f"in_ld{j}"), 16)
                for j in range(2):
                    x1 = ZT[:, bass.ds(i * 2 + (16 + j), 1), :].rearrange("p n t -> p (n t)")
                    act.wait_ge(tile_free[j % 2], c.tile_half(j) + 1)
                    act.dma_start(y_dr[bass.ds(i * 2 + j, 1)].rearrange("n p t -> (n p) t"), x1
                                  ).then_inc(c.up(f"y_st{j}"), 16)
                    c.own(A(H2[:, j, :], x1, ACT.Square), "sq_ready")
                c.end()
            c = Pass(act, "n2")
            act.wait_ge(sems["sum_done"], c.at("sum_done", 1))
            for j in range(2):
                act.wait_ge(sems[f"y_st{j}"], c.at(f"y_st{j}", 0) * 16)
            rstd(c, zt(0), PG[:, :], 1024.0, "rstd_ready")
            for ct in range(KD):
                act.wait_ge(sems["norm_ready"], c.at("norm_ready", ct + 1))
                c.own(A(HS[:, ct, :], zt(16 + ct), ACT.Identity, bias=MOD[:, 24 + ct:25 + ct]), "hi_ready")
            act.wait_ge(sems["lo_ready"], c.at("lo_ready", 8))
            c.end()
            for g in range(2):
                with act.Fori(0, TRIPS["up0"]) as i:
                    c = Pass(act, f"up{g}", i)
                    act.wait_ge(tile_done, c.tile(0) + 1)
                    c.free_tile(A(zt(24), PD[0][:, :], ACT.Silu), 0)
                    act.wait_ge(tile_free[1], c.tile_half(1) + 1)
                    c.own(A(BIG[:, bass.ds(i, 1), :].rearrange("p n t -> p (n t)"), zt(25), ACT.Copy), "hi_ready")
                    c.end()
                c = Pass(act, f"up{g}", TRIPS["up0"])
                act.wait_ge(sems["lo_ready"], c.at("lo_ready", 0))
                with act.Fori(0, TRIPS["dn0"]) as i:
                    c = Pass(act, f"dn{g}", i)
                    for j in range(2):
                        if g == 0:
                            act.wait_ge(sems[f"y_st{j}"], c.at(f"y_st{j}", 0) * 16)
                        else:
                            act.wait_ge(tile_free[j], c.tile_half(j))
                        act.dma_start(zt(24 + j), y_dr[bass.ds(i * 2 + j, 1)].rearrange("n p t -> (n p) t")
                                      ).then_inc(c.up(f"in_ld{j}"), 16)
                    if g == 0:
                        for j in range(2):
                            act.wait_ge(tile_free[j % 2], c.tile_half(j) + 1)
                            act.dma_start(y_dr[bass.ds(i * 2 + j, 1)].rearrange("n p t -> (n p) t"), zt(24 + j)
                                          ).then_inc(c.up(f"y_st{j}"), 16)
                    else:
                        for j in range(2):
                            act.wait_ge(tile_free[j % 2], c.tile_half(j) + 1)
                            y = H2[:, bass.ds(i * 2 + j, 1), :].rearrange("p n t -> p (n t)")
                            c.own(A(H2[:, 8 + j, :], y, ACT.Square), "sq_ready")
                    c.end()
                if g == 0:
                    for j in range(2):
                        act.wait_ge(sems[f"y_st{j}"], Pass(act, "up1").at(f"y_st{j}", 0) * 16)
            c = Pass(act, "fin")
            act.wait_ge(sems["sum_done"], c.at("sum_done", 1))
            rstd(c, H2[:, 10, :], PG[:, :], 1024.0, "rstd_ready")
            for ct in range(KD):
                act.wait_ge(sems["norm_ready"], c.at("norm_ready", ct + 1))
                act.dma_start(out[ct], H2[:, ct, :]).then_inc(c.up("out_st"), 16)
            act.wait_ge(sems["out_st"], c.at("out_st", 8) * 16)
            c.end()

        @block.vector
        def _(dve):
            tt, ts, stt = dve.tensor_tensor, dve.tensor_scalar, dve.scalar_tensor_tensor

            c = Pass(dve, "pre")
            own = lambda ins: c.own(ins, "dve_own")
            own(dve.memset(EP[:, 0:1], EPS))
            own(dve.memset(EP[:, 1:2], 1.0))
            dve.wait_ge(const_ld, 64)
            own(dve.tensor_copy(MASK[:, :, :], MASKF[:, :, :]))
            lb, lg = LB[:, 0, :], PRM[:, PC_LB:PC_LB + 8]
            c.own(tt(lb, lg, lg, ALU.subtract), "param_ready")
            dve.wait_ge(sems["act_own"], c.at("act_own", 1))
            own(tt(CB[:, :], CB[:, :], H2[:, 12, :], ALU.mult))
            dve.wait_ge(sems["act_own"], c.at("act_own", 2))
            own(dve.reciprocal(LB[:, 1, :], lb))
            own(tt(lb, lb, LB[:, 1, :], ALU.mult))
            own(tt(lb, lb, lb, ALU.subtract))
            own(ts(lb, lb, 0.0, 1.0, ALU.max, ALU.min))
            own(ts(LB[:, 1, :], lb, -1.0, 1.0, ALU.mult, ALU.add))

            def norm(c, first, cts, rb, w, s):
                x = lambda ct: zt(first + ct)
                for ct in list(cts) + [None]:
                    if ct is not None:
                        c.own(stt(x(ct), x(ct), SCL[:, s, ct:ct + 1], rb, ALU.mult, ALU.mult), "norm_ready")
                    done = cts[-1] if ct is None else ct - 1
                    if done >= cts[0]:
                        dve.wait_ge(sems["hi_ready"], c.at("hi_ready", done + 1))
                        c.own(stt(HS[:, KD + done, :], x(done), MOD[:, w + done:w + done + 1],
                                  HS[:, done, :].bitcast(F32), ALU.add, ALU.subtract), "lo_ready")

            mod1 = lambda a, n: MOD[:, 0:NADA].rearrange("p (s c) -> p s c", c=KD)[:, :, a:a + n]
            bias1 = PRM[:, PC_BADA:PC_BADA + NADA].rearrange("p (s c) -> p s c", c=KD)
            for k in range(4):
                dve.wait_ge(ada_pre[k], 16)
                for t in range(4 * k, 4 * k + 4):
                    to = KD * (t % 2) + t // 2
                    own(dve.tensor_tensor_reduce(zt(t), zt(t), CB[:, :], 1.0, 0.0, ALU.mult, ALU.add, MOD[:, to:to + 1]))
                own(tt(mod1(2 * k, 2), mod1(2 * k, 2), bias1[:, :, 2 * k:2 * k + 2], ALU.add))
                own(stt(SCL[:, 0, 2 * k:2 * k + 2], MOD[:, 8 + 2 * k:10 + 2 * k], 1.0, PRM[:, PC_N1 + 2 * k:PC_N1 + 2 * k + 2],
                        ALU.add, ALU.mult))
                if k == 1:
                    dve.wait_ge(sems["rstd_ready"], c.at("rstd_ready", 1))
                if k >= 1:
                    norm(c, 16, range(2 * k - 2, 2 * k), H2[:, 15, :], 0, 0)
            norm(c, 16, range(6, 8), H2[:, 15, :], 0, 0)
            dve.wait_ge(lr_st, 16)
            own(dve.memset(PX[:, :, :, 0:1], 0.0))
            c.end()

            def cumulate(c, d):
                for n in range(NC):
                    ins = dve.tensor_tensor_scan(PX[:, d, n, 1:P + 1], ONES, zt(F0 + d)[:, n * P:(n + 1) * P], 0.0,
                                                 ALU.mult, ALU.add)
                    c.own(ins, "dve_own")
                lo = 1 - d
                c.own(tt(chunked(zt(XB[d])), PX[:, d, :, lo:lo + P], px_last(d), ALU.subtract), "diff_ready")

            def decayed(c, k0, k1):
                dve.wait_ge(sems["exp_ready"], c.at("exp_ready", 1))
                c.own(tt(zt(F0), zt(k0), zt(XB[0]), ALU.mult), "kdec_ready")
                c.own(tt(zt(QD0), zt(QD0), zt(Q), ALU.mult), "dve_own")
                dve.wait_ge(sems["exp_ready"], c.at("exp_ready", 2))
                c.own(tt(zt(F1), zt(k1), zt(F1), ALU.mult), "kdec_ready")
                c.own(tt(zt(QD1), zt(Q), zt(XB[1]), ALU.mult), "dve_own")

            def level_diff(c, q):
                s, d = LEVELS[q // 2], q % 2
                v, r = px_view(d, s)
                o = zt(XB[q % 4]).rearrange("p (c b t) -> p c b t", c=NC, t=2 * s)
                c.own(tt(o, v, r, ALU.subtract), "diff_ready")

            def level_products(c, q, k0, k1):
                s, d = LEVELS[q // 2], q % 2
                dve.wait_ge(sems["exp_ready"], c.at("exp_ready", 2 + q + 1))
                x = blocks(zt(XB[q % 4]), s)
                a, b = (k0, Q) if d == 0 else (Q, k1)
                c.own(tt(x[:, :, 0:s], x[:, :, 0:s], blocks(zt(a), s)[:, :, 0:s], ALU.mult), "dve_own")
                c.own(tt(x[:, :, s:], x[:, :, s:], blocks(zt(b), s)[:, :, s:], ALU.mult), "x_ready")

            def level_select(c, l, a, use):
                for h in range(2):
                    dve.wait_ge(sems["gram_done"], c.at("gram_done", 2 * use + h + 1))
                    dve.sem_inc(dve_step, 1)
                    ins = dve.copy_predicated(chunked(zt(a)[:, h * HALF:(h + 1) * HALF]),
                                              MASK[:, l:l + 1, :].to_broadcast([P, 4, P]),
                                              chunked(PG[:, h * HALF:(h + 1) * HALF]))
                    c.free(ins, f"gram_free{h}", use)

            def carry(c, use, d):
                dve.wait_ge(sems["misc_done"], c.at("misc_done", use + 1))
                S = chunked(zt(S0 + d))
                ps = chunked(PM[:, :])
                order = list(range(0, 7)) if d == 0 else list(range(7, 0, -1))
                for m, n in enumerate(order):
                    to = S[:, n + 1 if d == 0 else n - 1, :]
                    if m == 0:
                        ins = dve.tensor_copy(to, ps[:, n, :])
                    else:
                        ins = stt(to, S[:, n, :], AN[:, d, n:n + 1], ps[:, n, :], ALU.mult, ALU.add)
                    if m == len(order) - 1:
                        c.free(ins, "misc_free", use)
                    else:
                        c.own(ins, "dve_own")

            def finish_head(c, nth, ob, rb, g, w, to):
                dve.wait_ge(sems["orstd_ready"], c.at("orstd_ready", nth + 1))
                c.own(stt(zt(ob), zt(ob), PRM[:, w:w + 1], zt(rb), ALU.mult, ALU.mult), "dve_own")
                c.own(tt(zt(to), zt(ob), zt(g), ALU.mult), "o_ready")

            def decay_in(c, d, head):
                f, x = zt(F0 + d), zt(LNX)
                dve.wait_ge(sems["f_ready"], c.at("f_ready", d + 1))
                c.own(ts(f, f, LB[:, 1, bass.ds(head + 4 * d, 1)], LB[:, 0, bass.ds(head + 4 * d, 1)], ALU.mult, ALU.add),
                      "dve_own")
                c.own(ts(x, f, 1.0 / LN_SPLIT, F_FLOOR / LN_SPLIT, ALU.mult, ALU.max), "dve_own")
                c.own(ts(x, x, 1.0, None, ALU.min), "dve_own")
                c.own(ts(f, f, LN_SPLIT, None, ALU.max), "ln_in")

            def decay_out(c, d):
                dve.wait_ge(sems["ln_out"], c.at("ln_out", d + 1))
                c.own(tt(zt(F0 + d), zt(F0 + d), zt(LNX), ALU.add), "dve_own")

            def keys(c, head):
                for d in range(2):
                    c.own(ts(zt(K0 + d), zt(GB + d), LB[:, 1, bass.ds(head + 4 * d, 1)], None, ALU.mult), "dve_own")

            def hgrn_head(c, i, last):
                dve.wait_ge(sems["sig_ready"], c.at("sig_ready", 1))
                c.own(tt(zt(Q), zt(Q), zt(QRAW), ALU.mult), "dve_own")
                decayed(c, K0, K1)
                level_diff(c, 0)
                level_diff(c, 1)
                dve.wait_ge(sems["sig_ready"], c.at("sig_ready", 2))
                c.free_tile(tt(zt(G), zt(G), PD[0][:, :], ALU.mult), 0)
                dve.wait_ge(sems["misc_done"], c.at("misc_done", 1))
                c.own(tt(zt(V), zt(K0), zt(K1), ALU.add), "ksum_ready")
                level_products(c, 0, K0, K1)
                level_products(c, 1, K0, K1)
                carry(c, 3, 0)
                level_diff(c, 2)
                level_diff(c, 3)
                carry(c, 4, 1)
                dve.wait_ge(sems["gram_free0"], c.at("gram_free0", 1))
                dve.wait_ge(sems["gram_free1"], c.at("gram_free1", 1))
                for q in range(2, NQ):
                    level_products(c, q, K0, K1)
                    if q + 2 < NQ:
                        dve.wait_ge(sems["gram_done"], c.at("gram_done", 2 * (q // 2 + 1)))
                        level_diff(c, q + 2)
                    if q % 2:
                        level_select(c, q // 2 - 1, A0, q // 2)
                    if not last:
                        if q == 9:
                            decay_in(c, 0, i + 1)
                        if q == 11:
                            decay_out(c, 0)
                            decay_in(c, 1, i + 1)
                        if q == 13:
                            decay_out(c, 1)
                            keys(c, i + 1)
                level_select(c, NQ // 2 - 1, A0, NQ // 2)
                c.own(dve.memset(SM[:, 15:16], 0.0), "attn_ready")
                if not last:
                    cumulate(c, 0)
                    cumulate(c, 1)
                finish_head(c, 0, KT1, S0, G, PC_HN, KT1)
                c.end()

            c = Pass(dve, "hgrn_in")
            for d in range(2):
                decay_in(c, d, 0)
                decay_out(c, d)
            keys(c, 0)
            cumulate(c, 0)
            cumulate(c, 1)
            c.end()
            with dve.Fori(0, TRIPS["hgrn"]) as i:
                hgrn_head(Pass(dve, "hgrn", i), i, False)
            hgrn_head(Pass(dve, "hgrn_last"), 3, True)

            def gla_pair(c, first):
                own = lambda ins: c.own(ins, "dve_own")
                for d in range(2):
                    dve.wait_ge(sems["z_ready"], c.at("z_ready", d - 1))
                    f, x = zt(F0 + d), zt(XB[d])
                    c.own(stt(x, f, -1.0, f, ALU.mult, ALU.max), "ln_in")
                for d in range(2):
                    dve.wait_ge(sems["ln_out"], c.at("ln_out", d + 1))
                    f = zt(F0 + d)
                    own(stt(f, f, 0.0, zt(XB[d]), ALU.min, ALU.subtract))
                    own(ts(f, f, 1.0 / 16.0, None, ALU.mult))
                    cumulate(c, d)
                if first:
                    dve.wait_ge(tile_free[0], c.tile_half(0) + 1)
                    dve.wait_ge(tile_free[1], c.tile_half(1) + 1)
                else:
                    dve.wait_ge(sems["qk_ready"], c.at("qk_ready", 2))
                decayed(c, K0, K0)
                dve.wait_ge(sems["sig_ready"], c.at("sig_ready", 1))
                c.free_tile(tt(zt(gG[0]), zt(gG[0]), PD[0][:, :], ALU.mult), first + 2)
                level_diff(c, 0)
                level_diff(c, 1)
                level_products(c, 0, K0, K0)
                level_products(c, 1, K0, K0)
                carry(c, 4, 0)
                level_diff(c, 2)
                level_diff(c, 3)
                carry(c, 5, 1)
                dve.wait_ge(sems["gram_free0"], c.at("gram_free0", 2))
                dve.wait_ge(sems["gram_free1"], c.at("gram_free1", 2))
                for q in range(2, NQ + 2):
                    if q < NQ:
                        level_products(c, q, K0, K0)
                    if q % 2 == 0:
                        level_select(c, q // 2 - 1, gA[0], q)
                    if q + 2 < NQ:
                        dve.wait_ge(sems["gram_done"], c.at("gram_done", 4 * (q // 2 + 1)))
                        level_diff(c, q + 2)
                    if q % 2:
                        level_select(c, q // 2 - 1, gA[1], q)
                    if q == 5:
                        dve.wait_ge(sems["sig_ready"], c.at("sig_ready", 2))
                        c.free_tile(tt(zt(gG[1]), zt(gG[1]), PD[1][:, :], ALU.mult), first + 3)
                for hh in range(2):
                    c.own(dve.memset(SM[:, 15:16], 0.0), "attn_ready")
                for hh in range(2):
                    finish_head(c, hh, gVT[hh], XB[hh], gG[hh], PC_GN, gG[hh])
                c.end()

            gla_pair(Pass(dve, "gla0"), 2)
            gla_pair(Pass(dve, "gla1"), 0)

            dve.wait_ge(cmask_ld, 16)
            with dve.Fori(0, TRIPS["na"]) as i:
                c = Pass(dve, "na", i)
                own = lambda ins: c.own(ins, "dve_own")
                for u in range(2):
                    dve.wait_ge(sems["bias_ld"], c.at("bias_ld", u + 1) * 16)
                    tr = NTR[:, :, :].rearrange("p e (r k) -> p (e r) k", k=64)
                    cm = NCM[:, 0:64].rearrange("p (o k) -> p o k", o=1).to_broadcast([P, 28, 64])
                    own(tt(tr, tr, cm, ALU.add))
                    for e in range(2):
                        own(tt(NTI[:, e, :], NTR[:, e, P:6 * P], NCM[:, 64:64 + 5 * P], ALU.add))
                    for k in range(17):
                        if k < 16:
                            head, t, us = na_step(k)
                            n = len(us) * P
                            at = (us[0] - t + 3) * P
                            bias = NTI[:, head, 0:n] if len(us) == 5 else NTR[:, head, at:at + n]
                            dve.wait_ge(sems["s_done"], c.at("s_done", 16 * u + k + 1))
                            dve.sem_inc(dve_step, 1)
                            c.own(dve.tensor_tensor_reduce(NS[:, k % 3, 0:n], PD[k % 2][:, 0:n], bias, 1.0, -3.0e38, ALU.add,
                                                           ALU.max, SM[:, k % 2:k % 2 + 1]), "s_read")
                            c.own(ts(SM[:, 4 + k % 2:5 + k % 2], SM[:, k % 2:k % 2 + 1], -1.0, None, ALU.mult), "max_ready")
                        if k >= 1:
                            m, p = (k - 1) % 2, NS[:, (k - 1) % 3, 0:len(na_step(k - 1)[2]) * P]
                            dve.wait_ge(sems["p_exp"], c.at("p_exp", 16 * u + k))
                            own(dve.reciprocal(SM[:, 12 + m:13 + m], SM[:, 8 + m:9 + m]))
                            c.own(ts(p, p, SM[:, 12 + m:13 + m], None, ALU.mult), "p_norm")
                        if 8 <= k < 16:
                            t = k - 8
                            if t % 4 == 0:
                                dve.wait_ge(sems[f"ada_ld{t // 4}"], c.at(f"ada_ld{t // 4}", u + 1) * 16)
                                dve.sem_inc(dve_step, 1)
                            own(dve.tensor_tensor_reduce(zt(NW + t), zt(NW + t), CB[:, :], 1.0, 0.0, ALU.mult, ALU.add,
                                                         MT[:, t:t + 1]))
                    c.own(tt(MOD[:, bass.ds(i * 16 + (NADA + 8 * u), 8)], MT[:, :],
                             PRM[:, bass.ds(i * 16 + (PC_BADA + NADA + 8 * u), 8)], ALU.add), "mod_ready")
                c.end()

            c = Pass(dve, "mid")
            for n in range(12):
                at = 8 * (n // 4) + n % 4
                dve.wait_ge(sems["hi_ready"], c.at("hi_ready", n + 1))
                c.own(tt(BIG[:, at + 4, :], H2[:, n, :], BIG[:, at, :].bitcast(F32), ALU.subtract), "lo_ready")
            c.end()
            with dve.Fori(0, TRIPS["merge"]) as i:
                c = Pass(dve, "merge", i)
                for j in range(6):
                    m = H2[:, bass.ds(i * 2 + (4 + j // 3), 1), :].rearrange("p n t -> p (n t)")
                    dve.wait_ge(sems[f"in_ld{j % 2}"], c.at(f"in_ld{j % 2}", j // 2 + 1) * 16)
                    dve.wait_ge(tile_done, c.tile(j) + 1)
                    to = m if j % 3 == 0 else H2[:, 2, :]
                    c.free_tile(tt(to, zt(24 + j % 2), PD[j % 2][:, :], ALU.mult), j)
                    if j % 3:
                        c.own(tt(m, m, H2[:, 2, :], ALU.add), "dve_own" if j % 3 == 1 else "merged")
                c.end()
            c = Pass(dve, "mid2")
            for ct in range(KD):
                dve.wait_ge(sems["hi_ready"], c.at("hi_ready", ct + 1))
                c.own(tt(BIG[:, KD + ct, :], H2[:, 4 + ct, :], BIG[:, ct, :].bitcast(F32), ALU.subtract), "lo_ready")
            c.own(dve.memset(H2[:, 2, :], 0.0), "dve_own")
            c.end()

            def add_square(c, j, sq, acc):
                dve.wait_ge(sems["sq_ready"], c.at("sq_ready", j + 1))
                c.own(tt(acc, acc, sq, ALU.add), "acc_ready")

            with dve.Fori(0, TRIPS["out"]) as i:
                c = Pass(dve, "out", i)
                for j in range(2):
                    x1 = ZT[:, bass.ds(i * 2 + (16 + j), 1), :].rearrange("p n t -> p (n t)")
                    dve.wait_ge(sems[f"in_ld{j}"], c.at(f"in_ld{j}", 1) * 16)
                    dve.wait_ge(tile_done, c.tile(j) + 1)
                    c.free_tile(stt(x1, PD[j][:, :], MOD[:, bass.ds(i * 2 + (16 + j), 1)], zt(24 + j), ALU.mult, ALU.add), j)
                for j in range(2):
                    add_square(c, j, H2[:, j, :], H2[:, 2, :])
                c.end()
            c = Pass(dve, "n2")
            own = lambda ins: c.own(ins, "dve_own")
            own(stt(SCL[:, 1, :], MOD[:, 32:40], 1.0, PRM[:, PC_N2:PC_N2 + KD], ALU.add, ALU.mult))
            dve.wait_ge(sems["rstd_ready"], c.at("rstd_ready", 1))
            norm(c, 16, range(KD), zt(0), 24, 1)
            c.end()
            for g in range(2):
                with dve.Fori(0, TRIPS["up0"]) as i:
                    c = Pass(dve, f"up{g}", i)
                    dve.wait_ge(tile_free[0], c.tile_half(0) + 1)
                    dve.wait_ge(tile_done, c.tile(1) + 1)
                    c.free_tile(tt(zt(25), zt(24), PD[1][:, :], ALU.mult), 1)
                    dve.wait_ge(sems["hi_ready"], c.at("hi_ready", 1))
                    hi = BIG[:, bass.ds(i, 1), :].rearrange("p n t -> p (n t)")
                    lo = BIG[:, bass.ds(i + KF, 1), :].rearrange("p n t -> p (n t)")
                    c.own(tt(lo, zt(25), hi.bitcast(F32), ALU.subtract), "lo_ready")
                    c.end()
                if g == 1:
                    c = Pass(dve, "up1", TRIPS["up1"])
                    dve.memset(H2[:, 11, :], 0.0).then_inc(acc_zero, 1)
                    dve.wait_ge(acc_zero, 1)
                with dve.Fori(0, TRIPS["dn0"]) as i:
                    c = Pass(dve, f"dn{g}", i)
                    for j in range(2):
                        y = zt(24 + j) if g == 0 else H2[:, bass.ds(i * 2 + j, 1), :].rearrange("p n t -> p (n t)")
                        dve.wait_ge(sems[f"in_ld{j}"], c.at(f"in_ld{j}", 1) * 16)
                        dve.wait_ge(tile_done, c.tile(j) + 1)
                        c.free_tile(stt(y, PD[j][:, :], MOD[:, bass.ds(i * 2 + (40 + j), 1)], zt(24 + j), ALU.mult, ALU.add), j)
                    if g == 1:
                        for j in range(2):
                            add_square(c, j, H2[:, 8 + j, :], H2[:, 11, :])
                    c.end()
            c = Pass(dve, "fin")
            dve.wait_ge(sems["rstd_ready"], c.at("rstd_ready", 1))
            for ct in range(KD):
                y = H2[:, ct, :]
                c.own(stt(y, y, PRM[:, PC_NF + ct:PC_NF + ct + 1], H2[:, 10, :], ALU.mult, ALU.mult), "norm_ready")
            c.end()


_NAMES = ["x", "c", "w_ada", "b_ada", "norm1_w", "w_in", "na_rpb", "gla_lr_up", "gla_lr_bias", "gla_norm_w",
          "hgrn_lb_logits", "hgrn_norm_w", "w_proj_na", "w_proj_gla", "w_proj_hgrn", "w_out", "norm2_w",
          "w_ffn_gate", "w_ffn_up", "w_ffn_down", "final_norm_w"]


def kernel(**inputs):
    import numpy as np
    import concourse.bacc as _bacc
    from concourse import mybir as _mybir
    from concourse.bass_utils import run_bass_kernel_spmd as _run

    a = {k: np.asarray(inputs[k]) for k in _NAMES}

    cols = lambda v: v.reshape(-1, P).T
    lrb = a["gla_lr_bias"][0].reshape(2, 2, P).reshape(4, P).T
    prm = np.concatenate([cols(a["b_ada"][0]), cols(a["norm1_w"][0]), cols(a["norm2_w"][0]),
                          cols(a["final_norm_w"]), cols(a["gla_norm_w"][0]), cols(a["hgrn_norm_w"][0]),
                          cols(a["hgrn_lb_logits"][0]), lrb], axis=1)
    xt = a["x"][0].T.reshape(KD, P, T).transpose(1, 0, 2)
    pieces = lambda w: w.reshape(w.shape[0] // P, P, w.shape[1] // P, P).transpose(2, 1, 0, 3)
    w_ada = a["w_ada"][0].T.reshape(48, P, D_MODEL).transpose(1, 0, 2)
    first = [n // 2 + KD * (n % 2) for n in range(NADA)]
    w_ada = np.concatenate([w_ada[:, first], w_ada[:, NADA:]], axis=1)
    w = a["w_in"][0]
    w_lr = np.concatenate([w[:, 3072:3104], np.zeros((D_MODEL, P - 32), w.dtype)], axis=1)
    w_lr = pieces(w_lr)[0]
    order = []
    gate = [5664 + (2 - g % 3) * D_MODEL + (g // 3) * P for g in range(24)]
    head = [[3616 + P * h, 4128 + P * h, 3104 + P * h, 4640 + P * h] for h in range(4)]
    order += head[0]
    for h in range(4):
        order += [5152 + P * h] + (gate[3 * h:3 * h + 3] + head[h + 1] if h < 3 else gate[9:16])
    gla = [[1536 + P * p, 1792 + P * p, 2048 + 2 * P * p, 2048 + 2 * P * p + P, 2560 + 2 * P * p, 2560 + 2 * P * p + P]
           for p in range(2)]
    order += gla[0] + gate[16:18] + gla[1] + gate[18:24]
    for p in range(4):
        order += [P * p, 512 + P * p, 1024 + P * p]
    w_in = pieces(np.concatenate([w[:, o:o + P] for o in order], axis=1))
    pr = [pieces(a[f"w_proj_{b}"][0]) for b in ("hgrn", "gla", "na")]
    w_proj = np.stack([pr[n % 3][n // 3] for n in range(24)])
    w_out = pieces(a["w_out"][0])
    wg, wu, wd = pieces(a["w_ffn_gate"][0]), pieces(a["w_ffn_up"][0]), pieces(a["w_ffn_down"][0])
    w_up = np.stack([wg, wu], axis=1).reshape(2, 2 * KF, P, KD, P)
    w_dn = np.stack([wd[:, :, 0:KF], wd[:, :, KF:2 * KF]])
    lup = np.zeros((32, 2, 2, P), w.dtype)
    for s in range(2):
        for p in range(2):
            lup[16 * s:16 * s + 16, p, s, :] = a["gla_lr_up"][0, s, :, p * P:(p + 1) * P]
    rpb = np.zeros((8, 15, P), w.dtype)
    rpb[:, :, 48:79] = a["na_rpb"][0]

    masks = np.zeros((P, len(LEVELS), P), np.float32)
    j, i = np.arange(P)[:, None], np.arange(P)[None, :]
    for n, s in enumerate(LEVELS):
        same = (j // (2 * s)) == (i // (2 * s))
        masks[:, n, :] = same & ((j % (2 * s) < s) != (i % (2 * s) < s))
    cmat = np.stack([np.ones((P, P), np.float32), np.eye(P, dtype=np.float32)], axis=1)
    qr, qc = np.arange(P) // 64, np.arange(P) % 64
    start = np.clip(qc - 8, 0, 48)
    kc = np.arange(64)
    cmask = np.zeros((P, 64 + 5 * P), np.float32)
    cmask[:, 0:64][(kc[None, :] < start[:, None]) | (kc[None, :] >= start[:, None] + 16)] = NEG_INF
    kr = np.arange(5 * P) // 64 - 4
    off = kr[None, :] - qr[:, None]
    cmask[:, 64:][(off < -4) | (off > 3)] = NEG_INF

    nc = _bacc.Bacc("TRN2", target_bir_lowering=False, num_devices=1)
    arrays, args = {}, []
    for name, v in (("c", a["c"]), ("prm", prm), ("masks", masks), ("cmat", cmat), ("cmask", cmask), ("xt", xt), ("w_ada", w_ada),
                    ("w_lr", w_lr), ("w_in", w_in), ("w_proj", w_proj), ("w_out", w_out), ("w_up", w_up),
                    ("w_dn", w_dn), ("lup", lup), ("rpb", rpb)):
        v = np.ascontiguousarray(v)
        arrays[f"in_{name}_dram"] = v
        args.append(nc.dram_tensor(f"in_{name}_dram", v.shape, _mybir.dt.from_np(v.dtype), kind="ExternalInput").ap())
    args.append(nc.dram_tensor("out_0_dram", (KD, P, T), _mybir.dt.float32, kind="ExternalOutput").ap())
    trunk(nc, *args)
    r = _run(nc, [arrays], core_ids=[0])
    got = r.results[0]["out_0_dram"]
    return got.transpose(2, 0, 1).reshape(1, T, D_MODEL)
```
